# Optimizing a Trainium2 kernel written in Bass

```python
import math
import jax, jax.numpy as jnp
from jax import lax
import numpy as np
import jax
import jax.numpy as jnp

D_MODEL = 1024
BATCH = 1
SEQ = 256
DEPTH = 1

MEM_LEN = 256
RMS_EPS = 1e-6
SB_HEADS = 16
SB_HEAD_DIM = 64
SB_WIDTH = SB_HEADS * SB_HEAD_DIM
SB_BLOCK = 128
SSM_EXPAND = 2
SSM_INNER = SSM_EXPAND * D_MODEL
SSM_HEAD_DIM = 64
SSM_HEADS = SSM_INNER // SSM_HEAD_DIM
SSM_GROUPS = 4
SSM_STATE = 128
SSM_CONV = 4
SSM_CHUNK = 128
SSM_CONV_DIM = SSM_INNER + 2 * SSM_GROUPS * SSM_STATE
XA_HEADS = 4
XA_HEAD_DIM = D_MODEL // XA_HEADS
FFN_HIDDEN = ((8 * D_MODEL + 767) // 768) * 256
IN_SIZES = (SB_WIDTH, SB_WIDTH, SB_WIDTH, SSM_INNER, SSM_CONV_DIM, SSM_HEADS, D_MODEL, D_MODEL)
IN_WIDTH = 3 * SB_WIDTH + SSM_INNER + SSM_CONV_DIM + SSM_HEADS + 2 * D_MODEL


def _split(a, sizes):
    idx = tuple(int(i) for i in np.cumsum(sizes)[:-1])
    return jnp.split(a, idx, axis=-1)

def rms_norm(x, g):
    xf = x.astype(jnp.float32)
    y = xf * lax.rsqrt(jnp.mean(xf * xf, axis=-1, keepdims=True) + RMS_EPS)
    return (y * g.astype(jnp.float32)).astype(x.dtype)

def stick_breaking_attention(q, k, v):
    bsz, seq = q.shape[0], q.shape[1]
    qf = jnp.swapaxes(q.astype(jnp.float32), 1, 2) * (SB_HEAD_DIM ** -0.5)
    kf = jnp.swapaxes(k.astype(jnp.float32), 1, 2)
    vf = jnp.swapaxes(v.astype(jnp.float32), 1, 2)
    outs = []
    for blk in range(seq // SB_BLOCK):
        t0 = blk * SB_BLOCK
        t1 = t0 + SB_BLOCK
        z = jnp.einsum('bhtd,bhsd->bhts', qf[:, :, t0:t1], kf[:, :, :t1])
        causal = jnp.arange(t1)[None, :] < (t0 + jnp.arange(SB_BLOCK))[:, None]
        log_1mb = jnp.where(causal, jax.nn.log_sigmoid(-z), 0.0)
        tail = lax.cumsum(log_1mb, axis=3, reverse=True)
        w = jnp.where(causal, jnp.exp(z + tail), 0.0)
        outs.append(jnp.einsum('bhts,bhsd->bhtd', w, vf[:, :, :t1]))
    o = jnp.concatenate(outs, axis=2)
    return jnp.swapaxes(o, 1, 2).reshape(bsz, seq, SB_WIDTH)

def ssd_chunked(x, dt, a, bm, cm):
    b, l, h, p = x.shape
    g, n = bm.shape[2], bm.shape[3]
    e = h // g
    c = l // SSM_CHUNK
    xc = (x * dt[..., None]).reshape(b, c, SSM_CHUNK, g, e, p)
    a_dt = (dt * a).reshape(b, c, SSM_CHUNK, g, e).transpose(0, 1, 3, 4, 2)
    a_cs = jnp.cumsum(a_dt, axis=-1)
    bc = bm.reshape(b, c, SSM_CHUNK, g, n)
    cc = cm.reshape(b, c, SSM_CHUNK, g, n)
    tril = jnp.tril(jnp.ones((SSM_CHUNK, SSM_CHUNK), dtype=bool))
    decay = jnp.exp(jnp.where(tril, a_cs[..., :, None] - a_cs[..., None, :], -jnp.inf))
    cb = jnp.einsum('bclgn,bcsgn->bcgls', cc, bc)
    y_diag = jnp.einsum('bcgls,bcgels,bcsgep->bclgep', cb, decay, xc)
    decay_to_end = jnp.exp(a_cs[..., -1:] - a_cs)
    states = jnp.einsum('bclgn,bcgel,bclgep->bcgepn', bc, decay_to_end, xc)
    chunk_decay = jnp.exp(a_cs[..., -1])

    def step(prev, inp):
        st, dec = inp
        return prev * dec[..., None, None] + st, prev

    init = jnp.zeros((b, g, e, p, n), dtype=states.dtype)
    _, prev_states = lax.scan(step, init, (jnp.moveaxis(states, 1, 0), jnp.moveaxis(chunk_decay, 1, 0)))
    prev_states = jnp.moveaxis(prev_states, 0, 1)
    y_off = jnp.einsum('bclgn,bcgepn,bcgel->bclgep', cc, prev_states, jnp.exp(a_cs))
    return (y_diag + y_off).reshape(b, l, h, p)

def ssd_branch(z, xbc, dt_raw, conv_w, conv_b, dt_bias, a_log, d_skip, g_norm):
    bsz, seq = xbc.shape[0], xbc.shape[1]
    xbc = lax.conv_general_dilated(
        xbc, conv_w[:, None, :].astype(xbc.dtype), window_strides=(1,),
        padding=[(SSM_CONV - 1, 0)], dimension_numbers=('NWC', 'WIO', 'NWC'),
        feature_group_count=SSM_CONV_DIM)
    xbc = jax.nn.silu(xbc.astype(jnp.float32) + conv_b.astype(jnp.float32))
    xs, bm, cm = _split(xbc, (SSM_INNER, SSM_GROUPS * SSM_STATE, SSM_GROUPS * SSM_STATE))
    dt = jax.nn.softplus(dt_raw.astype(jnp.float32) + dt_bias.astype(jnp.float32))
    a = -jnp.exp(a_log.astype(jnp.float32))
    xh = xs.reshape(bsz, seq, SSM_HEADS, SSM_HEAD_DIM)
    y = ssd_chunked(xh, dt, a,
                    bm.reshape(bsz, seq, SSM_GROUPS, SSM_STATE),
                    cm.reshape(bsz, seq, SSM_GROUPS, SSM_STATE))
    y = y + d_skip.astype(jnp.float32)[:, None] * xh
    y = y.reshape(bsz, seq, SSM_INNER) * jax.nn.silu(z.astype(jnp.float32))
    yg = y.reshape(bsz, seq, SSM_GROUPS, SSM_INNER // SSM_GROUPS)
    yg = yg * lax.rsqrt(jnp.mean(yg * yg, axis=-1, keepdims=True) + RMS_EPS)
    return yg.reshape(bsz, seq, SSM_INNER) * g_norm.astype(jnp.float32)

def memory_cross_attention(h, mem_n, w_xq, w_xkv, w_xo):
    bsz, seq = h.shape[0], h.shape[1]
    q = (h @ w_xq).reshape(bsz, seq, XA_HEADS, XA_HEAD_DIM)
    k, v = _split(mem_n @ w_xkv, (D_MODEL, D_MODEL))
    k = k.reshape(bsz, MEM_LEN, XA_HEADS, XA_HEAD_DIM)
    v = v.reshape(bsz, MEM_LEN, XA_HEADS, XA_HEAD_DIM)
    s = jnp.einsum('bshd,bmhd->bhsm', q.astype(jnp.float32), k.astype(jnp.float32)) * (XA_HEAD_DIM ** -0.5)
    p = jax.nn.softmax(s, axis=-1)
    o = jnp.einsum('bhsm,bmhd->bshd', p, v.astype(jnp.float32)).reshape(bsz, seq, D_MODEL)
    return o.astype(h.dtype) @ w_xo

def swiglu(h, w_gu, w_down):
    gate, up = _split(h @ w_gu, (FFN_HIDDEN, FFN_HIDDEN))
    return (jax.nn.silu(gate) * up) @ w_down

def first_inputs(seed: int = 0) -> dict:
    key = jax.random.key(seed)
    ks = jax.random.split(key, 32)
    f32 = jnp.float32

    def dense(k, shape, fan_in):
        return jax.random.normal(k, shape, f32) * (fan_in ** -0.5)

    def gain(k, shape):
        return 1.0 + 0.02 * jax.random.normal(k, shape, f32)

    dt0 = jnp.exp(jax.random.uniform(ks[5], (DEPTH, SSM_HEADS), f32,
                                     minval=math.log(1e-3), maxval=math.log(1e-1)))
    dt_bias = dt0 + jnp.log(-jnp.expm1(-dt0))
    a_log = jnp.log(jax.random.uniform(ks[6], (DEPTH, SSM_HEADS), f32, minval=1.0, maxval=16.0))
    return {
        "x": jax.random.normal(ks[0], (BATCH, SEQ, D_MODEL), f32),
        "mem": jax.random.normal(ks[1], (BATCH, MEM_LEN, D_MODEL), f32),
        "g_pre_mix": gain(ks[2], (DEPTH, D_MODEL)),
        "w_in": dense(ks[3], (DEPTH, D_MODEL, IN_WIDTH), D_MODEL),
        "conv_w": dense(ks[4], (DEPTH, SSM_CONV, SSM_CONV_DIM), SSM_CONV),
        "conv_b": 0.01 * jax.random.normal(ks[7], (DEPTH, SSM_CONV_DIM), f32),
        "dt_bias": dt_bias,
        "a_log": a_log,
        "d_skip": 1.0 + 0.1 * jax.random.normal(ks[8], (DEPTH, SSM_HEADS), f32),
        "g_ssm_norm": gain(ks[9], (DEPTH, SSM_INNER)),
        "w_br_att": dense(ks[10], (DEPTH, SB_WIDTH, D_MODEL), SB_WIDTH),
        "w_br_ssm": dense(ks[11], (DEPTH, SSM_INNER, D_MODEL), SSM_INNER),
        "w_mix_out": dense(ks[12], (DEPTH, D_MODEL, D_MODEL), D_MODEL),
        "g_post_mix": gain(ks[13], (DEPTH, D_MODEL)),
        "g_pre_xa": gain(ks[14], (DEPTH, D_MODEL)),
        "g_mem": gain(ks[15], (DEPTH, D_MODEL)),
        "w_xq": dense(ks[16], (DEPTH, D_MODEL, D_MODEL), D_MODEL),
        "w_xkv": dense(ks[17], (DEPTH, D_MODEL, 2 * D_MODEL), D_MODEL),
        "w_xo": dense(ks[18], (DEPTH, D_MODEL, D_MODEL), D_MODEL),
        "g_post_xa": gain(ks[19], (DEPTH, D_MODEL)),
        "g_pre_ffn": gain(ks[20], (DEPTH, D_MODEL)),
        "w_gu": dense(ks[21], (DEPTH, D_MODEL, 2 * FFN_HIDDEN), D_MODEL),
        "w_down": dense(ks[22], (DEPTH, FFN_HIDDEN, D_MODEL), FFN_HIDDEN),
        "g_post_ffn": gain(ks[23], (DEPTH, D_MODEL)),
    }

def first_block(x, mem, g_pre_mix, w_in, conv_w, conv_b, dt_bias, a_log, d_skip, g_ssm_norm,
              w_br_att, w_br_ssm, w_mix_out, g_post_mix, g_pre_xa, g_mem, w_xq, w_xkv, w_xo,
              g_post_xa, g_pre_ffn, w_gu, w_down, g_post_ffn):
    bsz, seq = x.shape[0], x.shape[1]
    for l in range(DEPTH):
        h = rms_norm(x, g_pre_mix[l])
        q, k, v, z, xbc, dt_raw, ga, gs = _split(h @ w_in[l], IN_SIZES)
        o_att = stick_breaking_attention(
            q.reshape(bsz, seq, SB_HEADS, SB_HEAD_DIM),
            k.reshape(bsz, seq, SB_HEADS, SB_HEAD_DIM),
            v.reshape(bsz, seq, SB_HEADS, SB_HEAD_DIM)).astype(x.dtype)
        o_ssm = ssd_branch(z, xbc, dt_raw, conv_w[l], conv_b[l], dt_bias[l], a_log[l],
                           d_skip[l], g_ssm_norm[l]).astype(x.dtype)
        merged = jax.nn.sigmoid(ga) * (o_att @ w_br_att[l]) + jax.nn.sigmoid(gs) * (o_ssm @ w_br_ssm[l])
        x = x + rms_norm(merged @ w_mix_out[l], g_post_mix[l])
        h = rms_norm(x, g_pre_xa[l])
        mem_n = rms_norm(mem, g_mem[l])
        x = x + rms_norm(memory_cross_attention(h, mem_n, w_xq[l], w_xkv[l], w_xo[l]), g_post_xa[l])
        h = rms_norm(x, g_pre_ffn[l])
        x = x + rms_norm(swiglu(h, w_gu[l], w_down[l]), g_post_ffn[l])
    return x


DEPTH_2 = 2

N_MIXERS = 3
HEAD_DIM = 64
N_MIX_HEADS = 12
MIX_WIDTH = N_MIX_HEADS * HEAD_DIM
N_MEM_HEADS = 4
MEM_WIDTH = N_MEM_HEADS * HEAD_DIM
OUT_WIDTH = MIX_WIDTH + MEM_WIDTH
Q_BLOCK = 128
MLA_Q_RANK = 256
MLA_KV_RANK = 128
MLA_NOPE_DIM = 64
MLA_ROPE_DIM = 32
MLA_QK_DIM = MLA_NOPE_DIM + MLA_ROPE_DIM
MLA_V_DIM = 64
ROPE_THETA = 10000.0
MOBA_BLOCK = 256
MOBA_TOPK = 3
D_FF = 2816
CONV_WIDTH = 3
EPS = 1e-6
POS_OFFSET_MAX = 1024

FOX_IN = 3 * MIX_WIDTH + N_MIX_HEADS + MEM_WIDTH
MLA_IN = MLA_Q_RANK + MLA_KV_RANK + MLA_ROPE_DIM + MEM_WIDTH
MOBA_IN = 3 * MIX_WIDTH + MEM_WIDTH


def rmsnorm(x, g):
    xf = x.astype(jnp.float32)
    y = xf * lax.rsqrt(jnp.mean(xf * xf, axis=-1, keepdims=True) + EPS)
    return (y * g.astype(jnp.float32)).astype(x.dtype)

def alibi_slopes(n_heads):
    return 2.0 ** (-8.0 * jnp.arange(1, n_heads + 1, dtype=jnp.float32) / n_heads)

def rope(x, cos, sin):
    half = x.shape[-1] // 2
    x1, x2 = x[..., :half], x[..., half:]
    return jnp.concatenate([x1 * cos - x2 * sin, x1 * sin + x2 * cos], axis=-1)

def to_heads(t, n_heads):
    b, s, _ = t.shape
    return t.reshape(b, s, n_heads, -1).transpose(0, 2, 1, 3)

def from_heads(t):
    b, h, s, d = t.shape
    return t.transpose(0, 2, 1, 3).reshape(b, s, h * d)

def causal_block_attention(q, k, v, log_decay=None):
    b, h, s, dk = q.shape
    nq = s // Q_BLOCK
    q_chunks = q.reshape(b, h, nq, Q_BLOCK, dk).transpose(2, 0, 1, 3, 4)
    key_idx = jnp.arange(s)
    xs = [q_chunks, jnp.arange(nq)]
    if log_decay is not None:
        xs.append(log_decay.reshape(b, h, nq, Q_BLOCK).transpose(2, 0, 1, 3))

    def step(args):
        qc, i = args[0], args[1]
        logits = jnp.einsum('bhqd,bhkd->bhqk', qc, k).astype(jnp.float32)
        if log_decay is not None:
            logits = logits + args[2][..., None] - log_decay[:, :, None, :]
        q_idx = i * Q_BLOCK + jnp.arange(Q_BLOCK)
        logits = jnp.where(key_idx[None, :] <= q_idx[:, None], logits, -jnp.inf)
        p = jax.nn.softmax(logits, axis=-1).astype(v.dtype)
        return jnp.einsum('bhqk,bhkd->bhqd', p, v)

    out = lax.map(step, tuple(xs))
    return out.transpose(1, 2, 0, 3, 4).reshape(b, h, s, v.shape[-1])

def fox_mixer(p, b_f, q_gain, k_gain):
    q, k, v, f = jnp.split(p, [MIX_WIDTH, 2 * MIX_WIDTH, 3 * MIX_WIDTH], axis=-1)
    q = rmsnorm(to_heads(q, N_MIX_HEADS), q_gain) * HEAD_DIM ** -0.5
    k = rmsnorm(to_heads(k, N_MIX_HEADS), k_gain)
    log_f = jax.nn.log_sigmoid(f.astype(jnp.float32) + b_f.astype(jnp.float32))
    cum = lax.cumsum(log_f, axis=1).transpose(0, 2, 1)
    return from_heads(causal_block_attention(q, k, to_heads(v, N_MIX_HEADS), cum))

def mla_mixer(p, cos, sin, qa_norm, kva_norm, w_q_up, w_kv_up, q_gain, k_gain):
    b, s, _ = p.shape
    q_lat, kv_lat, k_r = jnp.split(p, [MLA_Q_RANK, MLA_Q_RANK + MLA_KV_RANK], axis=-1)
    q = (rmsnorm(q_lat, qa_norm) @ w_q_up).reshape(b, s, N_MIX_HEADS, MLA_QK_DIM)
    kv = (rmsnorm(kv_lat, kva_norm) @ w_kv_up).reshape(b, s, N_MIX_HEADS, MLA_NOPE_DIM + MLA_V_DIM)
    q = jnp.concatenate([q[..., :MLA_NOPE_DIM], rope(q[..., MLA_NOPE_DIM:], cos, sin)], axis=-1)
    k_rope = jnp.broadcast_to(rope(k_r[:, :, None, :], cos, sin), (b, s, N_MIX_HEADS, MLA_ROPE_DIM))
    k = jnp.concatenate([kv[..., :MLA_NOPE_DIM], k_rope], axis=-1)
    v = kv[..., MLA_NOPE_DIM:]
    q = rmsnorm(q, q_gain).transpose(0, 2, 1, 3) * MLA_QK_DIM ** -0.5
    k = rmsnorm(k, k_gain).transpose(0, 2, 1, 3)
    return from_heads(causal_block_attention(q, k, v.transpose(0, 2, 1, 3)))

def moba_attention(q, k, v, positions, slopes):
    b, h, s, d = q.shape
    nb = -(-s // MOBA_BLOCK)
    pad = nb * MOBA_BLOCK - s
    kb = jnp.pad(k, ((0, 0), (0, 0), (0, pad), (0, 0))).reshape(b, h, nb, MOBA_BLOCK, d)
    vb = jnp.pad(v, ((0, 0), (0, 0), (0, pad), (0, 0))).reshape(b, h, nb, MOBA_BLOCK, d)
    posb = jnp.pad(positions, ((0, 0), (0, pad))).reshape(b, nb, MOBA_BLOCK)
    n_sel = min(MOBA_TOPK, nb - 1)
    nq = s // Q_BLOCK

    def chunks(t):
        tail = t.shape[3:]
        t = t.reshape((b, h, nq, Q_BLOCK) + tail)
        perm = (0, 2, 1, 3) + tuple(range(4, t.ndim))
        return t.transpose(perm).reshape((b * nq, h, Q_BLOCK) + tail)

    xs = [chunks(q), positions.reshape(b * nq, Q_BLOCK),
          jnp.repeat(jnp.arange(b), nq), jnp.tile(jnp.arange(nq), b)]
    if n_sel > 0:
        k_mean = kb.mean(axis=3)
        gate = jnp.einsum('bhsd,bhnd->bhsn', q, k_mean).astype(jnp.float32)
        q_blk = jnp.arange(s) // MOBA_BLOCK
        gate = jnp.where(jnp.arange(nb)[None, :] < q_blk[:, None], gate, -jnp.inf)
        g_val, g_idx = lax.top_k(gate, n_sel)
        xs += [chunks(g_idx), chunks(jnp.isfinite(g_val))]

    def step(args):
        qc, pq, bi, ci = args[0], args[1], args[2], args[3]
        t_idx = ci * Q_BLOCK + jnp.arange(Q_BLOCK)
        own = (ci * Q_BLOCK) // MOBA_BLOCK
        kb_b, vb_b, posb_b = kb[bi], vb[bi], posb[bi]
        k_own = lax.dynamic_index_in_dim(kb_b, own, axis=1, keepdims=False)
        v_own = lax.dynamic_index_in_dim(vb_b, own, axis=1, keepdims=False)
        pos_own = lax.dynamic_index_in_dim(posb_b, own, axis=0, keepdims=False)
        dist_own = (pq[:, None] - pos_own[None, :]).astype(jnp.float32)
        s_own = (jnp.einsum('hqd,hjd->hqj', qc, k_own).astype(jnp.float32)
                 - slopes[:, None, None] * dist_own[None])
        own_idx = own * MOBA_BLOCK + jnp.arange(MOBA_BLOCK)
        s_own = jnp.where(own_idx[None, None, :] <= t_idx[None, :, None], s_own, -jnp.inf)
        if n_sel == 0:
            p_own = jax.nn.softmax(s_own, axis=-1).astype(v.dtype)
            return jnp.einsum('hqj,hjd->hqd', p_own, v_own)
        idx, ok = args[4], args[5]
        k_sel = jax.vmap(lambda blocks, i: blocks[i])(kb_b, idx)
        v_sel = jax.vmap(lambda blocks, i: blocks[i])(vb_b, idx)
        dist_sel = (pq[None, :, None, None] - posb_b[idx]).astype(jnp.float32)
        s_sel = (jnp.einsum('hqd,hqkjd->hqkj', qc, k_sel).astype(jnp.float32)
                 - slopes[:, None, None, None] * dist_sel)
        s_sel = jnp.where(ok[..., None], s_sel, -jnp.inf).reshape(h, Q_BLOCK, n_sel * MOBA_BLOCK)
        p = jax.nn.softmax(jnp.concatenate([s_sel, s_own], axis=-1), axis=-1).astype(v.dtype)
        p_sel = p[..., :n_sel * MOBA_BLOCK].reshape(h, Q_BLOCK, n_sel, MOBA_BLOCK)
        p_own = p[..., n_sel * MOBA_BLOCK:]
        return (jnp.einsum('hqkj,hqkjd->hqd', p_sel, v_sel)
                + jnp.einsum('hqj,hjd->hqd', p_own, v_own))

    out = lax.map(step, tuple(xs))
    return out.reshape(b, nq, h, Q_BLOCK, d).transpose(0, 2, 1, 3, 4).reshape(b, h, s, d)

def moba_mixer(p, positions, q_gain, k_gain):
    q, k, v = jnp.split(p, [MIX_WIDTH, 2 * MIX_WIDTH], axis=-1)
    q = rmsnorm(to_heads(q, N_MIX_HEADS), q_gain) * HEAD_DIM ** -0.5
    k = rmsnorm(to_heads(k, N_MIX_HEADS), k_gain)
    out = moba_attention(q, k, to_heads(v, N_MIX_HEADS), positions, alibi_slopes(N_MIX_HEADS))
    return from_heads(out)

def memory_cross(qm, k_mem, v_mem, q_gain, k_gain):
    b, s, _ = qm.shape
    q = rmsnorm(qm.reshape(b, s, N_MEM_HEADS, HEAD_DIM), q_gain) * HEAD_DIM ** -0.5
    k = rmsnorm(k_mem, k_gain)
    logits = jnp.einsum('bshd,bmhd->bhsm', q, k).astype(jnp.float32)
    p = jax.nn.softmax(logits, axis=-1).astype(v_mem.dtype)
    return jnp.einsum('bhsm,bmhd->bshd', p, v_mem).reshape(b, s, MEM_WIDTH)

def conv_ffn(h, w_up, conv_w, conv_b, w_down):
    u = h @ w_up
    c = u.shape[-1]
    u = lax.conv_general_dilated(u, conv_w[:, None, :].astype(u.dtype), window_strides=(1,),
                                 padding=[(CONV_WIDTH - 1, 0)],
                                 dimension_numbers=('NWC', 'WIO', 'NWC'),
                                 feature_group_count=c) + conv_b
    gate, val = jnp.split(u, 2, axis=-1)
    return (jax.nn.silu(gate) * val) @ w_down

def second_inputs(seed: int = 0) -> dict:
    key = jax.random.key(seed)
    ks = iter(jax.random.split(key, 32))
    f32 = jnp.float32

    def dense(shape):
        return jax.random.normal(next(ks), shape, f32) * shape[-2] ** -0.5

    def gain(shape):
        return 1.0 + 0.05 * jax.random.normal(next(ks), shape, f32)

    n_fox = len(range(0, DEPTH_2, N_MIXERS))
    n_mla = len(range(1, DEPTH_2, N_MIXERS))
    n_moba = len(range(2, DEPTH_2, N_MIXERS))
    x = jax.random.normal(next(ks), (BATCH, SEQ, D_MODEL), f32)
    mem = jax.random.normal(next(ks), (BATCH, MEM_LEN, D_MODEL), f32)
    positions = (jnp.arange(SEQ, dtype=jnp.int32)[None, :]
                 + jax.random.randint(next(ks), (BATCH, 1), 0, POS_OFFSET_MAX, dtype=jnp.int32))
    return {
        'x': x,
        'mem': mem,
        'positions': positions,
        'norm_mix': gain((DEPTH_2, D_MODEL)),
        'norm_ffn': gain((DEPTH_2, D_MODEL)),
        'w_out': dense((DEPTH_2, OUT_WIDTH, D_MODEL)),
        'mem_norm': gain((D_MODEL,)),
        'w_mem_kv': dense((D_MODEL, 2 * MEM_WIDTH)),
        'mem_q_gain': gain((DEPTH_2, HEAD_DIM)),
        'mem_k_gain': gain((DEPTH_2, HEAD_DIM)),
        'fox_w_in': dense((n_fox, D_MODEL, FOX_IN)),
        'fox_b_f': jax.random.uniform(next(ks), (n_fox, N_MIX_HEADS), f32, 1.0, 5.0),
        'fox_q_gain': gain((n_fox, HEAD_DIM)),
        'fox_k_gain': gain((n_fox, HEAD_DIM)),
        'mla_w_in': dense((n_mla, D_MODEL, MLA_IN)),
        'mla_qa_norm': gain((n_mla, MLA_Q_RANK)),
        'mla_kva_norm': gain((n_mla, MLA_KV_RANK)),
        'mla_w_q_up': dense((n_mla, MLA_Q_RANK, N_MIX_HEADS * MLA_QK_DIM)),
        'mla_w_kv_up': dense((n_mla, MLA_KV_RANK, N_MIX_HEADS * (MLA_NOPE_DIM + MLA_V_DIM))),
        'mla_q_gain': gain((n_mla, MLA_QK_DIM)),
        'mla_k_gain': gain((n_mla, MLA_QK_DIM)),
        'moba_w_in': dense((n_moba, D_MODEL, MOBA_IN)),
        'moba_q_gain': gain((n_moba, HEAD_DIM)),
        'moba_k_gain': gain((n_moba, HEAD_DIM)),
        'ffn_w_up': dense((DEPTH_2, D_MODEL, 2 * D_FF)),
        'ffn_conv_w': dense((DEPTH_2, CONV_WIDTH, 2 * D_FF)),
        'ffn_conv_b': 0.01 * jax.random.normal(next(ks), (DEPTH_2, 2 * D_FF), f32),
        'ffn_w_down': dense((DEPTH_2, D_FF, D_MODEL)),
    }

def second_block(x, mem, positions, norm_mix, norm_ffn, w_out, mem_norm, w_mem_kv, mem_q_gain,
              mem_k_gain, fox_w_in, fox_b_f, fox_q_gain, fox_k_gain, mla_w_in, mla_qa_norm,
              mla_kva_norm, mla_w_q_up, mla_w_kv_up, mla_q_gain, mla_k_gain, moba_w_in,
              moba_q_gain, moba_k_gain, ffn_w_up, ffn_conv_w, ffn_conv_b, ffn_w_down):
    b, m = mem.shape[0], mem.shape[1]
    mem_kv = rmsnorm(mem, mem_norm) @ w_mem_kv
    k_mem = mem_kv[..., :MEM_WIDTH].reshape(b, m, N_MEM_HEADS, HEAD_DIM)
    v_mem = mem_kv[..., MEM_WIDTH:].reshape(b, m, N_MEM_HEADS, HEAD_DIM)
    inv_freq = ROPE_THETA ** (-jnp.arange(0, MLA_ROPE_DIM, 2, dtype=jnp.float32) / MLA_ROPE_DIM)
    ang = positions.astype(jnp.float32)[..., None] * inv_freq
    cos = jnp.cos(ang)[:, :, None, :].astype(x.dtype)
    sin = jnp.sin(ang)[:, :, None, :].astype(x.dtype)

    for i in range(DEPTH_2):
        kind, j = i % N_MIXERS, i // N_MIXERS
        h = rmsnorm(x, norm_mix[i])
        if kind == 0:
            p = h @ fox_w_in[j]
            o_mix = fox_mixer(p[..., :-MEM_WIDTH], fox_b_f[j], fox_q_gain[j], fox_k_gain[j])
        elif kind == 1:
            p = h @ mla_w_in[j]
            o_mix = mla_mixer(p[..., :-MEM_WIDTH], cos, sin, mla_qa_norm[j], mla_kva_norm[j],
                              mla_w_q_up[j], mla_w_kv_up[j], mla_q_gain[j], mla_k_gain[j])
        else:
            p = h @ moba_w_in[j]
            o_mix = moba_mixer(p[..., :-MEM_WIDTH], positions, moba_q_gain[j], moba_k_gain[j])
        o_mem = memory_cross(p[..., -MEM_WIDTH:], k_mem, v_mem, mem_q_gain[i], mem_k_gain[i])
        x = x + jnp.concatenate([o_mix, o_mem], axis=-1) @ w_out[i]
        x = x + conv_ffn(rmsnorm(x, norm_ffn[i]), ffn_w_up[i], ffn_conv_w[i], ffn_conv_b[i],
                         ffn_w_down[i])
    return x


def setup_inputs(seed=0):
    out = dict(first_inputs(seed))
    for name, value in second_inputs(seed + 1).items():
        if name != "x":
            out[name + "_2"] = value
    return out


def reference(
    x, mem, g_pre_mix, w_in, conv_w, conv_b, dt_bias, a_log, d_skip, g_ssm_norm, w_br_att,
    w_br_ssm, w_mix_out, g_post_mix, g_pre_xa, g_mem, w_xq, w_xkv, w_xo, g_post_xa, g_pre_ffn,
    w_gu, w_down, g_post_ffn, mem_2, positions_2, norm_mix_2, norm_ffn_2, w_out_2, mem_norm_2,
    w_mem_kv_2, mem_q_gain_2, mem_k_gain_2, fox_w_in_2, fox_b_f_2, fox_q_gain_2, fox_k_gain_2,
    mla_w_in_2, mla_qa_norm_2, mla_kva_norm_2, mla_w_q_up_2, mla_w_kv_up_2, mla_q_gain_2,
    mla_k_gain_2, moba_w_in_2, moba_q_gain_2, moba_k_gain_2, ffn_w_up_2, ffn_conv_w_2,
    ffn_conv_b_2, ffn_w_down_2,
):
    x = first_block(
        x, mem, g_pre_mix, w_in, conv_w, conv_b, dt_bias, a_log, d_skip, g_ssm_norm, w_br_att,
        w_br_ssm, w_mix_out, g_post_mix, g_pre_xa, g_mem, w_xq, w_xkv, w_xo, g_post_xa,
        g_pre_ffn, w_gu, w_down, g_post_ffn,
    )
    return second_block(
        x, mem_2, positions_2, norm_mix_2, norm_ffn_2, w_out_2, mem_norm_2, w_mem_kv_2,
        mem_q_gain_2, mem_k_gain_2, fox_w_in_2, fox_b_f_2, fox_q_gain_2, fox_k_gain_2,
        mla_w_in_2, mla_qa_norm_2, mla_kva_norm_2, mla_w_q_up_2, mla_w_kv_up_2, mla_q_gain_2,
        mla_k_gain_2, moba_w_in_2, moba_q_gain_2, moba_k_gain_2, ffn_w_up_2, ffn_conv_w_2,
        ffn_conv_b_2, ffn_w_down_2,
    )


_drawn_inputs = setup_inputs


def setup_inputs(seed=0):
    import zlib

    import numpy as np

    out = dict(_drawn_inputs(seed))
    spreads = {}
    factors = {'conv_b': 5.692,
     'g_ssm_norm': 3.977,
     'g_post_mix': 3.158,
     'g_pre_xa': 4.147,
     'g_mem': 2.731,
     'g_post_xa': 3.94,
     'g_pre_ffn': 3.745,
     'g_post_ffn': 5.345,
     'norm_mix_2': 3.481,
     'mem_norm_2': 8.0,
     'mem_q_gain_2': 8.0,
     'mem_k_gain_2': 8.0,
     'fox_q_gain_2': 8.0,
     'fox_k_gain_2': 8.0,
     'mla_qa_norm_2': 8.0,
     'mla_kva_norm_2': 5.242,
     'mla_q_gain_2': 8.0,
     'mla_k_gain_2': 8.0,
     'ffn_conv_b_2': 8.0}
    for name, (base, spread) in spreads.items():
        noise = np.random.default_rng([zlib.crc32(name.encode()), seed]).standard_normal(out[name].shape)
        drawn = base * np.exp(spread * noise) if base else spread * noise
        out[name] = jnp.asarray(drawn.astype(out[name].dtype))
    for name, factor in factors.items():
        out[name] = (out[name] * factor).astype(out[name].dtype)
    return out
```

```python
from contextlib import ExitStack, contextmanager
import math

import concourse.bass as bass
from concourse import mybir

F32 = mybir.dt.float32
F32R = mybir.dt.float32r
I32 = mybir.dt.int32
ALU = mybir.AluOpType
ACT = mybir.ActivationFunctionType
AX = mybir.AxisListType.X
ENG = mybir.EngineType

P = 128
SEQ = 256
MT = SEQ // P
D = 1024
KD = D // P
EPS = 1e-6
SLOTS = 4
PIECE = 2048
NEG = -1.0e30

SB_HEADS, SB_DIM = 16, 64
SSM_INNER, SSM_HEADS, SSM_HD, SSM_GROUPS, SSM_STATE = 2048, 32, 64, 4, 128
XBC = SSM_INNER + 2 * SSM_GROUPS * SSM_STATE
GROUP_HEADS = SSM_HEADS // SSM_GROUPS
XA_HEADS, XA_DIM = 4, 256
FFN = 2816
FT = FFN // P
C_Q, C_K, C_V, C_Z = 0, D, 2 * D, 3 * D
C_XBC = C_Z + SSM_INNER
C_DT = C_XBC + XBC
C_GA = C_DT + SSM_HEADS
C_GS = C_GA + D

HEADS, HD = 12, 64
MIX = HEADS * HD
MEM_HEADS = 4
MEM_W = MEM_HEADS * HD
FOX_IN = 3 * MIX + HEADS + MEM_W
Q_RANK, KV_RANK, ROPE = 256, 128, 32
QK = HD + ROPE
MLA_IN = Q_RANK + KV_RANK + ROPE + MEM_W


class Count:

    def __init__(self, core, name, unit=1):
        self.name, self.unit = name, unit
        self.sem = core.ctx.enter_context(core.nc.semaphore(name))
        self.base, self.k, self.least = 0, 0, 0
        core.counts.append(self)

    def value(self):
        return self.base + self.k

    def mark(self, ins, units=1):
        ins.then_inc(self.sem, self.unit * units)
        self.k += units
        return self.now()

    def now(self, ahead=0):
        return (self, self.base, self.k + ahead)


class Lane:

    def __init__(self, core, engine, name):
        self.e = engine
        self.done = Count(core, name + "_done")
        self.seen = {}
        self.gate = core.ctx.enter_context(core.nc.semaphore(name + "_gate")) if name == "pool" else None

    def after(self, *tokens):
        computed = False
        for count, base, k in tokens:
            if isinstance(base, int) and base + k <= 0:
                continue
            key = (count.name, base if isinstance(base, int) else id(base))
            if self.seen.get(key, -1 << 30) >= k:
                continue
            self.seen[key] = k
            self.e.wait_ge(count.sem, (base + k) * count.unit)
            if not isinstance(base, int):
                assert count.least + k > 0, count.name
                computed = True
        if computed and self.gate is not None:
            self.e.sem_inc(self.gate)
        return self

    def do(self, ins, by=None):
        return (by or self.done).mark(ins)


class Core:
    def __init__(self, nc, ctx, strides):
        self.nc, self.ctx, self.strides, self.new_strides, self.counts = nc, ctx, strides, {}, []
        self.pe = Lane(self, nc.tensor, "pe")
        self.act = Lane(self, nc.scalar, "act")
        self.dve = Lane(self, nc.vector, "dve")
        self.pool = Lane(self, nc.gpsimd, "pool")
        self.lanes = [self.pe, self.act, self.dve, self.pool]
        self.piece = 0

    def sb(self, name, shape, dt=F32, ctx=None):
        return (ctx or self.ctx).enter_context(self.nc.sbuf_tensor(name, shape, dt))

    def forget(self):
        for lane in self.lanes:
            lane.seen = {}

    @contextmanager
    def loop(self, name, n):
        stride = self.strides.get(name, {})
        for c in self.counts:
            if c.k == 0 and isinstance(c.base, int) and c.base == 0 and stride.get(c.name):
                self.nc.vector.sem_inc(c.sem, c.unit)
                c.k = 1
        starts = {c.name: (c.base + c.k) for c in self.counts}
        piece = self.piece
        self.forget()
        with self.nc.Fori(0, n, engines=[ENG.PE, ENG.Activation, ENG.DVE, ENG.Pool]) as i:
            for c in self.counts:
                d = stride.get(c.name, 0)
                c.base, c.k = (i * d + starts[c.name] if d else starts[c.name]), 0
                c.least = starts[c.name]
            yield i
        self.new_strides[name] = {c.name: c.k for c in self.counts if c.k}
        for c in self.counts:
            c.base, c.k = starts[c.name] + n * c.k, 0
        self.piece = piece + n * (self.piece - piece)
        self.forget()

    def fence(self, *lanes):
        for lane in lanes or self.lanes:
            lane.after(*[c.now() for c in self.counts if c.unit == 1])


def emit(nc, ins, out, strides):
    with ExitStack() as ctx:
        core = Core(nc, ctx, strides)
        program(core, ins, out)
        return core.new_strides


def program(core, ins, out):
    nc, pe, act, dve, pool = core.nc, core.pe, core.act, core.dve, core.pool
    sp = nc.sync
    sb = core.sb

    def count(name, unit=1):
        return Count(core, name, unit)

    raw = sb("raw", [P, SLOTS, PIECE])
    w_hi = sb("w_hi", [P, SLOTS, PIECE], F32R)
    w_lo = sb("w_lo", [P, SLOTS, PIECE], F32R)
    x_hi = sb("x_hi", [P, KD, SEQ], F32R)
    x_lo = sb("x_lo", [P, KD, SEQ], F32R)
    y_hi = sb("y_hi", [P, 2 * KD, SEQ], F32R)
    y_lo = sb("y_lo", [P, 2 * KD, SEQ], F32R)
    res = sb("res", [P, MT, D])
    ident = sb("ident", [P, P])
    ones = sb("ones", [P, P])
    upto = sb("upto", [P, P])
    beyond = sb("beyond", [P, P])
    neg_from = sb("neg_from", [P, P])
    neg_ones = sb("neg_ones", [P, P])
    strict = sb("strict", [P, P])
    causal = sb("causal", [P, P])
    half_neg = sb("half_neg", [P, 64])
    cols = sb("cols", [P, 5 * P])
    small = sb("small", [P, 256])
    psum_a = ctx_psum(core, "psum_a", [P, 1024])
    psum_b = ctx_psum(core, "psum_b", [P, 1024])
    psum_c = ctx_psum(core, "psum_c", [P, 2048])

    arrived = [count(f"arrived{s}", 16) for s in range(SLOTS)]
    rounded = count("rounded")
    split = count("split")
    used = count("used")
    a_free = count("a_free")
    b_free = count("b_free")
    loaded = count("loaded", 16)
    stored = count("stored", 16)
    rows_loaded = count("rows_loaded", 16)

    w_in = ins["w_in"][0].rearrange("(k p) n -> p k n", p=P)

    def block(w, k0, nk, col, n):
        view = w.rearrange("(k p) n -> p k n", p=P)
        return [(0, nk, n, view[:, k0:k0 + nk, bass.ds(col, n)])]

    def gate_up(w, h):
        view = w.rearrange("(k p) n -> p k n", p=P)
        return [(j * P, KD, 2 * P, view[:, :, bass.ds(h * P + j * FFN, P)]) for j in range(2)]

    def down(w, h):
        view = w.rearrange("(k p) n -> k p n", p=P)
        return [(0, 1, D, view[bass.ds(h, 1), :, :].rearrange("k p n -> p k n"))]

    def halves(w, col, n=512, k0=0):
        return [block(w, k0, 4, col, n), block(w, k0 + 4, 4, col, n)]

    def square(w, col=0):
        return [q for c in range(2) for q in halves(w, col + 512 * c)]

    W = {k: v[0] for k, v in ins.items() if len(v.shape) == 3 and k.startswith(("w_", "fox_w", "mla_w"))}
    win = W["w_in"]

    def ffn_entries(gu, dn):
        return [("once", [gate_up(gu, 0)]),
                ("loop", (FT - 2) // 2, lambda i: [q for u in (1, 2) for q in (
                    gate_up(gu, i * 2 + u), down(dn, i * 2 + (u - 1)))]),
                ("once", [gate_up(gu, FT - 1), down(dn, FT - 2), down(dn, FT - 1)])]

    wo2 = ins["w_out_2"]
    plan = [("once", square(win, C_Q) + square(win, C_K) + square(win, C_V)),
            ("once", square(win, C_GA) + square(W["w_br_att"])),
            ("loop", 2, lambda i: [q for c in range(2) for q in halves(win, i * 1024 + (C_XBC + 512 * c))]),
            ("once", square(win, C_XBC + SSM_INNER) + halves(win, C_DT, SSM_HEADS)),
            ("loop", 2, lambda i: [q for c in range(2) for q in halves(win, i * 1024 + (C_Z + 512 * c))]),
            ("once", square(win, C_GS) + [q for c in range(2) for k0 in (0, KD) for q in halves(W["w_br_ssm"], 512 * c, k0=k0)]),
            ("once", square(W["w_mix_out"])),
            ("once", square(W["w_xkv"]) + square(W["w_xkv"], D) + square(W["w_xq"]) + square(W["w_xo"])),
            *ffn_entries(W["w_gu"], W["w_down"]),
            ("once", halves(ins["w_mem_kv_2"], 0)),
            ("once", [q for c in range(5) for q in halves(W["fox_w_in_2"], 512 * c)] + halves(W["fox_w_in_2"], 2560, FOX_IN - 2560)),
            ("once", square(wo2[0])),
            *ffn_entries(ins["ffn_w_up_2"][0], ins["ffn_w_down_2"][0]),
            ("once", halves(W["mla_w_in_2"], 0) + halves(W["mla_w_in_2"], 512, MLA_IN - 512)),
            ("once", [block(W["mla_w_q_up_2"], 0, 2, 0, 1024), block(W["mla_w_q_up_2"], 0, 2, 1024, HEADS * QK - 1024),
                      block(W["mla_w_kv_up_2"], 0, 1, 0, 1024), block(W["mla_w_kv_up_2"], 0, 1, 1024, 512)]),
            ("once", square(wo2[1])),
            *ffn_entries(ins["ffn_w_up_2"][1], ins["ffn_w_down_2"][1])]
    shapes = []
    for kind, *rest in plan:
        for q in (rest[0] if kind == "once" else rest[1](0) * rest[0]):
            shapes.append((q[0][1] * q[0][2], len(q)))

    def weight_stream():
        at = 0

        def load(pieces, at0, step):
            for j, parts in enumerate(pieces):
                s = (at0 + j) % SLOTS
                need = step + (at0 + j - SLOTS + 1)
                if not isinstance(need, int) or need > 0:
                    sp.wait_ge(split.sem, need)
                for off, nk, n, src in parts:
                    dst = raw[:, s, 0:nk * n].rearrange("p (k n) -> p k n", n=n)[:, :, off:off + src.shape[2]]
                    sp.dma_start(dst, src).then_inc(arrived[s].sem, 16)

        for kind, *rest in plan:
            if kind == "once":
                load(rest[0], at, 0)
                at += len(rest[0])
            else:
                n, pieces = rest
                per = len(pieces(0))
                assert per % SLOTS == 0 and at >= SLOTS
                with sp.Fori(0, n) as i:
                    load(pieces(i), at, i * per)
                at += n * per

    split_at = [0]

    def split_ahead(n=2):
        for _ in range(n):
            if split_at[0] >= len(shapes):
                return
            size, loads = shapes[split_at[0]]
            s = split_at[0] % SLOTS
            split_at[0] += 1
            arrived[s].k += loads
            act.after(arrived[s].now(), (used, rounded.base, rounded.k + 1 - SLOTS))
            act.do(nc.scalar.activation(w_hi[:, s, 0:size], raw[:, s, 0:size], ACT.Copy), rounded)
            dve.after(rounded.now())
            dve.do(nc.vector.tensor_tensor(w_lo[:, s, 0:size], raw[:, s, 0:size],
                                           w_hi[:, s, 0:size].bitcast(F32), ALU.subtract), split)

    @contextmanager
    def loop(name, n):
        start = split_at[0]
        with core.loop(name, n) as i:
            yield i
        split_at[0] = start + n * (split_at[0] - start)

    def three(out_ap, l, r, start, stop):
        nc.tensor.matmul(out_ap, l[0], r[0], start=start, stop=False, skip_group_check=True)
        nc.tensor.matmul(out_ap, l[0], r[1], start=False, stop=False, skip_group_check=True)
        return nc.tensor.matmul(out_ap, l[1], r[0], start=False, stop=stop, skip_group_check=True)

    def take_piece():
        s = core.piece % SLOTS
        core.piece += 1
        pe.after((split, used.base, used.k + 1))
        return s

    def weights(s, nk, n):
        return [w[:, s, 0:nk * n].rearrange("p (k n) -> p k n", n=n) for w in (w_hi, w_lo)]

    X, Y = (x_hi, x_lo), (y_hi, y_lo)

    def product_turned(ps, act_in, k0=0, first=True, last=True):
        for half in range(2):
            s = take_piece()
            w = weights(s, 4, 512)
            for k in range(4):
                kk = half * 4 + k
                for c in range(4):
                    mm = three(ps[:, c * SEQ:(c + 1) * SEQ], [x[:, k, c * P:(c + 1) * P] for x in w],
                               [x[:, k0 + kk, :] for x in act_in], first and kk == 0 and c % 2 == 0, last and kk == 7)
            pe.do(mm, used)

    def product_natural(ps, act_in, n=512):
        for half in range(2):
            s = take_piece()
            w = weights(s, 4, n)
            for k in range(4):
                kk = half * 4 + k
                for m in range(MT):
                    mm = three(ps[:, m * 512:m * 512 + n], [x[:, kk, m * P:(m + 1) * P] for x in act_in],
                               [x[:, k, :] for x in w], kk == 0, kk == 7)
            pe.do(mm, used)

    banks = [(psum_a, a_free), (psum_b, b_free)]
    turn = [0]

    def next_bank():
        ps, free = banks[turn[0] % 2]
        turn[0] += 1
        pe.after(free.now())
        return ps, free

    def run_product(kind, act_in, evacuate, **kw):
        ps, free = next_bank()
        kind(ps, act_in, **kw)
        split_ahead()
        evacuate(ps, free, used.now())

    def seq(lane, *steps):
        t = None
        for f in steps:
            if t:
                lane.after(t)
            t = lane.do(f())
        return t

    def round_split(hi, lo, src_f32, ready, free=None, scale=None):
        act.after(ready)
        sc = 1.0 if scale is None else scale
        t = act.do(nc.scalar.activation(hi, src_f32, ACT.Copy, scale=sc))
        dve.after(t, ready)
        return dve.do(nc.vector.scalar_tensor_tensor(out=lo, in0=src_f32, scalar=sc, in1=hi.bitcast(F32),
                                                     op0=ALU.mult, op1=ALU.subtract), free)

    def power(out_ap, in_ap, n, ready):
        pool.after(ready)
        return pool.do(nc.gpsimd.tensor_tensor(out_ap, in_ap, half_neg[:, 0:n], ALU.pow))

    def row_rstd(parts, width, slot, ready, junk):
        n = len(parts)
        act.after(*ready)
        for j, part in enumerate(parts):
            act.after(act.done.now())
            t = act.do(nc.scalar.activation(junk[:, 0:width], part, ACT.Square, accum_out=small[:, slot + j:slot + j + 1]))
        dve.after(t)
        t = dve.do(nc.vector.tensor_scalar(small[:, slot:slot + n], small[:, slot:slot + n], 1.0 / width, EPS, ALU.mult, ALU.add))
        return power(small[:, slot + n:slot + 2 * n], small[:, slot:slot + n], n, t)

    def turn_and_split(src, dst, kd, gain, ready, k_to=0):
        t = None
        for k in range(kd):
            ps, free = banks[k % 2]
            pe.after(ready, free.now())
            for m in range(MT):
                mm = nc.tensor.transpose(ps[:, m * P:(m + 1) * P], src[:, m, k * P:(k + 1) * P], ident[:])
            t = pe.do(mm)
            t = round_split(dst[0][:, k_to + k, :], dst[1][:, k_to + k, :], ps[:, 0:SEQ], t, free,
                            scale=cols[:, gain + k:gain + k + 1])
        pe.after(a_free.now(), b_free.now())
        return t

    def rms_turned(src, dst, gain, ready, ctx, kd=KD):
        n = kd * P
        h = core.sb(f"normed{core.piece}_{gain}", [P, MT, n], ctx=ctx)
        t = row_rstd([src[:, m, :] for m in range(MT)], n, 0, ready, h[:, 0, :])
        for m in range(MT):
            dve.after(t)
            v = dve.do(nc.vector.tensor_scalar(h[:, m, :], src[:, m, :], small[:, 2 + m:3 + m], None, ALU.mult))
        return turn_and_split(h, dst, kd, gain, v)

    names = [("g_pre_mix", 8), ("g_pre_xa", 8), ("g_mem", 8), ("g_pre_ffn", 8), ("norm_mix_2", 16), ("norm_ffn_2", 16),
             ("mem_norm_2", 8), ("g_ssm_norm", 16), ("conv_w", 96), ("conv_b", 24), ("ffn_conv_w_2", 264),
             ("ffn_conv_b_2", 88), ("mla_qa_norm_2", 2), ("mla_kva_norm_2", 1)]
    col_of, at = {}, 0
    for name, n in names:
        col_of[name] = at
        at += n
    assert at <= 5 * P
    rowed = {}
    for name, n in names:
        v = ins[name]
        letters = "abc"[:len(v.shape)]
        rowed[name] = v.rearrange(f"{' '.join(letters)} -> ({' '.join(letters)})") if len(v.shape) > 1 else v

    head_cols = sb("head_cols", [P, 16])
    HC = {"fox_q_gain_2": 0, "fox_k_gain_2": 1, "mla_q_gain_2": 2, "mla_k_gain_2": 3, "mem_q_gain_2": 4, "mem_k_gain_2": 6}
    bcast = sb("bcast", [P, 4, 32])
    inv_freq = sb("inv_freq", [P, 16])
    pos_i = sb("pos_i", [P, MT], I32)
    scales = sb("scales", [P, 1])

    def load_on(where, dst, src):
        return where.mark(nc.gpsimd.dma_start(dst, src))

    def load(dst, src):
        return load_on(loaded, dst, src)

    with ExitStack() as phase:
        sp.dma_start(res[:, :, :], ins["x"][0].rearrange("(m p) d -> p m d", p=P)).then_inc(stored.sem, 16)
        stored.k += 1
        x_in = stored.now()
        weight_stream()
        stage = core.sb("stage", [P, 5, P], ctx=phase)
        ts = []
        ts.append(pool.do(nc.gpsimd.memset(stage[:], 0.0)))
        ts.append(pool.do(nc.gpsimd.memset(head_cols[:], 1.0)))
        ts.append(pool.do(nc.gpsimd.memset(bcast[:], 0.0)))
        ts.append(pool.do(nc.gpsimd.memset(half_neg[:], -0.5)))
        ts.append(pool.do(nc.gpsimd.memset(ones[:], 1.0)))
        ts.append(pool.do(nc.gpsimd.memset(neg_ones[:], -1.0)))
        t0 = pool.do(nc.gpsimd.memset(causal[:], 0.0))
        for f in range(16):
            pool.do(nc.gpsimd.memset(inv_freq[:, f:f + 1], float(10000.0 ** (-2.0 * f / ROPE))))
        pool.after(t0, pool.done.now())
        for name, n in names:
            done = 0
            while done < n:
                r, tile = (col_of[name] + done) % P, (col_of[name] + done) // P
                k = min(n - done, P - r)
                load_on(rows_loaded, stage[r:r + k, tile, :], rowed[name][done * P:(done + k) * P].rearrange("(r c) -> r c", c=P))
                done += k
        rows_in = rows_loaded.now()
        for name, c in HC.items():
            for l in range(ins[name].shape[0]):
                load(head_cols[0:ins[name].shape[1], c + l:c + l + 1], ins[name][l].rearrange("(d a) -> d a", a=1))
        for j, name in enumerate(("dt_bias", "a_log", "d_skip", "fox_b_f_2")):
            n = ins[name].shape[1]
            load(bcast[:, j, 0:n], ins[name][0].partition_broadcast(P))
        for m in range(MT):
            load(pos_i[:, m:m + 1], ins["positions_2"][0, m * P:(m + 1) * P].rearrange("(d a) -> d a", a=1))
        all_in = loaded.now()

        def sel(dst, src, pattern, mult, op, fill, base=0):
            return pool.do(nc.gpsimd.affine_select(out=dst, in_=src, compare_op=op, fill=fill, base=base,
                                                   pattern=pattern, channel_multiplier=mult))
        sel(upto[:], ones[:], [[1, P]], -1, ALU.is_ge, 0.0)
        sel(beyond[:], ones[:], [[-1, P]], 1, ALU.is_gt, 0.0)
        sel(strict[:], ones[:], [[1, P]], -1, ALU.is_gt, 0.0)
        sel(neg_from[:], neg_ones[:], [[-1, P]], 1, ALU.is_ge, 0.0)
        sel(causal[:], causal[:], [[-1, P]], 1, ALU.is_ge, NEG)
        sel(ident[:], ones[:], [[-1, P]], 1, ALU.is_equal, 0.0)
        consts = pool.done.now()
        split_ahead(2)
        pe.after(rows_in, consts)
        for j in range(5):
            mm = nc.tensor.transpose(psum_c[:, j * P:(j + 1) * P], stage[:, j, :], ident[:])
        t = pe.do(mm)
        dve.after(t)
        v = dve.do(nc.vector.tensor_copy(cols[:, :], psum_c[:, 0:5 * P]))
        for lane in (act, pe, pool):
            lane.after(v, all_in, consts)
        dve.after(all_in, consts, v)
        for c, l, dim in ((HC["fox_q_gain_2"], 1, HD), (HC["mla_q_gain_2"], 1, QK), (HC["mem_q_gain_2"], 2, HD)):
            v = dve.do(nc.vector.tensor_scalar(head_cols[0:dim, c:c + l], head_cols[0:dim, c:c + l], float(dim) ** -0.5, None, ALU.mult))
        act.after(v)
        rms_turned(res, X, col_of["g_pre_mix"], [x_in], phase)
        core.fence()

    def copy_out(dst, scale=1.0):
        def evacuate(ps, free, ready):
            act.after(ready)
            dve.after(ready)
            a = act.do(nc.scalar.activation(dst(0), ps[:, 0:512].rearrange("p (c t) -> p c t", c=dst(0).shape[1]), ACT.Copy, scale=scale), free)
            dve.do(nc.vector.tensor_scalar(dst(1), ps[:, 512:1024].rearrange("p (c t) -> p c t", c=dst(1).shape[1]), scale, None, ALU.mult), free)
        return evacuate

    mix = ExitStack()
    merged = core.sb("merged", [P, KD, SEQ], ctx=mix)
    with ExitStack() as phase:
        q_t = core.sb("q_t", [P, KD, SEQ], ctx=phase)
        k_t = core.sb("k_t", [P, KD, SEQ], ctx=phase)
        v_n = core.sb("v_n", [P, MT, D], ctx=phase)
        for dst, scale in ((q_t, SB_DIM ** -0.5), (k_t, 1.0)):
            for c in range(2):
                run_product(product_turned, X, copy_out(lambda j: dst[:, 4 * c + 2 * j:4 * c + 2 * j + 2, :], scale))
        for c in range(2):
            run_product(product_natural, X, copy_out(lambda j: v_n[:, j:j + 1, 512 * c:512 * c + 512]))
        stick_attention(core, locals())
        core.fence()

    def gate(dst, c):
        def evacuate(ps, free, ready):
            act.after(ready)
            for j in range(2):
                act.do(nc.scalar.activation(dst[:, 4 * c + 2 * j:4 * c + 2 * j + 2, :],
                                            ps[:, 512 * j:512 * j + 512].rearrange("p (c t) -> p c t", c=2), ACT.Sigmoid), free)
        return evacuate

    for c in range(2):
        run_product(product_turned, X, gate(merged, c))
    for c in range(2):
        def evacuate(ps, free, ready, c=c):
            dve.after(ready, a_free.now(), b_free.now())
            for j in range(2):
                m = merged[:, 4 * c + 2 * j:4 * c + 2 * j + 2, :]
                dve.do(nc.vector.tensor_tensor(m, ps[:, 512 * j:512 * j + 512].rearrange("p (c t) -> p c t", c=2), m, ALU.mult), free)
        run_product(product_turned, Y, evacuate)
    core.fence(act, dve, pool)

    mamba(core, locals())

    with ExitStack() as phase:
        gate_s = core.sb("gate_s", [P, KD, SEQ], ctx=phase)
        for c in range(2):
            run_product(product_turned, X, gate(gate_s, c))
        for c in range(2):
            ps, free = next_bank()
            for h in range(2):
                product_turned(ps, Y, k0=KD * h, first=h == 0, last=h == 1)
                split_ahead()
            dve.after(used.now(), a_free.now(), b_free.now())
            for j in range(2):
                g = gate_s[:, 4 * c + 2 * j:4 * c + 2 * j + 2, :]
                m = merged[:, 4 * c + 2 * j:4 * c + 2 * j + 2, :]
                t = dve.do(nc.vector.tensor_tensor(g, ps[:, 512 * j:512 * j + 512].rearrange("p (c t) -> p c t", c=2), g, ALU.mult), free)
                dve.after(t)
                t = dve.do(nc.vector.tensor_tensor(g, g, m, ALU.add))
                round_split(x_hi[:, 4 * c + 2 * j:4 * c + 2 * j + 2, :], x_lo[:, 4 * c + 2 * j:4 * c + 2 * j + 2, :], g, t)
        core.fence()
    mix.close()

    def post_norm(gain_name, act_in):
        with ExitStack() as phase:
            o = core.sb("post_" + gain_name, [P, MT, D], ctx=phase)
            g = core.sb("gain_" + gain_name, [P, D], ctx=phase)
            core.fence(pool)
            t = load(g[:, :], ins[gain_name][0].partition_broadcast(P))
            pe.after(dve.done.now(), act.done.now())
            for c in range(2):
                run_product(product_natural, act_in, copy_out(lambda j: o[:, j:j + 1, 512 * c:512 * c + 512]))
            finish_post(o, g, t, phase, gain_name)
            core.fence()

    def finish_post(o, g, gain_in, phase, tag):
        junk = core.sb("junk_" + tag, [P, D], ctx=phase)
        t = row_rstd([o[:, m, :] for m in range(MT)], D, 0, [a_free.now(), b_free.now(), dve.done.now(), act.done.now()], junk)
        for m in range(MT):
            dve.after(t, gain_in)
            v = dve.do(nc.vector.scalar_tensor_tensor(out=o[:, m, :], in0=o[:, m, :], scalar=small[:, 2 + m:3 + m],
                                                      in1=g[:, :], op0=ALU.mult, op1=ALU.mult))
            dve.after(v)
            dve.do(nc.vector.tensor_tensor(res[:, m, :], res[:, m, :], o[:, m, :], ALU.add))

    post_norm("g_post_mix", X)

    with ExitStack() as phase:
        kx = core.sb("kx", [P, KD, SEQ], ctx=phase)
        vx = core.sb("vx", [P, MT, D], ctx=phase)
        with ExitStack() as inner:
            mem = core.sb("mem", [P, MT, D], ctx=inner)
            t = load(mem[:, :, :], ins["mem"][0].rearrange("(m p) d -> p m d", p=P))
            rms_turned(mem, Y, col_of["g_mem"], [t], inner)
            core.fence()
        for c in range(2):
            run_product(product_turned, Y, copy_out(lambda j: kx[:, 4 * c + 2 * j:4 * c + 2 * j + 2, :]))
        for c in range(2):
            run_product(product_natural, Y, copy_out(lambda j: vx[:, j:j + 1, 512 * c:512 * c + 512]))
        with ExitStack() as inner:
            rms_turned(res, X, col_of["g_pre_xa"], [dve.done.now()], inner)
            core.fence()
        qx = core.sb("qx", [P, KD, SEQ], ctx=phase)
        for c in range(2):
            run_product(product_turned, X, copy_out(lambda j: qx[:, 4 * c + 2 * j:4 * c + 2 * j + 2, :], XA_DIM ** -0.5))
        cross_attention(core, locals())
        core.fence()
    post_norm("g_post_xa", X)

    with ExitStack() as phase:
        with ExitStack() as inner:
            rms_turned(res, X, col_of["g_pre_ffn"], [dve.done.now()], inner)
            core.fence()
        ffn(core, locals(), None)
        o = core.sb("ffn_out", [P, MT, D], ctx=phase)
        g = core.sb("gain_ffn", [P, D], ctx=phase)
        t = load(g[:, :], ins["g_post_ffn"][0].partition_broadcast(P))
        act.do(nc.scalar.activation(o[:, 0, :], psum_c[:, 0:1024], ACT.Copy))
        dve.do(nc.vector.tensor_copy(o[:, 1, :], psum_c[:, 1024:2048]))
        finish_post(o, g, t, phase, "g_post_ffn")
        core.fence()

    L2 = ExitStack()
    mk_n = core.sb("mk_n", [P, MT, MEM_W], ctx=L2)
    mv_n = core.sb("mv_n", [P, MT, MEM_W], ctx=L2)
    with ExitStack() as phase:
        mem = core.sb("mem2", [P, MT, D], ctx=phase)
        t = load(mem[:, :, :], ins["mem_2"][0].rearrange("(m p) d -> p m d", p=P))
        rms_turned(mem, Y, col_of["mem_norm_2"], [t], phase)
        kv = core.sb("mem_kv", [P, MT, 2 * MEM_W], ctx=phase)
        run_product(product_natural, Y, copy_out(lambda j: kv[:, j:j + 1, :]))
        m_rstd = core.sb("mem_rstd", [P, MT, MEM_HEADS], ctx=phase)
        core.fence(dve)

        def keys(m):
            return split_heads(kv[:, m, 0:MEM_W], HD)
        t = head_rstd(core, dict(psum_c=psum_c, half_neg=half_neg), keys, MEM_HEADS, (HD, HD), m_rstd)
        scale_heads(core, lambda m: split_heads(mk_n[:, m, :], HD), keys, MEM_HEADS, m_rstd, t)
        dve.do(nc.vector.tensor_copy(mv_n[:, :, :], kv[:, :, MEM_W:2 * MEM_W]))
        core.fence()

    for layer in range(2):
        with ExitStack() as phase:
            with ExitStack() as inner:
                rms_turned(res, X, col_of["norm_mix_2"] + KD * layer, [dve.done.now()], inner)
                core.fence()
            (fox if layer == 0 else mla)(core, locals())
            core.fence()
        for c in range(2):
            def evacuate(ps, free, ready, c=c):
                dve.after(ready)
                for m in range(MT):
                    r = res[:, m, 512 * c:512 * c + 512]
                    dve.do(nc.vector.tensor_tensor(r, ps[:, 512 * m:512 * m + 512], r, ALU.add), free)
            run_product(product_natural, Y, evacuate)
        core.fence()
        with ExitStack() as phase:
            with ExitStack() as inner:
                rms_turned(res, X, col_of["norm_ffn_2"] + KD * layer, [a_free.now(), b_free.now()], inner)
                core.fence()
            ffn(core, locals(), layer)
            for m in range(MT):
                dve.do(nc.vector.tensor_tensor(res[:, m, :], psum_c[:, 1024 * m:1024 * m + 1024], res[:, m, :], ALU.add))
            core.fence()
    L2.close()

    act.after(dve.done.now())
    stored.mark(nc.scalar.dma_start(out[0].rearrange("(m p) d -> p m d", p=P), res[:, :, :]))
    act.after(stored.now())


def ctx_psum(core, name, shape):
    return core.ctx.enter_context(core.nc.psum_tensor(name, shape, F32))


def stick_attention(core, env):
    nc, pe, act, dve, pool = core.nc, core.pe, core.act, core.dve, core.pool
    q_t, k_t, v_n, phase = env["q_t"], env["k_t"], env["v_n"], env["phase"]
    psum_a, psum_b, psum_c = env["psum_a"], env["psum_b"], env["psum_c"]
    y_hi, y_lo = env["Y"]
    W = 384
    kb = core.sb("stick_k", [P, 2, SEQ], ctx=phase)
    vb = core.sb("stick_v", [P, 2, MT, P], ctx=phase)
    e = core.sb("stick_e", [P, 2, W], ctx=phase)
    L = core.sb("stick_l", [P, 2, W], ctx=phase)
    w = core.sb("stick_w", [P, 2, W], ctx=phase)
    core.fence()

    def diagonal(x):
        return x.rearrange("p (b t) -> p b t", t=P)[:, 0:3:2, :]

    strict = env["strict"][:].unsqueeze(1).to_broadcast([P, 2, P])
    staged = Count(core, "stick_staged")
    v_free = Count(core, "stick_v_free")
    o_free = [Count(core, f"stick_o_free{b}") for b in range(2)]
    nc.scalar.preload_act_table_set("natural_log_exp_and_others")
    with env["loop"]("stick", SB_HEADS // 2) as i:
        pool.after(v_free.now())
        pool.do(nc.gpsimd.tensor_copy(kb[:, 0, :], k_t[:, bass.ds(i, 1), :].rearrange("p a t -> p (a t)")), staged)
        for m in range(MT):
            pool.do(nc.gpsimd.tensor_copy(vb[:, 0, m, :], v_n[:, m, bass.ds(i * P, P)]), staged)
        pool.do(nc.gpsimd.tensor_copy(kb[:, 1, :], q_t[:, bass.ds(i, 1), :].rearrange("p a t -> p (a t)")), staged)
        ready = staged.now()
        z, tz = [psum_a[:, 0:W], psum_a[:, 512:512 + W]], []
        for b in range(2):
            r = slice(64 * b, 64 * b + 64)
            pe.after(ready, act.done.now())
            nc.tensor.matmul(z[b][:, 0:SEQ], kb[r, 0, 0:P], kb[r, 1, :], start=True, stop=False, skip_group_check=True)
            tz.append(pe.do(nc.tensor.matmul(z[b][:, SEQ:W], kb[r, 0, P:SEQ], kb[r, 1, P:SEQ], start=False, stop=False,
                                             skip_group_check=True)))
        tl = []
        for b in range(2):
            dve.after(tz[b], act.done.now())
            t = dve.do(nc.vector.tensor_scalar(e[:, b, :], z[b], 30.0, None, ALU.min))
            act.after(t)
            t = act.do(nc.scalar.activation(e[:, b, :], e[:, b, :], ACT.Exp))
            act.after(t)
            t = act.do(nc.scalar.activation(e[:, b, :], e[:, b, :], ACT.Ln, bias=1.0))
            dve.after(t, v_free.now())
            t = dve.do(nc.vector.tensor_tensor(L[:, b, :], z[b], e[:, b, :], ALU.max))
            dve.after(t)
            tl.append(dve.do(nc.vector.tensor_tensor(diagonal(L[:, b, :]), diagonal(L[:, b, :]), strict, ALU.mult)))
        tw = []
        for b in range(2):
            pe.after(tl[b])
            nc.tensor.matmul(z[b][:, 0:SEQ], env["neg_from"][:], L[:, b, 0:SEQ], start=False, stop=False, skip_group_check=True)
            nc.tensor.matmul(z[b][:, P:SEQ], env["neg_ones"][:], L[:, b, SEQ:W], start=False, stop=False, skip_group_check=True)
            t = pe.do(nc.tensor.matmul(z[b][:, SEQ:W], env["neg_from"][:], L[:, b, SEQ:W], start=False, stop=True,
                                       skip_group_check=True))
            act.after(t, v_free.now())
            t = act.do(nc.scalar.activation(w[:, b, :], z[b], ACT.Exp))
            dve.after(t)
            tw.append(dve.do(nc.vector.scalar_tensor_tensor(out=diagonal(w[:, b, :]), in0=diagonal(w[:, b, :]), scalar=3.0e38,
                                                            in1=strict, op0=ALU.min, op1=ALU.mult)))
        for b in range(2):
            o = psum_b[:, 512 * b:512 * b + SEQ]
            r = slice(64 * b, 64 * b + 64)
            pe.after(tw[b], o_free[b].now())
            nc.tensor.matmul(o, vb[:, 0, 0, :], w[:, b, 0:SEQ], start=True, stop=False, skip_group_check=True)
            t = pe.do(nc.tensor.matmul(o[:, P:SEQ], vb[:, 0, 1, :], w[:, b, SEQ:W], start=False, stop=True,
                                       skip_group_check=True), v_free)
            act.after(t)
            dst = [y[r, bass.ds(i, 1), :].rearrange("p a t -> p (a t)") for y in (y_hi, y_lo)]
            a = act.do(nc.scalar.activation(dst[0], o[r, :], ACT.Copy))
            dve.after(a)
            dve.do(nc.vector.tensor_tensor(dst[1], o[r, :], dst[0].bitcast(F32), ALU.subtract), o_free[b])


def mamba(core, env):
    nc, pe, act, dve, pool = core.nc, core.pe, core.act, core.dve, core.pool
    psum_a, psum_b, psum_c = env["psum_a"], env["psum_b"], env["psum_c"]
    cols, small, bcast, upto, beyond, ident = (env[n] for n in ("cols", "small", "bcast", "upto", "beyond", "ident"))
    a_free, b_free, used, free_c = env["a_free"], env["b_free"], env["used"], Count(core, "c_free")
    X, col_of, run_product, loop = env["X"], env["col_of"], env["run_product"], env["loop"]
    GH, GW = GROUP_HEADS, SSM_INNER // SSM_GROUPS
    with ExitStack() as phase:
        b_t = core.sb("b_t", [P, SSM_GROUPS, SEQ], ctx=phase)
        c_t = core.sb("c_t", [P, SSM_GROUPS, SEQ], ctx=phase)
        y_n = core.sb("y_n", [P, MT, SSM_INNER], ctx=phase)
        dts = core.sb("dts", [P, 5, MT, SSM_HEADS], ctx=phase)
        dt, adt, tmp, eac = (dts[:, j, :, :] for j in range(4))
        to_end = dts[:, 4, 0, :]

        with ExitStack() as inner:
            conv = core.sb("conv", [P, 2, 4, SEQ], ctx=inner)
            nc.scalar.preload_act_table_set("silu_and_others")

            def convolve(u, tile, dst):
                def col(name, tap, j):
                    at = tile + (col_of[name] + tap * (XBC // P) + j)
                    return cols[:, bass.ds(at, 1)]

                def evacuate(ps, free, ready):
                    act.after(ready, pe.done.now(), act.done.now())
                    for j in range(4):
                        t = act.do(nc.scalar.activation(conv[:, u, j, :], ps[:, j * SEQ:(j + 1) * SEQ], ACT.Identity,
                                                        scale=col("conv_w", 3, j), bias=col("conv_b", 0, j)))
                    dve.after(t)
                    for d in (1, 2, 3):
                        for j in range(4):
                            t = dve.do(nc.vector.scalar_tensor_tensor(
                                out=conv[:, u, j, d:], in0=ps[:, j * SEQ:(j + 1) * SEQ - d], scalar=col("conv_w", 3 - d, j),
                                in1=conv[:, u, j, d:], op0=ALU.mult, op1=ALU.add), free if (d, j) == (3, 3) else None)
                        dve.after(t)
                    act.after(t)
                    act.do(nc.scalar.activation(dst, conv[:, u, :, :], ACT.Silu))
                return evacuate

            def turn_back(u, ready, at):
                pe.after(ready, free_c.now())
                for j in range(4):
                    for m in range(MT):
                        mm = nc.tensor.transpose(psum_c[:, 1024 * u + 512 * m + j * P:1024 * u + 512 * m + (j + 1) * P],
                                                 conv[:, u, j, m * P:(m + 1) * P], ident[:])
                t = pe.do(mm)
                dve.after(t)
                act.after(t)
                act.do(nc.scalar.activation(y_n[:, 0, bass.ds(at, GW)], psum_c[:, 1024 * u:1024 * u + 512], ACT.Copy), free_c)
                dve.do(nc.vector.tensor_copy(y_n[:, 1, bass.ds(at, GW)], psum_c[:, 1024 * u + 512:1024 * u + 1024]), free_c)

            with loop("xbc", 2) as i:
                run_product(env["product_turned"], X, convolve(0, i * 8, conv[:, 0, :, :]))
                first = act.done.now()
                run_product(env["product_turned"], X, convolve(1, i * 8 + 4, conv[:, 1, :, :]))
                turn_back(0, first, i * 1024)
                turn_back(1, act.done.now(), i * 1024 + 512)
            act.after(free_c.now())
            dve.after(free_c.now())
            for u, dst in ((0, b_t), (1, c_t)):
                run_product(env["product_turned"], X, convolve(u, 16 + 4 * u, dst[:, :, :]))
            core.fence()

        def evacuate(ps, free, ready):
            nc.scalar.preload_act_table_set("natural_log_exp_and_others")
            act.do(nc.scalar.activation(bcast[:, 1, :], bcast[:, 1, :], ACT.Exp))
            dve.after(ready)
            for m in range(MT):
                t = dve.do(nc.vector.tensor_tensor(dt[:, m, :], ps[:, 512 * m:512 * m + SSM_HEADS], bcast[:, 0, :], ALU.add), free)
            dve.after(t)
            t = dve.do(nc.vector.tensor_scalar(tmp, dt, 30.0, None, ALU.min))
            act.after(t, act.done.now())
            t = act.do(nc.scalar.activation(tmp, tmp, ACT.Exp))
            act.after(t)
            t = act.do(nc.scalar.activation(tmp, tmp, ACT.Ln, bias=1.0))
            dve.after(t)
            t = dve.do(nc.vector.tensor_tensor(dt, dt, tmp, ALU.max))
            dve.after(t)
            for m in range(MT):
                dve.do(nc.vector.scalar_tensor_tensor(out=adt[:, m, :], in0=dt[:, m, :], scalar=-1.0, in1=bcast[:, 1, :],
                                                      op0=ALU.mult, op1=ALU.mult))
        run_product(env["product_natural"], X, evacuate, n=SSM_HEADS)
        pe.after(dve.done.now())
        for c in range(MT):
            nc.tensor.matmul(psum_c[:, 32 * c:32 * c + 32], upto[:], adt[:, c, :], start=c == 0, stop=True, skip_group_check=True)
        t = pe.do(nc.tensor.matmul(psum_c[:, 64:96], beyond[:], adt[:, 0, :], start=False, stop=True, skip_group_check=True))
        act.after(t)
        act.do(nc.scalar.activation(eac, psum_c[:, 0:64].rearrange("p (c h) -> p c h", c=MT), ACT.Exp))
        act.do(nc.scalar.activation(to_end, psum_c[:, 64:96], ACT.Exp))

        with ExitStack() as inner:
            bg = core.sb("bg", [P, SEQ], ctx=inner)
            cg = core.sb("cg", [P, SEQ], ctx=inner)
            b_n = core.sb("b_n", [P, P], ctx=inner)
            cb = core.sb("cb", [P, MT, P], ctx=inner)
            xc = core.sb("xc", [P, MT, GH, SSM_HD], ctx=inner)
            xd = core.sb("xd", [P, GH, SSM_HD], ctx=inner)
            state = xd[:, :, :].rearrange("p h d -> p (h d)")
            rows = core.sb("rows", [P, 2, 4, P], ctx=inner)
            staged = Count(core, "ssd_staged")
            state_free = Count(core, "ssd_state_free")
            core.fence()
            with loop("ssd", SSM_GROUPS) as g:
                def heads(x, c, h0=0, n=GH):
                    return x[:, c, bass.ds(g * GH + h0, n)].unsqueeze(2)

                pool.after(pe.done.now(), state_free.now())
                pool.do(nc.gpsimd.tensor_copy(bg[:], b_t[:, bass.ds(g, 1), :].rearrange("p a t -> p (a t)")), staged)
                pool.do(nc.gpsimd.tensor_copy(cg[:], c_t[:, bass.ds(g, 1), :].rearrange("p a t -> p (a t)")), staged)
                bc_in = staged.now()
                pe.after(bc_in, act.done.now(), dve.done.now())
                for c in range(MT):
                    nc.tensor.matmul(psum_a[:, P * c:P * c + P], bg[:, P * c:P * c + P], cg[:, P * c:P * c + P],
                                     start=c == 0, stop=True, skip_group_check=True)
                t_cb = pe.do(nc.tensor.transpose(psum_c[:, 1024:1024 + P], bg[:, 0:P], ident[:]))
                act.after(t_cb)
                t_bn = act.do(nc.scalar.activation(b_n[:], psum_c[:, 1024:1024 + P], ACT.Copy))
                dve.after(t_cb, pe.done.now())
                t_cb = dve.do(nc.vector.tensor_tensor(cb[:, :, :], psum_a[:, 0:2 * P].rearrange("p (c t) -> p c t", c=MT),
                                                      upto[:].unsqueeze(1).to_broadcast([P, MT, P]), ALU.mult))
                for c in range(MT):
                    x_c = y_n[:, c, bass.ds(g * GW, GW)].rearrange("p (h d) -> p h d", d=SSM_HD)
                    t_xc = dve.do(nc.vector.tensor_tensor(xc[:, c, :, :], x_c, heads(dt, c).to_broadcast([P, GH, SSM_HD]), ALU.mult))
                    if c == 0:
                        dve.after(t_xc, state_free.now())
                        t_xd = dve.do(nc.vector.tensor_tensor(xd[:, :, :], xc[:, 0, :, :], to_end[:, bass.ds(g * GH, GH)].unsqueeze(2)
                                                              .to_broadcast([P, GH, SSM_HD]), ALU.mult))
                pe.after(t_bn, t_xd)
                t = pe.do(nc.tensor.matmul(psum_b[:, 0:GW], b_n[:], state, start=True, stop=True))
                act.after(t)
                t = act.do(nc.scalar.activation(state, psum_b[:, 0:GW], ACT.Copy))
                pe.after(t)
                pe.do(nc.tensor.matmul(psum_b[:, 512:512 + GW], cg[:, P:SEQ], state, start=True, stop=True), state_free)
                last_y = [pe.done.now(), pe.done.now()]
                for qd in range(4):
                    c, h0, u = qd // 2, 4 * (qd % 2), qd % 2
                    pool.after(last_y[u])
                    t = pool.do(nc.gpsimd.tensor_tensor(rows[:, u, :, :], upto[:].unsqueeze(1).to_broadcast([P, 4, P]),
                                                        heads(adt, c, h0, 4).to_broadcast([P, 4, P]), ALU.mult))
                    seg = (psum_a[:, 512:1024], psum_a[:, 0:512])[u]
                    pe.after(t, t_cb, act.done.now())
                    t = pe.do(nc.tensor.matmul(seg, beyond[:], rows[:, u, :, :].rearrange("p h t -> p (h t)"), start=True, stop=True))
                    act.after(t)
                    t = act.do(nc.scalar.activation(rows[:, u, :, :], seg.rearrange("p (h t) -> p h t", h=4), ACT.Exp))
                    dve.after(t, t_cb)
                    t = dve.do(nc.vector.tensor_tensor(rows[:, u, :, :], rows[:, u, :, :],
                                                       cb[:, c, :].unsqueeze(1).to_broadcast([P, 4, P]), ALU.mult))
                    pe.after(t, t_xc)
                    for h in range(4):
                        at = 512 * c + (h0 + h) * SSM_HD
                        mm = nc.tensor.matmul(psum_c[:, at:at + SSM_HD], rows[:, u, h, :], xc[:, c, h0 + h, :],
                                              start=h0 == 0 and h == 0, stop=True, skip_group_check=True)
                    t_y = last_y[u] = pe.do(mm)
                for c in range(MT):
                    x_c = y_n[:, c, bass.ds(g * GW, GW)].rearrange("p (h d) -> p h d", d=SSM_HD)
                    skip = bcast[:, 2, bass.ds(g * GH, GH)].unsqueeze(2).to_broadcast([P, GH, SSM_HD])
                    own = psum_c[:, 512 * c:512 * c + 512].rearrange("p (h d) -> p h d", d=SSM_HD)
                    dve.after(t_y, t_xc)
                    t = dve.do(nc.vector.tensor_tensor(x_c, x_c, skip, ALU.mult))
                    dve.after(t)
                    t = dve.do(nc.vector.tensor_tensor(x_c, own, x_c, ALU.add))
                    if c == 1:
                        dve.after(t, state_free.now())
                        t = dve.do(nc.vector.tensor_tensor(xc[:, 1, :, :], psum_b[:, 512:1024].rearrange("p (h d) -> p h d", d=SSM_HD),
                                                           heads(eac, 1).to_broadcast([P, GH, SSM_HD]), ALU.mult))
                        dve.after(t)
                        dve.do(nc.vector.tensor_tensor(x_c, x_c, xc[:, 1, :, :], ALU.add))
            core.fence()

        with ExitStack() as inner:
            gated = core.sb("gated", [P, 2, MT, GW], ctx=inner)
            junk = core.sb("junk_z", [P, GW], ctx=inner)
            turned_y = [Count(core, f"turned_y{u}") for u in range(2)]
            nc.scalar.preload_act_table_set("silu_and_others")

            def gate_norm(u, g):
                def evacuate(ps, free, ready):
                    act.after(ready, turned_y[u].now())
                    t = act.do(nc.scalar.activation(gated[:, u, :, :], ps[:, :].rearrange("p (m n) -> p m n", m=MT), ACT.Silu), free)
                    dve.after(t)
                    t = dve.do(nc.vector.tensor_tensor(gated[:, u, :, :], gated[:, u, :, :], y_n[:, :, bass.ds(g * GW, GW)], ALU.mult))
                    t = env["row_rstd"]([gated[:, u, m, :] for m in range(MT)], GW, 8 * u, [t], junk)
                    for m in range(MT):
                        dve.after(t)
                        dve.do(nc.vector.tensor_scalar(gated[:, u, m, :], gated[:, u, m, :], small[:, 8 * u + 2 + m:8 * u + 3 + m],
                                                       None, ALU.mult))
                return evacuate

            def turn(u, g, ready):
                pe.after(ready, free_c.now())
                for j in range(4):
                    for m in range(MT):
                        mm = nc.tensor.transpose(psum_c[:, 1024 * u + j * SEQ + m * P:1024 * u + j * SEQ + (m + 1) * P],
                                                 gated[:, u, m, j * P:(j + 1) * P], ident[:])
                t = pe.do(mm, turned_y[u])
                for bank in range(2):
                    parts = []
                    for j in (2 * bank, 2 * bank + 1):
                        hi, lo = (y[:, bass.ds(g * 4 + j, 1), :].rearrange("p a t -> p (a t)") for y in env["Y"])
                        parts.append((hi, lo, psum_c[:, 1024 * u + j * SEQ:1024 * u + (j + 1) * SEQ],
                                      cols[:, bass.ds(g * 4 + (j + col_of["g_ssm_norm"]), 1)]))
                    act.after(t)
                    for hi, lo, src, gain in parts:
                        a = act.do(nc.scalar.activation(hi, src, ACT.Copy, scale=gain))
                    dve.after(a)
                    for hi, lo, src, gain in parts:
                        dve.do(nc.vector.scalar_tensor_tensor(out=lo, in0=src, scalar=gain, in1=hi.bitcast(F32),
                                                              op0=ALU.mult, op1=ALU.subtract), free_c)

            with loop("z", 2) as i:
                run_product(env["product_natural"], X, gate_norm(0, i * 2))
                first = dve.done.now()
                run_product(env["product_natural"], X, gate_norm(1, i * 2 + 1))
                turn(0, i * 2, first)
                turn(1, i * 2 + 1, dve.done.now())
            core.fence()


class Softmax:

    def __init__(self, core, env, tag, phase):
        self.core, self.env = core, env
        self.p = core.sb(tag + "_prob", [P, 2, 512], ctx=phase)
        self.pt = core.sb(tag + "_prob_t", [P, 2, 512], ctx=phase)
        self.peak = core.sb(tag + "_peak", [P, 2, MT], ctx=phase)
        self.total = core.sb(tag + "_total", [P, 2, MT], ctx=phase)
        self.o_free = [Count(core, f"{tag}_o_free{b}") for b in range(2)]
        self.tag = tag

    def scores(self, b):
        return self.env["psum_b"][:, 512 * b:512 * b + 512]

    def probabilities(self, scored, causal):
        core, nc = self.core, self.core.nc
        pe, act, dve = core.pe, core.act, core.dve
        w0 = P if causal else SEQ
        parts = [(0, w0), (w0, w0 + SEQ)]
        exped = []
        for b in range(2):
            sc = self.scores(b)
            dve.after(scored[b])
            if causal:
                d = sc[:, 0:384].rearrange("p (b t) -> p b t", t=P)[:, 0:3:2, :]
                t = dve.do(nc.vector.tensor_tensor(d, d, self.env["causal"][:].unsqueeze(1).to_broadcast([P, 2, P]), ALU.add))
                dve.after(t)
            for m, (lo, hi) in enumerate(parts):
                t = dve.do(nc.vector.tensor_reduce(self.peak[:, b, m:m + 1], sc[:, lo:hi], AX, ALU.max))
            dve.after(t)
            t = dve.do(nc.vector.tensor_scalar(self.peak[:, b, :], self.peak[:, b, :], -1.0, None, ALU.mult))
            act.after(t)
            for m, (lo, hi) in enumerate(parts):
                t = act.do(nc.scalar.activation(self.p[:, b, lo:hi], sc[:, lo:hi], ACT.Exp, bias=self.peak[:, b, m:m + 1],
                                                accum_out=self.total[:, b, m:m + 1]))
            exped.append(t)
        normed = []
        for b in range(2):
            dve.after(exped[b])
            t = dve.do(nc.vector.reciprocal(self.total[:, b, :], self.total[:, b, :]))
            dve.after(t)
            for m, (lo, hi) in enumerate(parts):
                t = dve.do(nc.vector.tensor_scalar(self.p[:, b, lo:hi], self.p[:, b, lo:hi], self.total[:, b, m:m + 1], None, ALU.mult))
            normed.append(t)
        out = []
        order = [0, P, SEQ] if causal else [0, SEQ, P, SEQ + P]
        for b in range(2):
            pe.after(normed[b])
            psum = self.env["psum_c"][:, 512 * b:512 * b + 512]
            for j, at in enumerate(order):
                mm = nc.tensor.transpose(psum[:, j * P:(j + 1) * P], self.p[:, b, at:at + P], self.env["ident"][:])
            t = pe.do(mm)
            act.after(t)
            n = len(order) * P
            out.append(act.do(nc.scalar.activation(self.pt[:, b, 0:n], psum[:, 0:n], ACT.Copy)))
        return out

    def weigh(self, b, at, values, turned, causal):
        nc, pe = self.core.nc, self.core.pe
        o = self.env["psum_c"][:, 1024 + 512 * b + at:1024 + 512 * b + at + SEQ]
        pe.after(turned, self.o_free[b].now())
        nc.tensor.matmul(o, values[0], self.pt[:, b, 0:SEQ], start=at == 0, stop=False, skip_group_check=True)
        if causal:
            mm = nc.tensor.matmul(o[:, P:SEQ], values[1], self.pt[:, b, SEQ:384], start=False, stop=True, skip_group_check=True)
        else:
            mm = nc.tensor.matmul(o, values[1], self.pt[:, b, SEQ:512], start=False, stop=True, skip_group_check=True)
        return o, mm


def cross_attention(core, env):
    nc, pe, act, dve = core.nc, core.pe, core.act, core.dve
    qx, kx, vx = env["qx"], env["kx"], env["vx"]
    x_hi, x_lo = env["X"]
    soft = Softmax(core, env, "xa", env["phase"])
    core.fence()
    nc.scalar.preload_act_table_set("natural_log_exp_and_others")
    for pair in range(XA_HEADS // 2):
        scored = []
        for b in range(2):
            tiles = range(2 * (2 * pair + b), 2 * (2 * pair + b) + 2)
            pe.after(act.done.now())
            for m in range(MT):
                for kt in tiles:
                    mm = nc.tensor.matmul(soft.scores(b)[:, SEQ * m:SEQ * m + SEQ], qx[:, kt, m * P:(m + 1) * P], kx[:, kt, :],
                                          start=m == 0 and kt == tiles[0], stop=kt == tiles[1], skip_group_check=True)
            scored.append(pe.do(mm))
        turned = soft.probabilities(scored, False)
        for b in range(2):
            for j in range(2):
                kt = 2 * (2 * pair + b) + j
                o, mm = soft.weigh(b, SEQ * j, [vx[:, m, kt * P:(kt + 1) * P] for m in range(MT)], turned[b], False)
            t = pe.do(mm)
            kt = 2 * (2 * pair + b)
            src = env["psum_c"][:, 1024 + 512 * b:1536 + 512 * b].rearrange("p (j t) -> p j t", j=2)
            env["round_split"](x_hi[:, kt:kt + 2, :], x_lo[:, kt:kt + 2, :], src, t, soft.o_free[b])


def ffn(core, env, layer):
    nc, pe, act, dve, pool = core.nc, core.pe, core.act, core.dve, core.pool
    psum_a, psum_b, psum_c, cols, col_of = (env[n] for n in ("psum_a", "psum_b", "psum_c", "cols", "col_of"))
    used, X = env["used"], env["X"]
    phase = env["phase"]
    tag = f"ffn{'' if layer is None else layer + 1}"
    hid = [core.sb(f"{tag}_hidden_{part}", [P, 2, SEQ], F32R, ctx=phase) for part in ("hi", "lo")]
    pre = core.sb(tag + "_pre", [P, 2, 2, SEQ], ctx=phase)
    h32 = core.sb(tag + "_h32", [P, 2, SEQ], ctx=phase)
    zero = core.sb(tag + "_zero", [P, P], F32R, ctx=phase)
    ready = [Count(core, f"{tag}_ready{u}") for u in range(2)]
    free = [Count(core, f"{tag}_free{u}") for u in range(2)]
    core.fence()
    nc.scalar.preload_act_table_set("silu_and_others")
    t = act.do(nc.scalar.activation(zero[:], env["ones"][:], ACT.Copy, scale=0.0))
    pe.after(t)
    for bank in range(4):
        mm = nc.tensor.matmul(psum_c[:, 512 * bank:512 * bank + 512], zero[:], X[0][:, 0:2, :].rearrange("p k t -> p (k t)"),
                              start=True, stop=False, skip_group_check=True)
    pe.do(mm)

    def gate_up(u):
        ps = (psum_a, psum_b)[u][:, 0:512]
        s = env["take_piece"]()
        w = env["weights"](s, KD, SEQ)
        pe.after(free[u].now())
        for k in range(KD):
            for j in range(2):
                mm = env["three"](ps[:, j * SEQ:(j + 1) * SEQ], [x[:, k, j * P:(j + 1) * P] for x in w],
                                  [x[:, k, :] for x in X], k == 0 and j == 0, k == KD - 1)
        pe.do(mm, used)

    def down(u):
        s = env["take_piece"]()
        w = [x[:, 0, :] for x in env["weights"](s, 1, D)]
        pe.after(ready[u].now())
        for m in range(MT):
            for n in range(2):
                mm = env["three"](psum_c[:, D * m + 512 * n:D * m + 512 * n + 512], [x[:, u, m * P:(m + 1) * P] for x in hid],
                                  [x[:, 512 * n:512 * n + 512] for x in w], False, True)
        pe.do(mm, used)

    def hidden(u, h, made):
        ps = (psum_a, psum_b)[u]

        def col(name, tap, j):
            at = col_of[name] + (layer * 6 + tap * 2 + j if name == "ffn_conv_w_2" else layer * 2 + j) * FT + h
            return cols[:, bass.ds(at, 1)]

        act.after(made, ready[u].now())
        if layer is None:
            t = act.do(nc.scalar.activation(pre[:, u, 0, :], ps[:, 0:SEQ], ACT.Silu))
            dve.after(t)
            t = dve.do(nc.vector.tensor_tensor(h32[:, u, :], ps[:, SEQ:2 * SEQ], pre[:, u, 0, :], ALU.mult), free[u])
        else:
            for j in range(2):
                t = act.do(nc.scalar.activation(pre[:, u, j, :], ps[:, j * SEQ:(j + 1) * SEQ], ACT.Identity,
                                                scale=col("ffn_conv_w_2", 2, j), bias=col("ffn_conv_b_2", 0, j)))
            for d in (1, 2):
                dve.after(t)
                for j in range(2):
                    t = dve.do(nc.vector.scalar_tensor_tensor(
                        out=pre[:, u, j, d:], in0=ps[:, j * SEQ:(j + 1) * SEQ - d], scalar=col("ffn_conv_w_2", 2 - d, j),
                        in1=pre[:, u, j, d:], op0=ALU.mult, op1=ALU.add), free[u] if (d, j) == (2, 1) else None)
            act.after(t)
            t = act.do(nc.scalar.activation(pre[:, u, 0, :], pre[:, u, 0, :], ACT.Silu))
            dve.after(t)
            t = dve.do(nc.vector.tensor_tensor(h32[:, u, :], pre[:, u, 0, :], pre[:, u, 1, :], ALU.mult))
        pool.after(t, made)
        t = pool.do(nc.gpsimd.tensor_copy(hid[0][:, u, :], h32[:, u, :]))
        dve.after(t, made)
        dve.do(nc.vector.tensor_tensor(hid[1][:, u, :], h32[:, u, :], hid[0][:, u, :].bitcast(F32), ALU.subtract), ready[u])

    gate_up(0)
    first = used.now()
    env["split_ahead"](1)
    hidden(0, 0, first)
    with env["loop"](tag, (FT - 2) // 2) as i:
        for u in (1, 2):
            gate_up(u % 2)
            made = used.now()
            down((u - 1) % 2)
            env["split_ahead"]()
            hidden(u % 2, i * 2 + u, made)
    gate_up(1)
    made = used.now()
    down(0)
    env["split_ahead"]()
    hidden(1, FT - 1, made)
    down(1)
    env["split_ahead"](1)
    for lane in (act, dve):
        lane.after(used.now())


def head_rstd(core, env, x, heads, dim, rstd, extra=None):
    nc, dve = core.nc, core.dve
    psum_c = env["psum_c"]
    for m in range(MT):
        dve.after(dve.done.now())
        t = dve.do(nc.vector.tensor_tensor(psum_c[:, 0:heads * dim[0]].rearrange("p (h d) -> p h d", h=heads), x(m), x(m), ALU.mult))
        dve.after(t)
        t = dve.do(nc.vector.tensor_reduce(rstd[:, m, :], psum_c[:, 0:heads * dim[0]].rearrange("p (h d) -> p h d", h=heads), AX, ALU.add))
        if extra is not None:
            dve.after(t)
            t = dve.do(nc.vector.tensor_scalar(rstd[:, m, :], rstd[:, m, :], extra[:, m:m + 1], None, ALU.add))
    dve.after(t)
    t = dve.do(nc.vector.tensor_scalar(rstd[:, :, :], rstd[:, :, :], 1.0 / dim[1], EPS, ALU.mult, ALU.add))
    core.pool.after(t)
    return core.pool.do(nc.gpsimd.tensor_tensor(rstd[:, :, :], rstd[:, :, :], env["half_neg"][:, 0:MT * heads]
                                                .rearrange("p (m h) -> p m h", m=MT), ALU.pow))


def scale_heads(core, dst, x, heads, rstd, ready):
    core.dve.after(ready)
    for m in range(MT):
        t = core.dve.do(core.nc.vector.tensor_tensor(dst(m), x(m), rstd[:, m, :].unsqueeze(2).to_broadcast(list(x(m).shape)), ALU.mult))
    return t


class HeadPairs:

    def __init__(self, core, env, tag, dk, phase):
        self.core, self.env, self.dk = core, env, dk
        self.qh = core.sb(tag + "_qh", [P, 2, MT, dk], ctx=phase)
        self.kh = core.sb(tag + "_kh", [P, 2, MT, dk], ctx=phase)
        self.vh = core.sb(tag + "_vh", [P, MT, P], ctx=phase)
        self.qt = core.sb(tag + "_qt", [P, 2, SEQ], ctx=phase)
        self.kt = core.sb(tag + "_kt", [P, 2, SEQ], ctx=phase)
        self.soft = Softmax(core, env, tag, phase)
        self.turned = Count(core, tag + "_turned")
        self.weighed = Count(core, tag + "_weighed")

    def run(self, build, build_v, gains, dk, causal, tile):
        core, nc, env = self.core, self.core.nc, self.env
        pe, act, dve, pool = core.pe, core.act, core.dve, core.pool
        built = []
        pool.after(self.turned.now())
        for b in range(2):
            build(b, self.qh[:, b, :, :], self.kh[:, b, :, :])
            built.append(pool.done.now())
        pool.after(self.weighed.now())
        build_v(self.vh)
        v_in = pool.done.now()
        scored = []
        for b in range(2):
            ps = env["psum_a"][0:dk, 512 * b:512 * b + 512]
            pe.after(built[b], act.done.now())
            for j, x in enumerate((self.qh, self.kh)):
                for m in range(MT):
                    mm = nc.tensor.transpose(ps[:, (2 * j + m) * P:(2 * j + m + 1) * P], x[:, b, m, 0:dk], env["ident"][:])
            t = pe.do(mm, self.turned)
            gq, gk = (env["head_cols"][0:dk, g:g + 1] for g in gains)
            lane = (act, dve)[b]
            lane.after(t)
            if b == 0:
                act.do(nc.scalar.activation(self.qt[0:dk, b, :], ps[:, 0:SEQ], ACT.Copy, scale=gq))
                t = act.do(nc.scalar.activation(self.kt[0:dk, b, :], ps[:, SEQ:512], ACT.Copy, scale=gk))
            else:
                dve.do(nc.vector.tensor_scalar(self.qt[0:dk, b, :], ps[:, 0:SEQ], gq, None, ALU.mult))
                t = dve.do(nc.vector.tensor_scalar(self.kt[0:dk, b, :], ps[:, SEQ:512], gk, None, ALU.mult))
            pe.after(t)
            sc = self.soft.scores(b)
            w0 = P if causal else SEQ
            nc.tensor.matmul(sc[:, 0:w0], self.qt[0:dk, b, 0:P], self.kt[0:dk, b, 0:w0], start=True, stop=True, skip_group_check=True)
            scored.append(pe.do(nc.tensor.matmul(sc[:, w0:w0 + SEQ], self.qt[0:dk, b, P:SEQ], self.kt[0:dk, b, :],
                                                 start=False, stop=True, skip_group_check=True)))
        turned = self.soft.probabilities(scored, causal)
        pe.after(v_in)
        for b in range(2):
            o, mm = self.soft.weigh(b, 0, [self.vh[:, m, :] for m in range(MT)], turned[b], causal)
            t = pe.do(mm, self.weighed)
            r = slice(64 * b, 64 * b + 64)
            hi, lo = (y[r, bass.ds(tile, 1), :].rearrange("p a t -> p (a t)") for y in env["Y"])
            env["round_split"](hi, lo, o[r, :], t, self.soft.o_free[b])


def split_heads(x, d):
    return x.rearrange("p (h d) -> p h d", d=d)


def natural_units(core, env, dst, widths):
    nc, act, dve = core.nc, core.act, core.dve
    at = 0
    for n in widths:
        def evacuate(ps, free, ready, at=at, n=n):
            act.after(ready)
            dve.after(ready)
            act.do(nc.scalar.activation(dst[:, 0, at:at + n], ps[:, 0:n], ACT.Copy), free)
            dve.do(nc.vector.tensor_copy(dst[:, 1, at:at + n], ps[:, 512:512 + n]), free)
        env["run_product"](env["product_natural"], env["X"], evacuate, n=n)
        at += n
    dve.after(env["a_free"].now(), env["b_free"].now())


def memory_pairs(core, env, pairs, q, layer):
    pool, nc = core.pool, core.nc
    HC = env["HC"]
    for i in range(MEM_HEADS // 2):
        def build(b, qh, kh):
            at = (2 * i + b) * HD
            pool.do(nc.gpsimd.tensor_copy(qh[:, :, 0:HD], q[:, :, at:at + HD]))
            pool.do(nc.gpsimd.tensor_copy(kh[:, :, 0:HD], env["mk_n"][:, :, at:at + HD]))

        def build_v(vh):
            pool.do(nc.gpsimd.tensor_copy(vh[:, :, :], env["mv_n"][:, :, i * P:(i + 1) * P]))
        pairs.run(build, build_v, (HC["mem_q_gain_2"] + layer, HC["mem_k_gain_2"] + layer), HD, False, HEADS // 2 + i)


def fox(core, env):
    nc, pe, act, dve, pool = core.nc, core.pe, core.act, core.dve, core.pool
    phase, psum_c, bcast = env["phase"], env["psum_c"], env["bcast"]
    DK = HD + 2
    fp = core.sb("fox_p", [P, MT, FOX_IN], ctx=phase)
    rstd = core.sb("fox_rstd", [P, MT, 2 * HEADS], ctx=phase)
    mrstd = core.sb("fox_mem_rstd", [P, MT, MEM_HEADS], ctx=phase)
    cum = core.sb("fox_cum", [P, 3, MT, HEADS], ctx=phase)
    logf, pos, neg = (cum[:, j, :, :] for j in range(3))
    pairs = HeadPairs(core, env, "fox", DK, phase)
    core.fence()
    natural_units(core, env, fp, [512] * 5 + [FOX_IN - 2560])
    core.fence()
    q_at = MIX * 3 + HEADS

    def qk(m):
        return split_heads(fp[:, m, 0:2 * MIX], HD)

    def mq(m):
        return split_heads(fp[:, m, q_at:q_at + MEM_W], HD)
    scale_heads(core, qk, qk, 2 * HEADS, rstd, head_rstd(core, env, qk, 2 * HEADS, (HD, HD), rstd))
    scale_heads(core, mq, mq, MEM_HEADS, mrstd, head_rstd(core, env, mq, MEM_HEADS, (HD, HD), mrstd))
    nc.scalar.preload_act_table_set("natural_log_exp_and_others")
    for m in range(MT):
        t = dve.do(nc.vector.scalar_tensor_tensor(out=logf[:, m, :], in0=fp[:, m, 3 * MIX:3 * MIX + HEADS], scalar=-1.0,
                                                  in1=bcast[:, 3, 0:HEADS], op0=ALU.mult, op1=ALU.subtract))
    dve.after(t)
    t = dve.do(nc.vector.tensor_scalar(pos, logf, 30.0, None, ALU.min))
    act.after(t)
    t = act.do(nc.scalar.activation(pos, pos, ACT.Exp))
    act.after(t)
    t = act.do(nc.scalar.activation(pos, pos, ACT.Ln, bias=1.0))
    dve.after(t)
    t = dve.do(nc.vector.tensor_tensor(logf, logf, pos, ALU.max))
    pe.after(t)
    nc.tensor.matmul(psum_c[:, 0:HEADS], env["upto"][:], logf[:, 0, :], start=True, stop=True, skip_group_check=True)
    nc.tensor.matmul(psum_c[:, 32:32 + HEADS], env["ones"][:], logf[:, 0, :], start=False, stop=False, skip_group_check=True)
    t = pe.do(nc.tensor.matmul(psum_c[:, 32:32 + HEADS], env["upto"][:], logf[:, 1, :], start=False, stop=True, skip_group_check=True))
    dve.after(t)
    sums = psum_c[:, 0:64].rearrange("p (m h) -> p m h", m=MT)[:, :, 0:HEADS]
    dve.do(nc.vector.tensor_copy(neg, sums))
    dve.do(nc.vector.tensor_scalar(pos, sums, -1.0, None, ALU.mult))
    pool.do(nc.gpsimd.memset(pairs.qh[:, :, :, :], 1.0))
    pool.do(nc.gpsimd.memset(pairs.kh[:, :, :, :], 1.0))
    core.fence()
    with env["loop"]("fox", HEADS // 2) as i:
        def build(b, qh, kh):
            at = i * P + HD * b
            pool.do(nc.gpsimd.tensor_copy(qh[:, :, 0:HD], fp[:, :, bass.ds(at, HD)]))
            pool.do(nc.gpsimd.tensor_copy(qh[:, :, HD:HD + 1], pos[:, :, bass.ds(i * 2 + b, 1)]))
            pool.do(nc.gpsimd.tensor_copy(kh[:, :, 0:HD], fp[:, :, bass.ds(at + MIX, HD)]))
            pool.do(nc.gpsimd.tensor_copy(kh[:, :, HD + 1:HD + 2], neg[:, :, bass.ds(i * 2 + b, 1)]))

        def build_v(vh):
            pool.do(nc.gpsimd.tensor_copy(vh[:, :, :], fp[:, :, bass.ds(i * P + 2 * MIX, P)]))
        pairs.run(build, build_v, (env["HC"]["fox_q_gain_2"], env["HC"]["fox_k_gain_2"]), DK, True, i)
    memory_pairs(core, env, pairs, fp[:, :, q_at:q_at + MEM_W], 0)


def mla(core, env):
    nc, pe, act, dve, pool = core.nc, core.pe, core.act, core.dve, core.pool
    phase, psum_a, psum_b, psum_c = env["phase"], env["psum_a"], env["psum_b"], env["psum_c"]
    col_of, Y, used = env["col_of"], env["Y"], env["used"]
    lp = core.sb("mla_p", [P, MT, MLA_IN], ctx=phase)
    q_n = core.sb("mla_q", [P, MT, HEADS * QK], ctx=phase)
    kv_n = core.sb("mla_kv", [P, MT, HEADS * 2 * HD], ctx=phase)
    core.fence()
    natural_units(core, env, lp, [512, MLA_IN - 512])
    core.fence()
    k_r = lp[:, :, Q_RANK + KV_RANK:Q_RANK + KV_RANK + ROPE]
    mem_q = lp[:, :, MLA_IN - MEM_W:MLA_IN]
    for slot, at, n in ((0, 0, Q_RANK), (8, Q_RANK, KV_RANK)):
        t = env["row_rstd"]([lp[:, m, at:at + n] for m in range(MT)], n, slot, [dve.done.now()], q_n[:, 0, :])
        for m in range(MT):
            dve.after(t)
            t = dve.do(nc.vector.tensor_scalar(lp[:, m, at:at + n], lp[:, m, at:at + n], env["small"][:, slot + 2 + m:slot + 3 + m], None, ALU.mult))
    env["turn_and_split"](lp[:, :, 0:Q_RANK], Y, 2, col_of["mla_qa_norm_2"], t)
    t = env["turn_and_split"](lp[:, :, Q_RANK:Q_RANK + KV_RANK], Y, 1, col_of["mla_kva_norm_2"], t, k_to=2)
    pe.after(t)
    core.fence()

    def up(ps, stride, kt, k0, n):
        s = env["take_piece"]()
        w = env["weights"](s, kt, n)
        for k in range(kt):
            for m in range(MT):
                for c in range(0, n, 512):
                    wd = min(512, n - c)
                    mm = env["three"](ps[:, m * stride + c:m * stride + c + wd], [y[:, k0 + k, m * P:(m + 1) * P] for y in Y],
                                      [x[:, k, c:c + wd] for x in w], k == 0, k == kt - 1)
        return pe.do(mm, used)

    def evict(dst, ps, stride, n, ready):
        act.after(ready)
        dve.after(ready)
        a = act.do(nc.scalar.activation(dst(0), ps[:, 0:n], ACT.Copy))
        v = dve.do(nc.vector.tensor_copy(dst(1), ps[:, stride:stride + n]))
        return [a, v]

    for dst, kt, k0, rest, ps in ((q_n, 2, 0, HEADS * QK - 1024, psum_a), (kv_n, 1, 2, 512, psum_b)):
        t1 = up(psum_c, 1024, kt, k0, 1024)
        t2 = up(ps, 512, kt, k0, rest)
        env["split_ahead"]()
        t = evict(lambda m: dst[:, m, 0:1024], psum_c, 1024, 1024, t1)
        pe.after(*t)
        evict(lambda m: dst[:, m, 1024:1024 + rest], ps, 512, rest, t2)
    core.fence()

    rotary = ExitStack()
    rot = core.sb("mla_rot", [P, 6, MT, 16], ctx=rotary)
    ang, cos, sin, kk, red, posf = (rot[:, j, :, :] for j in range(6))
    TWO_PI = (6.28125, 0.0019350051879882812, 3.0199159819e-07)
    MAGIC = 12582912.0
    t = dve.do(nc.vector.tensor_copy(posf[:, :, 0:1], env["pos_i"][:].unsqueeze(2)))
    for m in range(MT):
        dve.after(t)
        t = dve.do(nc.vector.tensor_scalar(ang[:, m, :], env["inv_freq"][:], posf[:, m, 0:1], None, ALU.mult))
    nc.scalar.preload_act_table_set("silu_and_others")
    for dst, quarter in ((sin, 0.0), (cos, 0.25)):
        def step(ins):
            dve.after(dve.do(ins))
        dve.after(dve.done.now(), act.done.now())
        step(nc.vector.tensor_scalar(kk, ang, 1.0 / (2.0 * math.pi), quarter, ALU.mult, ALU.add))
        step(nc.vector.tensor_scalar(kk, kk, MAGIC, None, ALU.add))
        step(nc.vector.tensor_scalar(kk, kk, MAGIC, None, ALU.subtract))
        src = ang
        for part in TWO_PI:
            for m in range(MT):
                nc_ins = nc.vector.scalar_tensor_tensor(out=red[:, m, :], in0=kk[:, m, :], scalar=-part, in1=src[:, m, :],
                                                        op0=ALU.mult, op1=ALU.add)
                step(nc_ins)
            src = red
        step(nc.vector.tensor_scalar(red, red, quarter * 2.0 * math.pi, None, ALU.add))
        step(nc.vector.tensor_scalar(red, red, 3.1415925, -3.1415925, ALU.min, ALU.max))
        act.after(dve.done.now())
        act.do(nc.scalar.activation(dst, red, ACT.Sin))
    dve.after(act.done.now())

    def rope(x, heads):
        for m in range(MT):
            x1, x2 = x(m)[:, :, 0:16], x(m)[:, :, 16:32]
            c, s = (f[:, m, :].unsqueeze(1).to_broadcast([P, heads, 16]) for f in (cos, sin))
            tmp = [psum_c[:, 512 * j:512 * j + heads * 16].rearrange("p (h d) -> p h d", h=heads) for j in range(4)]
            sb_tmp = [core_tmp[:, j, 0:heads * 16].rearrange("p (h d) -> p h d", h=heads) for j in range(2)]
            dve.after(dve.done.now())
            dve.do(nc.vector.tensor_tensor(tmp[0], x1, c, ALU.mult))
            dve.do(nc.vector.tensor_tensor(sb_tmp[0], x2, s, ALU.mult))
            dve.do(nc.vector.tensor_tensor(tmp[1], x1, s, ALU.mult))
            t = dve.do(nc.vector.tensor_tensor(sb_tmp[1], x2, c, ALU.mult))
            dve.after(t)
            dve.do(nc.vector.tensor_tensor(x1, tmp[0], sb_tmp[0], ALU.subtract))
            dve.do(nc.vector.tensor_tensor(x2, tmp[1], sb_tmp[1], ALU.add))

    core_tmp = core.sb("mla_tmp", [P, 2, HEADS * 16], ctx=rotary)
    rope(lambda m: split_heads(q_n[:, m, :], QK)[:, :, HD:QK], HEADS)
    rope(lambda m: k_r[:, m, :].unsqueeze(1), 1)
    rotary.close()
    core.fence()

    rstd = core.sb("mla_rstd", [P, 3, MT, HEADS], ctx=phase)
    mrstd = core.sb("mla_mem_rstd", [P, MT, MEM_HEADS], ctx=phase)
    extra = core.sb("mla_extra", [P, MT], ctx=phase)
    dve.after(dve.done.now())
    for m in range(MT):
        dve.after(dve.done.now())
        dve.do(nc.vector.tensor_tensor(psum_c[:, 0:ROPE], k_r[:, m, :], k_r[:, m, :], ALU.mult))
        dve.after(dve.done.now())
        dve.do(nc.vector.tensor_reduce(extra[:, m:m + 1], psum_c[:, 0:ROPE], AX, ALU.add))

    def q(m):
        return split_heads(q_n[:, m, :], QK)

    def k(m):
        return split_heads(kv_n[:, m, :], 2 * HD)[:, :, 0:HD]

    def mq(m):
        return split_heads(mem_q[:, m, :], HD)
    scale_heads(core, q, q, HEADS, rstd[:, 0, :, :], head_rstd(core, env, q, HEADS, (QK, QK), rstd[:, 0, :, :]))
    t_k = head_rstd(core, env, k, HEADS, (HD, QK), rstd[:, 1, :, :], extra)
    scale_heads(core, k, k, HEADS, rstd[:, 1, :, :], t_k)
    scale_heads(core, mq, mq, MEM_HEADS, mrstd, head_rstd(core, env, mq, MEM_HEADS, (HD, HD), mrstd))
    pairs = HeadPairs(core, env, "mla", QK, phase)
    core.fence()
    nc.scalar.preload_act_table_set("natural_log_exp_and_others")
    with env["loop"]("mla", HEADS // 2) as i:
        def build(b, qh, kh):
            pool.do(nc.gpsimd.tensor_copy(qh[:, :, 0:QK], q_n[:, :, bass.ds(i * (2 * QK) + QK * b, QK)]))
            pool.do(nc.gpsimd.tensor_copy(kh[:, :, 0:HD], kv_n[:, :, bass.ds(i * (4 * HD) + 2 * HD * b, HD)]))
            pool.do(nc.gpsimd.tensor_tensor(kh[:, :, HD:QK], k_r, rstd[:, 1, :, bass.ds(i * 2 + b, 1)].to_broadcast([P, MT, ROPE]), ALU.mult))

        def build_v(vh):
            for b in range(2):
                pool.do(nc.gpsimd.tensor_copy(vh[:, :, HD * b:HD * b + HD], kv_n[:, :, bass.ds(i * (4 * HD) + (2 * HD * b + HD), HD)]))
        pairs.run(build, build_v, (env["HC"]["mla_q_gain_2"], env["HC"]["mla_k_gain_2"]), QK, True, i)
    memory_pairs(core, env, pairs, mem_q, 1)


_OUTS = [((1, SEQ, D), "float32")]


def kernel(**inputs):
    import numpy as _np
    import concourse.bacc as _bacc
    from concourse.bass_utils import run_bass_kernel_spmd as _run

    def build(strides):
        nc = _bacc.Bacc("TRN2", target_bir_lowering=False, num_devices=1)
        arrays, ins = {}, {}
        for name, value in inputs.items():
            a = _np.ascontiguousarray(value)
            if a.size == 0:
                continue
            arrays[f"in_{name}_dram"] = a
            ins[name] = nc.dram_tensor(f"in_{name}_dram", a.shape, mybir.dt.from_np(a.dtype), kind="ExternalInput").ap()
        out = nc.dram_tensor("out_0_dram", _OUTS[0][0], F32, kind="ExternalOutput").ap()
        return nc, arrays, emit(nc, ins, out, strides)

    _, _, strides = build({})
    nc, arrays, again = build(strides)
    assert again == strides
    r = _run(nc, [arrays], core_ids=[0])
    return r.results[0]["out_0_dram"]
```

```python
from contextlib import ExitStack, contextmanager
import math

import concourse.bass as bass
from concourse import mybir

F32 = mybir.dt.float32
F32R = mybir.dt.float32r
I32 = mybir.dt.int32
ALU = mybir.AluOpType
ACT = mybir.ActivationFunctionType
AX = mybir.AxisListType.X
ENG = mybir.EngineType

P = 128
SEQ = 256
MT = SEQ // P
D = 1024
KD = D // P
EPS = 1e-6
SLOTS = 4
PIECE = 2048
NEG = -1.0e30

SB_HEADS, SB_DIM = 16, 64
SSM_INNER, SSM_HEADS, SSM_HD, SSM_GROUPS, SSM_STATE = 2048, 32, 64, 4, 128
XBC = SSM_INNER + 2 * SSM_GROUPS * SSM_STATE
GROUP_HEADS = SSM_HEADS // SSM_GROUPS
XA_HEADS, XA_DIM = 4, 256
FFN = 2816
FT = FFN // P
C_Q, C_K, C_V, C_Z = 0, D, 2 * D, 3 * D
C_XBC = C_Z + SSM_INNER
C_DT = C_XBC + XBC
C_GA = C_DT + SSM_HEADS
C_GS = C_GA + D

HEADS, HD = 12, 64
MIX = HEADS * HD
MEM_HEADS = 4
MEM_W = MEM_HEADS * HD
FOX_IN = 3 * MIX + HEADS + MEM_W
Q_RANK, KV_RANK, ROPE = 256, 128, 32
QK = HD + ROPE
MLA_IN = Q_RANK + KV_RANK + ROPE + MEM_W


class Count:

    def __init__(self, core, name, unit=1):
        self.name, self.unit = name, unit
        self.sem = core.ctx.enter_context(core.nc.semaphore(name))
        self.base, self.k, self.least = 0, 0, 0
        core.counts.append(self)

    def value(self):
        return self.base + self.k

    def mark(self, ins, units=1):
        ins.then_inc(self.sem, self.unit * units)
        self.k += units
        return self.now()

    def now(self, ahead=0):
        return (self, self.base, self.k + ahead)


class Lane:

    def __init__(self, core, engine, name):
        self.e = engine
        self.done = Count(core, name + "_done")
        self.seen = {}
        self.gate = core.ctx.enter_context(core.nc.semaphore(name + "_gate")) if name == "pool" else None

    def after(self, *tokens):
        computed = False
        for count, base, k in tokens:
            if isinstance(base, int) and base + k <= 0:
                continue
            key = (count.name, base if isinstance(base, int) else id(base))
            if self.seen.get(key, -1 << 30) >= k:
                continue
            self.seen[key] = k
            self.e.wait_ge(count.sem, (base + k) * count.unit)
            if not isinstance(base, int):
                assert count.least + k > 0, count.name
                computed = True
        if computed and self.gate is not None:
            self.e.sem_inc(self.gate)
        return self

    def do(self, ins, by=None):
        return (by or self.done).mark(ins)


class Core:
    def __init__(self, nc, ctx, strides):
        self.nc, self.ctx, self.strides, self.new_strides, self.counts = nc, ctx, strides, {}, []
        self.pe = Lane(self, nc.tensor, "pe")
        self.act = Lane(self, nc.scalar, "act")
        self.dve = Lane(self, nc.vector, "dve")
        self.pool = Lane(self, nc.gpsimd, "pool")
        self.lanes = [self.pe, self.act, self.dve, self.pool]
        self.piece = 0
        self.address = {}

    def sb(self, name, shape, dt=F32, ctx=None):
        tensor = (ctx or self.ctx).enter_context(self.nc.sbuf_tensor(name, shape, dt))
        self.address[name] = self.nc.sbuf_base - 4 * math.prod(shape[1:])
        return tensor

    def over(self, name, host, skip, shape):
        return self.nc.alloc_sbuf_tensor_at(name, shape, F32, offset=self.address[host] + 4 * skip)

    def forget(self):
        for lane in self.lanes:
            lane.seen = {}

    @contextmanager
    def loop(self, name, n):
        stride = self.strides.get(name, {})
        for c in self.counts:
            if c.k == 0 and isinstance(c.base, int) and c.base == 0 and stride.get(c.name):
                self.nc.vector.sem_inc(c.sem, c.unit)
                c.k = 1
        starts = {c.name: (c.base + c.k) for c in self.counts}
        piece = self.piece
        self.forget()
        with self.nc.Fori(0, n, engines=[ENG.PE, ENG.Activation, ENG.DVE, ENG.Pool]) as i:
            for c in self.counts:
                d = stride.get(c.name, 0)
                c.base, c.k = (i * d + starts[c.name] if d else starts[c.name]), 0
                c.least = starts[c.name]
            yield i
        self.new_strides[name] = {c.name: c.k for c in self.counts if c.k}
        for c in self.counts:
            c.base, c.k = starts[c.name] + n * c.k, 0
        self.piece = piece + n * (self.piece - piece)
        self.forget()

    def fence(self, *lanes):
        for lane in lanes or self.lanes:
            lane.after(*[c.now() for c in self.counts if c.unit == 1])


def emit(nc, ins, out, strides):
    with ExitStack() as ctx:
        core = Core(nc, ctx, strides)
        program(core, ins, out)
        return core.new_strides


def program(core, ins, out):
    nc, pe, act, dve, pool = core.nc, core.pe, core.act, core.dve, core.pool
    sp = nc.sync
    sb = core.sb

    def count(name, unit=1):
        return Count(core, name, unit)

    raw = sb("raw", [P, SLOTS, PIECE])
    w_hi = sb("w_hi", [P, SLOTS, PIECE], F32R)
    w_lo = sb("w_lo", [P, SLOTS, PIECE], F32R)
    x_hi = sb("x_hi", [P, KD, SEQ], F32R)
    x_lo = sb("x_lo", [P, KD, SEQ], F32R)
    y_hi = sb("y_hi", [P, 2 * KD, SEQ], F32R)
    y_lo = sb("y_lo", [P, 2 * KD, SEQ], F32R)
    res = sb("res", [P, MT, D])
    ident = sb("ident", [P, P])
    ones = sb("ones", [P, P])
    upto = sb("upto", [P, P])
    beyond = sb("beyond", [P, P])
    neg_from = sb("neg_from", [P, P])
    neg_ones = sb("neg_ones", [P, P])
    strict = sb("strict", [P, P])
    causal = sb("causal", [P, P])
    half_neg = sb("half_neg", [P, 64])
    cols = sb("cols", [P, 5 * P])
    small = sb("small", [P, 256])
    psum_a = ctx_psum(core, "psum_a", [P, 1024])
    psum_b = ctx_psum(core, "psum_b", [P, 1024])
    psum_c = ctx_psum(core, "psum_c", [P, 2048])

    arrived = [count(f"arrived{s}", 16) for s in range(SLOTS)]
    rounded = count("rounded")
    split = count("split")
    used = count("used")
    a_free = count("a_free")
    b_free = count("b_free")
    loaded = count("loaded", 16)
    stored = count("stored", 16)
    rows_loaded = count("rows_loaded", 16)

    w_in = ins["w_in"][0].rearrange("(k p) n -> p k n", p=P)

    def block(w, k0, nk, col, n):
        view = w.rearrange("(k p) n -> p k n", p=P)
        return [(0, nk, n, view[:, k0:k0 + nk, bass.ds(col, n)])]

    def gate_up(w, h):
        view = w.rearrange("(k p) n -> p k n", p=P)
        return [(j * P, KD, 2 * P, view[:, :, bass.ds(h * P + j * FFN, P)]) for j in range(2)]

    def down(w, h):
        view = w.rearrange("(k p) n -> k p n", p=P)
        return [(0, 1, D, view[bass.ds(h, 1), :, :].rearrange("k p n -> p k n"))]

    def halves(w, col, n=512, k0=0):
        return [block(w, k0, 4, col, n), block(w, k0 + 4, 4, col, n)]

    def square(w, col=0):
        return [q for c in range(2) for q in halves(w, col + 512 * c)]

    W = {k: v[0] for k, v in ins.items() if len(v.shape) == 3 and k.startswith(("w_", "fox_w", "mla_w"))}
    win = W["w_in"]

    def ffn_entries(gu, dn):
        return [("once", [gate_up(gu, 0)]),
                ("loop", (FT - 2) // 2, lambda i: [q for u in (1, 2) for q in (
                    gate_up(gu, i * 2 + u), down(dn, i * 2 + (u - 1)))]),
                ("once", [gate_up(gu, FT - 1), down(dn, FT - 2), down(dn, FT - 1)])]

    wo2 = ins["w_out_2"]
    plan = [("once", square(win, C_Q) + square(win, C_K) + square(win, C_V)),
            ("once", square(win, C_GA) + square(W["w_br_att"])),
            ("loop", 2, lambda i: [q for c in range(2) for q in halves(win, i * 1024 + (C_XBC + 512 * c))]),
            ("once", square(win, C_XBC + SSM_INNER) + halves(win, C_DT, SSM_HEADS)),
            ("loop", 2, lambda i: [q for c in range(2) for q in halves(win, i * 1024 + (C_Z + 512 * c))]),
            ("once", square(win, C_GS) + [q for c in range(2) for k0 in (0, KD) for q in halves(W["w_br_ssm"], 512 * c, k0=k0)]),
            ("once", square(W["w_mix_out"])),
            ("once", square(W["w_xkv"]) + square(W["w_xkv"], D) + square(W["w_xq"]) + square(W["w_xo"])),
            *ffn_entries(W["w_gu"], W["w_down"]),
            ("once", halves(ins["w_mem_kv_2"], 0)),
            ("once", [q for c in range(5) for q in halves(W["fox_w_in_2"], 512 * c)] + halves(W["fox_w_in_2"], 2560, FOX_IN - 2560)),
            ("once", square(wo2[0])),
            *ffn_entries(ins["ffn_w_up_2"][0], ins["ffn_w_down_2"][0]),
            ("once", halves(W["mla_w_in_2"], 0) + halves(W["mla_w_in_2"], 512, MLA_IN - 512)),
            ("once", [block(W["mla_w_q_up_2"], 0, 2, 0, 1024), block(W["mla_w_q_up_2"], 0, 2, 1024, HEADS * QK - 1024),
                      block(W["mla_w_kv_up_2"], 0, 1, 0, 1024), block(W["mla_w_kv_up_2"], 0, 1, 1024, 512)]),
            ("once", square(wo2[1])),
            *ffn_entries(ins["ffn_w_up_2"][1], ins["ffn_w_down_2"][1])]
    shapes = []
    for kind, *rest in plan:
        for q in (rest[0] if kind == "once" else rest[1](0) * rest[0]):
            shapes.append((q[0][1] * q[0][2], len(q)))

    def weight_stream():
        at = 0

        def load(pieces, at0, step):
            for j, parts in enumerate(pieces):
                s = (at0 + j) % SLOTS
                need = step + (at0 + j - SLOTS + 1)
                if not isinstance(need, int) or need > 0:
                    sp.wait_ge(split.sem, need)
                for off, nk, n, src in parts:
                    dst = raw[:, s, 0:nk * n].rearrange("p (k n) -> p k n", n=n)[:, :, off:off + src.shape[2]]
                    sp.dma_start(dst, src).then_inc(arrived[s].sem, 16)

        for kind, *rest in plan:
            if kind == "once":
                load(rest[0], at, 0)
                at += len(rest[0])
            else:
                n, pieces = rest
                per = len(pieces(0))
                assert per % SLOTS == 0 and at >= SLOTS
                with sp.Fori(0, n) as i:
                    load(pieces(i), at, i * per)
                at += n * per

    split_at = [0]

    def split_ahead(n=2):
        for _ in range(n):
            if split_at[0] >= len(shapes):
                return
            size, loads = shapes[split_at[0]]
            s = split_at[0] % SLOTS
            split_at[0] += 1
            arrived[s].k += loads
            act.after(arrived[s].now(), (used, rounded.base, rounded.k + 1 - SLOTS))
            act.do(nc.scalar.activation(w_hi[:, s, 0:size], raw[:, s, 0:size], ACT.Copy), rounded)
            dve.after(rounded.now())
            dve.do(nc.vector.tensor_tensor(w_lo[:, s, 0:size], raw[:, s, 0:size],
                                           w_hi[:, s, 0:size].bitcast(F32), ALU.subtract), split)

    @contextmanager
    def loop(name, n):
        start = split_at[0]
        with core.loop(name, n) as i:
            yield i
        split_at[0] = start + n * (split_at[0] - start)

    def three(out_ap, l, r, start, stop):
        nc.tensor.matmul(out_ap, l[0], r[0], start=start, stop=False, skip_group_check=True)
        nc.tensor.matmul(out_ap, l[0], r[1], start=False, stop=False, skip_group_check=True)
        return nc.tensor.matmul(out_ap, l[1], r[0], start=False, stop=stop, skip_group_check=True)

    def take_piece():
        s = core.piece % SLOTS
        core.piece += 1
        pe.after((split, used.base, used.k + 1))
        return s

    def weights(s, nk, n):
        return [w[:, s, 0:nk * n].rearrange("p (k n) -> p k n", n=n) for w in (w_hi, w_lo)]

    X, Y = (x_hi, x_lo), (y_hi, y_lo)

    def product_turned(ps, act_in, k0=0, first=True, last=True):
        for half in range(2):
            s = take_piece()
            w = weights(s, 4, 512)
            for k in range(4):
                kk = half * 4 + k
                for c in range(4):
                    mm = three(ps[:, c * SEQ:(c + 1) * SEQ], [x[:, k, c * P:(c + 1) * P] for x in w],
                               [x[:, k0 + kk, :] for x in act_in], first and kk == 0 and c % 2 == 0, last and kk == 7)
            pe.do(mm, used)

    def product_natural(ps, act_in, n=512):
        for half in range(2):
            s = take_piece()
            w = weights(s, 4, n)
            for k in range(4):
                kk = half * 4 + k
                for m in range(MT):
                    mm = three(ps[:, m * 512:m * 512 + n], [x[:, kk, m * P:(m + 1) * P] for x in act_in],
                               [x[:, k, :] for x in w], kk == 0, kk == 7)
            pe.do(mm, used)

    banks = [(psum_a, a_free), (psum_b, b_free)]
    turn = [0]

    def next_bank():
        ps, free = banks[turn[0] % 2]
        turn[0] += 1
        pe.after(free.now())
        return ps, free

    def run_product(kind, act_in, evacuate, **kw):
        ps, free = next_bank()
        kind(ps, act_in, **kw)
        split_ahead()
        evacuate(ps, free, used.now())

    def seq(lane, *steps):
        t = None
        for f in steps:
            if t:
                lane.after(t)
            t = lane.do(f())
        return t

    def round_split(hi, lo, src_f32, ready, free=None, scale=None):
        act.after(ready)
        sc = 1.0 if scale is None else scale
        t = act.do(nc.scalar.activation(hi, src_f32, ACT.Copy, scale=sc))
        dve.after(t, ready)
        return dve.do(nc.vector.scalar_tensor_tensor(out=lo, in0=src_f32, scalar=sc, in1=hi.bitcast(F32),
                                                     op0=ALU.mult, op1=ALU.subtract), free)

    def power(out_ap, in_ap, n, ready):
        pool.after(ready)
        return pool.do(nc.gpsimd.tensor_tensor(out_ap, in_ap, half_neg[:, 0:n], ALU.pow))

    def row_rstd(parts, width, slot, ready, junk):
        n = len(parts)
        act.after(*ready)
        for j, part in enumerate(parts):
            act.after(act.done.now())
            t = act.do(nc.scalar.activation(junk[:, 0:width], part, ACT.Square, accum_out=small[:, slot + j:slot + j + 1]))
        dve.after(t)
        t = dve.do(nc.vector.tensor_scalar(small[:, slot:slot + n], small[:, slot:slot + n], 1.0 / width, EPS, ALU.mult, ALU.add))
        return power(small[:, slot + n:slot + 2 * n], small[:, slot:slot + n], n, t)

    quarters = [(psum_a[:, 0:512], count("quarter0")), (psum_b[:, 0:512], count("quarter1")),
                (psum_a[:, 512:1024], count("quarter2")), (psum_b[:, 512:1024], count("quarter3"))]

    def turn_and_split(src, dst, kd, gain, ready, k_to=0, diagonal=None):
        pe.after(a_free.now(), b_free.now(), ready)
        for k in range(kd):
            ps, free = quarters[k % 4]
            pe.after(free.now())
            for m in range(MT):
                part = src[:, m, k * P:(k + 1) * P]
                if diagonal is None:
                    mm = nc.tensor.transpose(ps[:, m * P:(m + 1) * P], part, ident[:])
                else:
                    mm = nc.tensor.matmul(ps[:, m * P:(m + 1) * P], part, diagonal[:, m, :], start=m == 0, stop=True,
                                          skip_group_check=True)
            t = pe.do(mm)
            t = round_split(dst[0][:, k_to + k, :], dst[1][:, k_to + k, :], ps[:, 0:SEQ], t, free,
                            scale=cols[:, gain + k:gain + k + 1])
        pe.after(*[q[1].now() for q in quarters])
        return t

    diag = sb("diag", [P, MT, P])
    squares = sb("squares", [P, 8])

    def mean_rstd(sums, out_cols, width, ready):
        dve.after(*ready)
        t = dve.do(nc.vector.tensor_scalar(sums, sums, 1.0 / width, EPS, ALU.mult, ALU.add))
        return power(out_cols, sums, sums.shape[1], t)

    def rms_turned(src, dst, gain, ready):
        act.after(*ready[0])
        ta = act.do(nc.scalar.activation(psum_c[:, 0:D], src[:, 0, :], ACT.Square, accum_out=squares[:, 0:1]))
        dve.after(*ready[1])
        tv = dve.do(nc.vector.scalar_tensor_tensor(out=psum_c[:, D:2 * D], in0=src[:, 1, :], scalar=1.0, in1=src[:, 1, :],
                                                   op0=ALU.mult, op1=ALU.mult, accum_out=squares[:, 1:2]))
        t = mean_rstd(squares[:, 0:2], squares[:, 2:4], D, [ta, tv])
        dve.after(t, pe.done.now())
        for m in range(MT):
            t = dve.do(nc.vector.tensor_scalar(diag[:, m, :], ident[:], squares[:, 2 + m:3 + m], None, ALU.mult))
        return turn_and_split(src, dst, KD, gain, t, diagonal=diag)

    def gain_and_squares(ps, og, g, sums, ready, free=None):
        act.after(ready)
        dve.after(ready)
        a = act.do(nc.scalar.activation(og[0], ps[0], ACT.Square, accum_out=sums[0]))
        v = dve.do(nc.vector.tensor_tensor(og[1], ps[1], g, ALU.mult))
        dve.after(a)
        act.after(v, a)
        ta = act.do(nc.scalar.activation(ps[1], ps[1], ACT.Square, accum_out=sums[1]), free)
        tv = dve.do(nc.vector.tensor_tensor(og[0], ps[0], g, ALU.mult), free)
        return ta, tv

    names = [("g_pre_mix", 8), ("g_pre_xa", 8), ("g_mem", 8), ("g_pre_ffn", 8), ("norm_mix_2", 16), ("norm_ffn_2", 16),
             ("mem_norm_2", 8), ("g_ssm_norm", 16), ("conv_w", 96), ("conv_b", 24), ("ffn_conv_w_2", 264),
             ("ffn_conv_b_2", 88), ("mla_qa_norm_2", 2), ("mla_kva_norm_2", 1)]
    col_of, at = {}, 0
    for name, n in names:
        col_of[name] = at
        at += n
    assert at <= 5 * P
    rowed = {}
    for name, n in names:
        v = ins[name]
        letters = "abc"[:len(v.shape)]
        rowed[name] = v.rearrange(f"{' '.join(letters)} -> ({' '.join(letters)})") if len(v.shape) > 1 else v

    head_cols = sb("head_cols", [P, 16])
    HC = {"fox_q_gain_2": 0, "fox_k_gain_2": 1, "mla_q_gain_2": 2, "mla_k_gain_2": 3, "mem_q_gain_2": 4, "mem_k_gain_2": 6}
    bcast = sb("bcast", [P, 4, 32])
    inv_freq = sb("inv_freq", [P, 16])
    pos_i = sb("pos_i", [P, MT], I32)
    scales = sb("scales", [P, 1])

    def load_on(where, dst, src, engine=nc.gpsimd):
        return where.mark(engine.dma_start(dst, src))

    def load(dst, src):
        return load_on(loaded, dst, src)

    with ExitStack() as phase:
        sp.dma_start(res[:, :, :], ins["x"][0].rearrange("(m p) d -> p m d", p=P)).then_inc(stored.sem, 16)
        stored.k += 1
        x_in = stored.now()
        weight_stream()
        stage = core.sb("stage", [P, 5, P], ctx=phase)
        pool.do(nc.gpsimd.memset(ones[:], 1.0))

        def sel(dst, src, pattern, mult, op, fill, base=0):
            pool.after(pool.done.now())
            return pool.do(nc.gpsimd.affine_select(out=dst, in_=src, compare_op=op, fill=fill, base=base,
                                                   pattern=pattern, channel_multiplier=mult))
        eye = sel(ident[:], ones[:], [[-1, P]], 1, ALU.is_equal, 0.0)
        pool.do(nc.gpsimd.memset(half_neg[:], -0.5))
        pool.do(nc.gpsimd.memset(head_cols[:], 1.0))
        pool.do(nc.gpsimd.memset(neg_ones[:], -1.0))
        pool.do(nc.gpsimd.memset(causal[:], 0.0))
        sel(upto[:], ones[:], [[1, P]], -1, ALU.is_ge, 0.0)
        sel(beyond[:], ones[:], [[-1, P]], 1, ALU.is_gt, 0.0)
        sel(strict[:], ones[:], [[1, P]], -1, ALU.is_gt, 0.0)
        sel(neg_from[:], neg_ones[:], [[-1, P]], 1, ALU.is_ge, 0.0)
        sel(causal[:], causal[:], [[-1, P]], 1, ALU.is_ge, NEG)
        for f in range(16):
            pool.do(nc.gpsimd.memset(inv_freq[:, f:f + 1], float(10000.0 ** (-2.0 * f / ROPE))))
        consts = pool.done.now()
        for name, n in names:
            done = 0
            while done < n:
                r, tile = (col_of[name] + done) % P, (col_of[name] + done) // P
                k = min(n - done, P - r)
                load_on(rows_loaded, stage[r:r + k, tile, :], rowed[name][done * P:(done + k) * P].rearrange("(r c) -> r c", c=P), nc.scalar)
                done += k
        rows_in = rows_loaded.now()
        for name, c in HC.items():
            for l in range(ins[name].shape[0]):
                load(head_cols[0:ins[name].shape[1], c + l:c + l + 1], ins[name][l].rearrange("(d a) -> d a", a=1))
        for j, name in enumerate(("dt_bias", "a_log", "d_skip", "fox_b_f_2")):
            n = ins[name].shape[1]
            load(bcast[:, j, 0:n], ins[name][0].partition_broadcast(P))
        for m in range(MT):
            load(pos_i[:, m:m + 1], ins["positions_2"][0, m * P:(m + 1) * P].rearrange("(d a) -> d a", a=1))
        all_in = loaded.now()

        split_ahead(2)
        pe.after(rows_in, eye)
        for j in range(5):
            n = min(P, at - j * P)
            mm = nc.tensor.transpose(psum_c[:, j * P:j * P + n], stage[0:n, j, :], ident[0:n, 0:n])
        t = pe.do(mm)
        dve.after(t)
        v = dve.do(nc.vector.tensor_copy(cols[:, 0:at], psum_c[:, 0:at]))
        act.after(v)
        dve.after(v)
        rms_turned(res, X, col_of["g_pre_mix"], [[x_in], [x_in]])
        core.fence(pool)

    def copy_out(dst, scale=1.0):
        def evacuate(ps, free, ready):
            act.after(ready)
            dve.after(ready)
            a = act.do(nc.scalar.activation(dst(0), ps[:, 0:512].rearrange("p (c t) -> p c t", c=dst(0).shape[1]), ACT.Copy, scale=scale), free)
            dve.do(nc.vector.tensor_scalar(dst(1), ps[:, 512:1024].rearrange("p (c t) -> p c t", c=dst(1).shape[1]), scale, None, ALU.mult), free)
        return evacuate

    mix = ExitStack()
    merged = core.sb("merged", [P, KD, SEQ], ctx=mix)
    with ExitStack() as phase:
        q_t = core.sb("q_t", [P, KD, SEQ], ctx=phase)
        k_t = core.sb("k_t", [P, KD, SEQ], ctx=phase)
        v_n = core.sb("v_n", [P, MT, D], ctx=phase)
        for dst, scale in ((q_t, SB_DIM ** -0.5), (k_t, 1.0)):
            for c in range(2):
                run_product(product_turned, X, copy_out(lambda j: dst[:, 4 * c + 2 * j:4 * c + 2 * j + 2, :], scale))
        for c in range(2):
            run_product(product_natural, X, copy_out(lambda j: v_n[:, j:j + 1, 512 * c:512 * c + 512]))
        for lane in (act, dve, pe, pool):
            lane.after(all_in, consts)
        for c, l, dim in ((HC["fox_q_gain_2"], 1, HD), (HC["mla_q_gain_2"], 1, QK), (HC["mem_q_gain_2"], 2, HD)):
            dve.do(nc.vector.tensor_scalar(head_cols[0:dim, c:c + l], head_cols[0:dim, c:c + l], float(dim) ** -0.5, None, ALU.mult))
        stick_attention(core, locals())
        core.fence()

    def gate(dst, c):
        def evacuate(ps, free, ready):
            act.after(ready)
            for j in range(2):
                act.do(nc.scalar.activation(dst[:, 4 * c + 2 * j:4 * c + 2 * j + 2, :],
                                            ps[:, 512 * j:512 * j + 512].rearrange("p (c t) -> p c t", c=2), ACT.Sigmoid), free)
        return evacuate

    for c in range(2):
        run_product(product_turned, X, gate(merged, c))
    for c in range(2):
        def evacuate(ps, free, ready, c=c):
            dve.after(ready, a_free.now(), b_free.now())
            for j in range(2):
                m = merged[:, 4 * c + 2 * j:4 * c + 2 * j + 2, :]
                dve.do(nc.vector.tensor_tensor(m, ps[:, 512 * j:512 * j + 512].rearrange("p (c t) -> p c t", c=2), m, ALU.mult), free)
        run_product(product_turned, Y, evacuate)
    core.fence(act, dve, pool)

    mamba(core, locals())

    with ExitStack() as phase:
        gate_s = core.sb("gate_s", [P, KD, SEQ], ctx=phase)
        for c in range(2):
            run_product(product_turned, X, gate(gate_s, c))
        for c in range(2):
            ps, free = next_bank()
            for h in range(2):
                product_turned(ps, Y, k0=KD * h, first=h == 0, last=h == 1)
                split_ahead()
            dve.after(used.now(), a_free.now(), b_free.now())
            for j in range(2):
                g = gate_s[:, 4 * c + 2 * j:4 * c + 2 * j + 2, :]
                m = merged[:, 4 * c + 2 * j:4 * c + 2 * j + 2, :]
                t = dve.do(nc.vector.tensor_tensor(g, ps[:, 512 * j:512 * j + 512].rearrange("p (c t) -> p c t", c=2), g, ALU.mult), free)
                dve.after(t)
                t = dve.do(nc.vector.tensor_tensor(g, g, m, ALU.add))
                round_split(x_hi[:, 4 * c + 2 * j:4 * c + 2 * j + 2, :], x_lo[:, 4 * c + 2 * j:4 * c + 2 * j + 2, :], g, t)
        core.fence()
    mix.close()

    def add_normed(og, columns, ready):
        dve.after(*ready)
        sums = squares[:, 4:4 + 2 * columns].rearrange("p (m c) -> p m c", m=MT)
        t = dve.do(nc.vector.tensor_reduce(squares[:, 0:2], sums, AX, ALU.add))
        t = mean_rstd(squares[:, 0:2], squares[:, 2:4], D, [t])
        dve.after(t)
        return [[dve.do(nc.vector.scalar_tensor_tensor(out=res[:, m, :], in0=og[:, m, :], scalar=squares[:, 2 + m:3 + m],
                                                       in1=res[:, m, :], op0=ALU.mult, op1=ALU.add))] for m in range(MT)]

    def post_norm(gain_name, act_in):
        with ExitStack() as phase:
            og = core.sb("post_" + gain_name, [P, MT, D], ctx=phase)
            g = core.sb("gain_" + gain_name, [P, D], ctx=phase)
            core.fence(pool)
            gain_in = load(g[:, :], ins[gain_name][0].partition_broadcast(P))
            done = []
            for c in range(2):
                cs = slice(512 * c, 512 * c + 512)

                def evacuate(ps, free, ready):
                    dve.after(gain_in)
                    gain_and_squares([ps[:, 0:512], ps[:, 512:1024]], [og[:, 0, cs], og[:, 1, cs]], g[:, cs],
                                     [squares[:, 4 + c:5 + c], squares[:, 6 + c:7 + c]], ready, free)
                run_product(product_natural, act_in, evacuate)
            t = add_normed(og, 2, [a_free.now(), b_free.now()])
            core.fence(pool)
            return t

    post_norm("g_post_mix", X)

    with ExitStack() as phase:
        kx = core.sb("kx", [P, KD, SEQ], ctx=phase)
        vx = core.sb("vx", [P, MT, D], ctx=phase)
        with ExitStack() as inner:
            mem = core.sb("mem", [P, MT, D], ctx=inner)
            t = load(mem[:, :, :], ins["mem"][0].rearrange("(m p) d -> p m d", p=P))
            rms_turned(mem, Y, col_of["g_mem"], [[t], [t]])
            core.fence()
        for c in range(2):
            run_product(product_turned, Y, copy_out(lambda j: kx[:, 4 * c + 2 * j:4 * c + 2 * j + 2, :]))
        for c in range(2):
            run_product(product_natural, Y, copy_out(lambda j: vx[:, j:j + 1, 512 * c:512 * c + 512]))
        rms_turned(res, X, col_of["g_pre_xa"], [[dve.done.now()], []])
        qx = core.sb("qx", [P, KD, SEQ], ctx=phase)
        for c in range(2):
            run_product(product_turned, X, copy_out(lambda j: qx[:, 4 * c + 2 * j:4 * c + 2 * j + 2, :], XA_DIM ** -0.5))
        cross_attention(core, locals())
        core.fence()
    res_ready = post_norm("g_post_xa", X)

    with ExitStack() as phase:
        rms_turned(res, X, col_of["g_pre_ffn"], res_ready)
        g = core.sb("gain_ffn", [P, D], ctx=phase)
        gain_in = load(g[:, :], ins["g_post_ffn"][0].partition_broadcast(P))
        ffn(core, locals(), None)
        og = core.sb("ffn_out", [P, MT, D], ctx=phase)
        dve.after(gain_in)
        ready = gain_and_squares([psum_c[:, 0:D], psum_c[:, D:2 * D]], [og[:, 0, :], og[:, 1, :]], g[:, :],
                                 [squares[:, 4:5], squares[:, 5:6]], used.now())
        add_normed(og, 1, ready)
        core.fence()

    L2 = ExitStack()
    mk_n = core.sb("mk_n", [P, MT, MEM_W], ctx=L2)
    mv_n = core.sb("mv_n", [P, MT, MEM_W], ctx=L2)
    with ExitStack() as phase:
        mem = core.sb("mem2", [P, MT, D], ctx=phase)
        t = load(mem[:, :, :], ins["mem_2"][0].rearrange("(m p) d -> p m d", p=P))
        rms_turned(mem, Y, col_of["mem_norm_2"], [[t], [t]])
        kv = core.sb("mem_kv", [P, MT, 2 * MEM_W], ctx=phase)
        run_product(product_natural, Y, copy_out(lambda j: kv[:, j:j + 1, :]))
        m_rstd = core.sb("mem_rstd", [P, MT, MEM_HEADS], ctx=phase)
        core.fence(dve)

        def keys(m):
            return split_heads(kv[:, m, 0:MEM_W], HD)
        t = head_rstd(core, dict(psum_c=psum_c, half_neg=half_neg), keys, MEM_HEADS, (HD, HD), m_rstd)
        scale_heads(core, lambda m: split_heads(mk_n[:, m, :], HD), keys, MEM_HEADS, m_rstd, t)
        dve.do(nc.vector.tensor_copy(mv_n[:, :, :], kv[:, :, MEM_W:2 * MEM_W]))
        core.fence()

    for layer in range(2):
        with ExitStack() as phase:
            rms_turned(res, X, col_of["norm_mix_2"] + KD * layer, [[dve.done.now()], []])
            (fox if layer == 0 else mla)(core, locals())
            core.fence()
        for c in range(2):
            def evacuate(ps, free, ready, c=c):
                dve.after(ready)
                for m in range(MT):
                    r = res[:, m, 512 * c:512 * c + 512]
                    dve.do(nc.vector.tensor_tensor(r, ps[:, 512 * m:512 * m + 512], r, ALU.add), free)
            run_product(product_natural, Y, evacuate)
        core.fence()
        with ExitStack() as phase:
            rms_turned(res, X, col_of["norm_ffn_2"] + KD * layer, [[a_free.now(), b_free.now()]] * 2)
            ffn(core, locals(), layer)
            for m in range(MT):
                dve.do(nc.vector.tensor_tensor(res[:, m, :], psum_c[:, 1024 * m:1024 * m + 1024], res[:, m, :], ALU.add))
            core.fence()
    L2.close()

    act.after(dve.done.now())
    stored.mark(nc.scalar.dma_start(out[0].rearrange("(m p) d -> p m d", p=P), res[:, :, :]))
    act.after(stored.now())


def ctx_psum(core, name, shape):
    return core.ctx.enter_context(core.nc.psum_tensor(name, shape, F32))


def stick_attention(core, env):
    nc, pe, act, dve, pool = core.nc, core.pe, core.act, core.dve, core.pool
    q_t, k_t, v_n, phase = env["q_t"], env["k_t"], env["v_n"], env["phase"]
    y_hi, y_lo = env["Y"]
    W = 384
    PAIRS = SB_HEADS // 2
    kq = core.sb("stick_kq", [P, 2, 2, SEQ], ctx=phase)
    vb = core.sb("stick_v", [P, 2, MT, P], ctx=phase)
    L, w = (core.over("stick_" + name, y, KD * SEQ, [P, 2, 2, W]) for name, y in (("l", "y_hi"), ("w", "y_lo")))
    z = [ps[:, 0:1024].rearrange("p (b w) -> p b w", b=2)[:, :, 0:W] for ps in (env["psum_a"], env["psum_c"])]
    core.fence()

    def diagonal(x):
        return x.rearrange("p b (k t) -> p b k t", t=P)[:, :, 0:3:2, :]

    strict = env["strict"][:].unsqueeze(1).unsqueeze(1).to_broadcast([P, 2, 2, P])
    kq_in, v_in, z_made, z_free, l_made, w_made, v_free = (
        [Count(core, f"stick_{name}{u}") for u in range(2)]
        for name in ("kq_in", "v_in", "z_made", "z_free", "l_made", "w_made", "v_free"))
    o_made = Count(core, "stick_o_made")
    o_free = [Count(core, f"stick_o_free{b}") for b in range(2)]

    def stage_kq(j, u):
        pool.after(z_made[u].now())
        pool.do(nc.gpsimd.tensor_copy(kq[:, u, 0, :], k_t[:, bass.ds(j, 1), :].rearrange("p a t -> p (a t)")), kq_in[u])
        pool.do(nc.gpsimd.tensor_copy(kq[:, u, 1, :], q_t[:, bass.ds(j, 1), :].rearrange("p a t -> p (a t)")), kq_in[u])

    def stage_v(j, u):
        pool.after(v_free[u].now())
        for m in range(MT):
            pool.do(nc.gpsimd.tensor_copy(vb[:, u, m, :], v_n[:, m, bass.ds(j * P, P)]), v_in[u])

    def scores(u):
        pe.after(kq_in[u].now(), z_free[u].now())
        for b in range(2):
            r = slice(64 * b, 64 * b + 64)
            nc.tensor.matmul(z[u][:, b, 0:SEQ], kq[r, u, 0, 0:P], kq[r, u, 1, :], start=True, stop=False, skip_group_check=True)
            mm = nc.tensor.matmul(z[u][:, b, SEQ:W], kq[r, u, 0, P:SEQ], kq[r, u, 1, P:SEQ], start=False, stop=False,
                                  skip_group_check=True)
        pe.do(mm, z_made[u])

    def softplus(u):
        dve.after(z_made[u].now())
        t = dve.do(nc.vector.tensor_scalar(L[:, u, :, :], z[u], 30.0, None, ALU.min))
        act.after(t)
        t = act.do(nc.scalar.activation(L[:, u, :, :], L[:, u, :, :], ACT.Exp))
        act.after(t)
        t = act.do(nc.scalar.activation(L[:, u, :, :], L[:, u, :, :], ACT.Ln, bias=1.0))
        dve.after(t)
        t = dve.do(nc.vector.tensor_tensor(L[:, u, :, :], z[u], L[:, u, :, :], ALU.max))
        dve.after(t)
        dve.do(nc.vector.tensor_tensor(diagonal(L[:, u, :, :]), diagonal(L[:, u, :, :]), strict, ALU.mult), l_made[u])

    def weights(u):
        pe.after(l_made[u].now())
        for b in range(2):
            nc.tensor.matmul(z[u][:, b, 0:SEQ], env["neg_from"][:], L[:, u, b, 0:SEQ], start=False, stop=False, skip_group_check=True)
            nc.tensor.matmul(z[u][:, b, P:SEQ], env["neg_ones"][:], L[:, u, b, SEQ:W], start=False, stop=False, skip_group_check=True)
            mm = nc.tensor.matmul(z[u][:, b, SEQ:W], env["neg_from"][:], L[:, u, b, SEQ:W], start=False, stop=True,
                                  skip_group_check=True)
        act.after(pe.do(mm))
        act.do(nc.scalar.activation(w[:, u, :, :], z[u], ACT.Exp), z_free[u])
        dve.after(z_free[u].now())
        for b in range(2):
            d = diagonal(w[:, u, b:b + 1, :])[:, 0, :, :]
            dve.do(nc.vector.scalar_tensor_tensor(out=d, in0=d, scalar=3.0e38, in1=strict[:, 0, :, :], op0=ALU.min, op1=ALU.mult),
                   w_made[u])

    def output(j, u):
        pe.after(w_made[u].now(), v_in[u].now())
        for b in range(2):
            o = env["psum_b"][:, 512 * b:512 * b + SEQ]
            pe.after(o_free[b].now())
            nc.tensor.matmul(o, vb[:, u, 0, :], w[:, u, b, 0:SEQ], start=True, stop=False, skip_group_check=True)
            t = pe.do(nc.tensor.matmul(o[:, P:SEQ], vb[:, u, 1, :], w[:, u, b, SEQ:W], start=False, stop=True,
                                       skip_group_check=True), o_made if b == 0 else v_free[u])
            r = slice(64 * b, 64 * b + 64)
            act.after(t)
            dst = [y[r, bass.ds(j, 1), :].rearrange("p a t -> p (a t)") for y in (y_hi, y_lo)]
            a = act.do(nc.scalar.activation(dst[0], o[r, :], ACT.Copy))
            dve.after(a)
            dve.do(nc.vector.tensor_tensor(dst[1], o[r, :], dst[0].bitcast(F32), ALU.subtract), o_free[b])

    nc.scalar.preload_act_table_set("natural_log_exp_and_others")
    stage_kq(0, 0)
    stage_kq(1, 1)
    stage_v(0, 0)
    for u in range(2):
        scores(u)
        softplus(u)
    weights(0)
    with env["loop"]("stick", PAIRS // 2 - 1) as i:
        for j, u in ((1, 1), (2, 0)):
            stage_kq(i * 2 + (j + 1), 1 - u)
            stage_v(i * 2 + j, u)
            scores(1 - u)
            softplus(1 - u)
            weights(u)
            output(i * 2 + (j - 1), 1 - u)
    stage_v(PAIRS - 1, 1)
    weights(1)
    output(PAIRS - 2, 0)
    output(PAIRS - 1, 1)


def mamba(core, env):
    nc, pe, act, dve, pool = core.nc, core.pe, core.act, core.dve, core.pool
    psum_a, psum_b, psum_c = env["psum_a"], env["psum_b"], env["psum_c"]
    cols, small, bcast, upto, beyond, ident = (env[n] for n in ("cols", "small", "bcast", "upto", "beyond", "ident"))
    a_free, b_free, used, free_c = env["a_free"], env["b_free"], env["used"], Count(core, "c_free")
    X, col_of, run_product, loop = env["X"], env["col_of"], env["run_product"], env["loop"]
    GH, GW = GROUP_HEADS, SSM_INNER // SSM_GROUPS
    with ExitStack() as phase:
        b_t = core.sb("b_t", [P, SSM_GROUPS, SEQ], ctx=phase)
        c_t = core.sb("c_t", [P, SSM_GROUPS, SEQ], ctx=phase)
        y_n = core.sb("y_n", [P, MT, SSM_INNER], ctx=phase)
        dts = core.sb("dts", [P, 5, MT, SSM_HEADS], ctx=phase)
        dt, adt, tmp, eac = (dts[:, j, :, :] for j in range(4))
        to_end = dts[:, 4, 0, :]

        with ExitStack() as inner:
            conv = core.sb("conv", [P, 2, 4, SEQ], ctx=inner)
            nc.scalar.preload_act_table_set("silu_and_others")

            def convolve(u, tile, dst):
                def col(name, tap, j):
                    at = tile + (col_of[name] + tap * (XBC // P) + j)
                    return cols[:, bass.ds(at, 1)]

                def evacuate(ps, free, ready):
                    act.after(ready, pe.done.now(), act.done.now())
                    for j in range(4):
                        t = act.do(nc.scalar.activation(conv[:, u, j, :], ps[:, j * SEQ:(j + 1) * SEQ], ACT.Identity,
                                                        scale=col("conv_w", 3, j), bias=col("conv_b", 0, j)))
                    dve.after(t)
                    for d in (1, 2, 3):
                        for j in range(4):
                            t = dve.do(nc.vector.scalar_tensor_tensor(
                                out=conv[:, u, j, d:], in0=ps[:, j * SEQ:(j + 1) * SEQ - d], scalar=col("conv_w", 3 - d, j),
                                in1=conv[:, u, j, d:], op0=ALU.mult, op1=ALU.add), free if (d, j) == (3, 3) else None)
                        dve.after(t)
                    act.after(t)
                    act.do(nc.scalar.activation(dst, conv[:, u, :, :], ACT.Silu))
                return evacuate

            def turn_back(u, ready, at):
                pe.after(ready, free_c.now())
                for j in range(4):
                    for m in range(MT):
                        mm = nc.tensor.transpose(psum_c[:, 1024 * u + 512 * m + j * P:1024 * u + 512 * m + (j + 1) * P],
                                                 conv[:, u, j, m * P:(m + 1) * P], ident[:])
                t = pe.do(mm)
                dve.after(t)
                act.after(t)
                act.do(nc.scalar.activation(y_n[:, 0, bass.ds(at, GW)], psum_c[:, 1024 * u:1024 * u + 512], ACT.Copy), free_c)
                dve.do(nc.vector.tensor_copy(y_n[:, 1, bass.ds(at, GW)], psum_c[:, 1024 * u + 512:1024 * u + 1024]), free_c)

            with loop("xbc", 2) as i:
                run_product(env["product_turned"], X, convolve(0, i * 8, conv[:, 0, :, :]))
                first = act.done.now()
                run_product(env["product_turned"], X, convolve(1, i * 8 + 4, conv[:, 1, :, :]))
                turn_back(0, first, i * 1024)
                turn_back(1, act.done.now(), i * 1024 + 512)
            act.after(free_c.now())
            dve.after(free_c.now())
            for u, dst in ((0, b_t), (1, c_t)):
                run_product(env["product_turned"], X, convolve(u, 16 + 4 * u, dst[:, :, :]))
            core.fence()

        def evacuate(ps, free, ready):
            nc.scalar.preload_act_table_set("natural_log_exp_and_others")
            act.do(nc.scalar.activation(bcast[:, 1, :], bcast[:, 1, :], ACT.Exp))
            dve.after(ready)
            for m in range(MT):
                t = dve.do(nc.vector.tensor_tensor(dt[:, m, :], ps[:, 512 * m:512 * m + SSM_HEADS], bcast[:, 0, :], ALU.add), free)
            dve.after(t)
            t = dve.do(nc.vector.tensor_scalar(tmp, dt, 30.0, None, ALU.min))
            act.after(t, act.done.now())
            t = act.do(nc.scalar.activation(tmp, tmp, ACT.Exp))
            act.after(t)
            t = act.do(nc.scalar.activation(tmp, tmp, ACT.Ln, bias=1.0))
            dve.after(t)
            t = dve.do(nc.vector.tensor_tensor(dt, dt, tmp, ALU.max))
            dve.after(t)
            for m in range(MT):
                dve.do(nc.vector.scalar_tensor_tensor(out=adt[:, m, :], in0=dt[:, m, :], scalar=-1.0, in1=bcast[:, 1, :],
                                                      op0=ALU.mult, op1=ALU.mult))
        run_product(env["product_natural"], X, evacuate, n=SSM_HEADS)
        pe.after(dve.done.now())
        for c in range(MT):
            nc.tensor.matmul(psum_c[:, 32 * c:32 * c + 32], upto[:], adt[:, c, :], start=c == 0, stop=True, skip_group_check=True)
        t = pe.do(nc.tensor.matmul(psum_c[:, 64:96], beyond[:], adt[:, 0, :], start=False, stop=True, skip_group_check=True))
        act.after(t)
        act.do(nc.scalar.activation(eac, psum_c[:, 0:64].rearrange("p (c h) -> p c h", c=MT), ACT.Exp))
        act.do(nc.scalar.activation(to_end, psum_c[:, 64:96], ACT.Exp))

        with ExitStack() as inner:
            bg = core.sb("bg", [P, 2, SEQ], ctx=inner)
            cg = core.sb("cg", [P, 2, SEQ], ctx=inner)
            b_n = core.sb("b_n", [P, 2, P], ctx=inner)
            cb = core.sb("cb", [P, 2, MT, P], ctx=inner)
            late = core.sb("late", [P, 2, GW], ctx=inner)
            rows = core.over("rows", "y_lo", 0, [P, 2, 4, 4, P])
            xc = core.over("xc", "y_hi", 0, [P, 2, MT, GH, SSM_HD])
            xd = core.over("xd", "y_hi", 2048, [P, 2, GH, SSM_HD])
            state = core.over("state", "y_hi", 3072, [P, 2, GW])
            (bc_in, bc_free, rows_in, own_made, cb_free, x_made, x_kept, seg_free) = (
                [Count(core, f"ssd_{name}{u}") for u in range(2)]
                for name in ("bc_in", "bc_free", "rows_in", "own_made", "cb_free", "x_made", "x_kept", "seg_free"))
            state_free, off_free = Count(core, "ssd_state_free"), Count(core, "ssd_off_free")
            own_free = [Count(core, f"ssd_own_free{c}") for c in range(MT)]
            ps_cb = [psum_a[:, 512 * u:512 * u + 2 * P] for u in range(2)]
            ps_state, ps_off = psum_b[:, 0:GW], psum_b[:, 512:512 + GW]
            ps_own = [psum_c[:, 512 * c:512 * c + 512] for c in range(MT)]
            ps_seg = [psum_c[:, 1024 + 512 * v:1536 + 512 * v] for v in range(2)]
            per_head = [P, MT, GH, SSM_HD]

            def group(x, g, n=GH, h0=0):
                return x[:, :, bass.ds(g * GH + h0, n)]

            def x_of(g):
                return y_n[:, :, bass.ds(g * GW, GW)].rearrange("p c (h d) -> p c h d", d=SSM_HD)

            def prepare(u, g):
                pe.after(bc_in[u].now(), cb_free[u].now())
                for c in range(MT):
                    mm = nc.tensor.matmul(ps_cb[u][:, P * c:P * c + P], bg[:, u, P * c:P * c + P], cg[:, u, P * c:P * c + P],
                                          start=c == 0, stop=True, skip_group_check=True)
                t_cb = pe.do(mm)
                pe.after(state_free.now())
                t = pe.do(nc.tensor.transpose(ps_state[:, 0:P], bg[:, u, 0:P], ident[:]))
                act.after(t)
                t_bn = act.do(nc.scalar.activation(b_n[:, u, :], ps_state[:, 0:P], ACT.Copy))
                dve.after(own_made[u].now())
                t = dve.do(nc.vector.tensor_tensor(xc[:, u, :, :, :], x_of(g), group(dt, g).unsqueeze(3).to_broadcast(per_head), ALU.mult),
                           x_made[u])
                dve.after(t)
                t_xd = dve.do(nc.vector.tensor_tensor(xd[:, u, :, :], xc[:, u, 0, :, :], to_end[:, bass.ds(g * GH, GH)].unsqueeze(2)
                                                      .to_broadcast([P, GH, SSM_HD]), ALU.mult))
                dve.after(t_cb)
                dve.do(nc.vector.tensor_tensor(cb[:, u, :, :], ps_cb[u].rearrange("p (c t) -> p c t", c=MT),
                                               upto[:].unsqueeze(1).to_broadcast([P, MT, P]), ALU.mult), cb_free[u])
                pe.after(t_bn, t_xd)
                t = pe.do(nc.tensor.matmul(ps_state, b_n[:, u, :], xd[:, u, :, :].rearrange("p h d -> p (h d)"), start=True, stop=True))
                act.after(t)
                t = act.do(nc.scalar.activation(state[:, u, :], ps_state, ACT.Copy), state_free)
                pe.after(t, off_free.now())
                t_off = pe.do(nc.tensor.matmul(ps_off, cg[:, u, P:SEQ], state[:, u, :], start=True, stop=True), bc_free[u])
                skip = bcast[:, 2, bass.ds(g * GH, GH)].unsqueeze(1).unsqueeze(3).to_broadcast(per_head)
                t_x = dve.do(nc.vector.tensor_tensor(x_of(g), x_of(g), skip, ALU.mult))
                dve.after(t_off)
                t = dve.do(nc.vector.tensor_tensor(late[:, u, :].rearrange("p (h d) -> p h d", d=SSM_HD),
                                                   ps_off.rearrange("p (h d) -> p h d", d=SSM_HD),
                                                   eac[:, 1, bass.ds(g * GH, GH)].unsqueeze(2).to_broadcast([P, GH, SSM_HD]), ALU.mult),
                           off_free)
                dve.after(t, t_x)
                x_1 = y_n[:, 1, bass.ds(g * GW, GW)]
                dve.do(nc.vector.tensor_tensor(x_1, x_1, late[:, u, :], ALU.add), x_kept[u])

            def decay(u, c, q):
                r, v = rows[:, u, 2 * c + q, :, :], q
                pe.after(rows_in[u].now(), seg_free[v].now())
                t = pe.do(nc.tensor.matmul(ps_seg[v], beyond[:], r.rearrange("p h t -> p (h t)"), start=True, stop=True))
                act.after(t)
                t = act.do(nc.scalar.activation(r, ps_seg[v].rearrange("p (h t) -> p h t", h=4), ACT.Exp), seg_free[v])
                dve.after(t, cb_free[u].now())
                return dve.do(nc.vector.tensor_tensor(r, r, cb[:, u, c, :].unsqueeze(1).to_broadcast([P, 4, P]), ALU.mult))

            def own(u, g, c, q, ready):
                pe.after(ready, own_free[c].now(), x_made[u].now())
                for h in range(4):
                    at = (4 * q + h) * SSM_HD
                    mm = nc.tensor.matmul(ps_own[c][:, at:at + SSM_HD], rows[:, u, 2 * c + q, h, :], xc[:, u, c, 4 * q + h, :],
                                          start=q == 0 and h == 0, stop=True, skip_group_check=True)
                t = pe.do(mm, own_made[u])
                if q == 1:
                    dve.after(t, x_kept[u].now())
                    x_c = y_n[:, c, bass.ds(g * GW, GW)]
                    dve.do(nc.vector.tensor_tensor(x_c, ps_own[c], x_c, ALU.add), own_free[c])

            core.fence()
            with loop("ssd", SSM_GROUPS // 2) as i:
                for u in range(2):
                    pool.after(bc_free[u].now())
                    pool.do(nc.gpsimd.tensor_copy(bg[:, u, :], b_t[:, bass.ds(i * 2 + u, 1), :].rearrange("p a t -> p (a t)")), bc_in[u])
                    pool.do(nc.gpsimd.tensor_copy(cg[:, u, :], c_t[:, bass.ds(i * 2 + u, 1), :].rearrange("p a t -> p (a t)")), bc_in[u])
                for u in range(2):
                    pool.after(own_made[u].now())
                    for c in range(MT):
                        for q in range(2):
                            heads = adt[:, c, bass.ds((i * 2 + u) * GH + 4 * q, 4)].unsqueeze(2).to_broadcast([P, 4, P])
                            pool.do(nc.gpsimd.tensor_tensor(rows[:, u, 2 * c + q, :, :], upto[:].unsqueeze(1).to_broadcast([P, 4, P]),
                                                            heads, ALU.mult), rows_in[u])
                for u in range(2):
                    prepare(u, i * 2 + u)
                steps = [(u, c, q) for u in range(2) for c in range(MT) for q in range(2)]
                ready = decay(*steps[0])
                for this, following in zip(steps, steps[1:] + [None]):
                    following_ready = following and decay(*following)
                    own(this[0], i * 2 + this[0], this[1], this[2], ready)
                    ready = following_ready
            core.fence()

        with ExitStack() as inner:
            gated = core.sb("gated", [P, 2, MT, GW], ctx=inner)
            junk = core.sb("junk_z", [P, GW], ctx=inner)
            turned_y = [Count(core, f"turned_y{u}") for u in range(2)]
            nc.scalar.preload_act_table_set("silu_and_others")

            def gate_norm(u, g):
                def evacuate(ps, free, ready):
                    act.after(ready, turned_y[u].now())
                    t = act.do(nc.scalar.activation(gated[:, u, :, :], ps[:, :].rearrange("p (m n) -> p m n", m=MT), ACT.Silu), free)
                    dve.after(t)
                    t = dve.do(nc.vector.tensor_tensor(gated[:, u, :, :], gated[:, u, :, :], y_n[:, :, bass.ds(g * GW, GW)], ALU.mult))
                    t = env["row_rstd"]([gated[:, u, m, :] for m in range(MT)], GW, 8 * u, [t], junk)
                    for m in range(MT):
                        dve.after(t)
                        dve.do(nc.vector.tensor_scalar(gated[:, u, m, :], gated[:, u, m, :], small[:, 8 * u + 2 + m:8 * u + 3 + m],
                                                       None, ALU.mult))
                return evacuate

            def turn(u, g, ready):
                pe.after(ready, free_c.now())
                for j in range(4):
                    for m in range(MT):
                        mm = nc.tensor.transpose(psum_c[:, 1024 * u + j * SEQ + m * P:1024 * u + j * SEQ + (m + 1) * P],
                                                 gated[:, u, m, j * P:(j + 1) * P], ident[:])
                t = pe.do(mm, turned_y[u])
                for bank in range(2):
                    parts = []
                    for j in (2 * bank, 2 * bank + 1):
                        hi, lo = (y[:, bass.ds(g * 4 + j, 1), :].rearrange("p a t -> p (a t)") for y in env["Y"])
                        parts.append((hi, lo, psum_c[:, 1024 * u + j * SEQ:1024 * u + (j + 1) * SEQ],
                                      cols[:, bass.ds(g * 4 + (j + col_of["g_ssm_norm"]), 1)]))
                    act.after(t)
                    for hi, lo, src, gain in parts:
                        a = act.do(nc.scalar.activation(hi, src, ACT.Copy, scale=gain))
                    dve.after(a)
                    for hi, lo, src, gain in parts:
                        dve.do(nc.vector.scalar_tensor_tensor(out=lo, in0=src, scalar=gain, in1=hi.bitcast(F32),
                                                              op0=ALU.mult, op1=ALU.subtract), free_c)

            with loop("z", 2) as i:
                run_product(env["product_natural"], X, gate_norm(0, i * 2))
                first = dve.done.now()
                run_product(env["product_natural"], X, gate_norm(1, i * 2 + 1))
                turn(0, i * 2, first)
                turn(1, i * 2 + 1, dve.done.now())
            core.fence()


class Softmax:

    def __init__(self, core, env, tag, phase, host=None):
        self.core, self.env = core, env
        self.p, self.pt = (core.sb(tag + name, [P, 2, 512], ctx=phase) if host is None else
                           core.over(tag + name, host, at, [P, 2, 512]) for name, at in (("_prob", 0), ("_prob_t", 1024)))
        self.peak = core.sb(tag + "_peak", [P, 2, MT], ctx=phase)
        self.total = core.sb(tag + "_total", [P, 2, MT], ctx=phase)
        self.o_free = [Count(core, f"{tag}_o_free{b}") for b in range(2)]
        self.exped = [Count(core, f"{tag}_exped{b}") for b in range(2)]

    def scores(self, b):
        return self.env["psum_b"][:, 512 * b:512 * b + 512]

    def probabilities(self, scored, causal, meanwhile=lambda: None):
        core, nc = self.core, self.core.nc
        pe, act, dve = core.pe, core.act, core.dve
        w0 = P if causal else SEQ
        parts = [(0, w0), (w0, w0 + SEQ)]
        exped = []
        for b in range(2):
            sc = self.scores(b)
            dve.after(scored[b])
            if causal:
                d = sc[:, 0:384].rearrange("p (b t) -> p b t", t=P)[:, 0:3:2, :]
                t = dve.do(nc.vector.tensor_tensor(d, d, self.env["causal"][:].unsqueeze(1).to_broadcast([P, 2, P]), ALU.add))
                dve.after(t)
            for m, (lo, hi) in enumerate(parts):
                t = dve.do(nc.vector.tensor_reduce(self.peak[:, b, m:m + 1], sc[:, lo:hi], AX, ALU.max))
            dve.after(t)
            t = dve.do(nc.vector.tensor_scalar(self.peak[:, b, :], self.peak[:, b, :], -1.0, None, ALU.mult))
            act.after(t)
            for m, (lo, hi) in enumerate(parts):
                t = act.do(nc.scalar.activation(self.p[:, b, lo:hi], sc[:, lo:hi], ACT.Exp, bias=self.peak[:, b, m:m + 1],
                                                accum_out=self.total[:, b, m:m + 1]), self.exped[b])
            exped.append(t)
        normed = []
        for b in range(2):
            dve.after(exped[b])
            t = dve.do(nc.vector.reciprocal(self.total[:, b, :], self.total[:, b, :]))
            dve.after(t)
            for m, (lo, hi) in enumerate(parts):
                t = dve.do(nc.vector.tensor_scalar(self.p[:, b, lo:hi], self.p[:, b, lo:hi], self.total[:, b, m:m + 1], None, ALU.mult))
            normed.append(t)
        meanwhile()
        out = []
        order = [0, P, SEQ] if causal else [0, SEQ, P, SEQ + P]
        for b in range(2):
            pe.after(normed[b])
            psum = self.env["psum_c"][:, 512 * b:512 * b + 512]
            for j, at in enumerate(order):
                mm = nc.tensor.transpose(psum[:, j * P:(j + 1) * P], self.p[:, b, at:at + P], self.env["ident"][:])
            t = pe.do(mm)
            act.after(t)
            n = len(order) * P
            out.append(act.do(nc.scalar.activation(self.pt[:, b, 0:n], psum[:, 0:n], ACT.Copy)))
        return out

    def weigh(self, b, at, values, turned, causal):
        nc, pe = self.core.nc, self.core.pe
        o = self.env["psum_c"][:, 1024 + 512 * b + at:1024 + 512 * b + at + SEQ]
        pe.after(turned, self.o_free[b].now())
        nc.tensor.matmul(o, values[0], self.pt[:, b, 0:SEQ], start=at == 0, stop=False, skip_group_check=True)
        if causal:
            mm = nc.tensor.matmul(o[:, P:SEQ], values[1], self.pt[:, b, SEQ:384], start=False, stop=True, skip_group_check=True)
        else:
            mm = nc.tensor.matmul(o, values[1], self.pt[:, b, SEQ:512], start=False, stop=True, skip_group_check=True)
        return o, mm


def cross_attention(core, env):
    nc, pe, act, dve = core.nc, core.pe, core.act, core.dve
    qx, kx, vx = env["qx"], env["kx"], env["vx"]
    x_hi, x_lo = env["X"]
    soft = Softmax(core, env, "xa", env["phase"])
    core.fence()
    nc.scalar.preload_act_table_set("natural_log_exp_and_others")
    for pair in range(XA_HEADS // 2):
        scored = []
        for b in range(2):
            tiles = range(2 * (2 * pair + b), 2 * (2 * pair + b) + 2)
            pe.after(soft.exped[b].now())
            for m in range(MT):
                for kt in tiles:
                    mm = nc.tensor.matmul(soft.scores(b)[:, SEQ * m:SEQ * m + SEQ], qx[:, kt, m * P:(m + 1) * P], kx[:, kt, :],
                                          start=m == 0 and kt == tiles[0], stop=kt == tiles[1], skip_group_check=True)
            scored.append(pe.do(mm))
        turned = soft.probabilities(scored, False)
        for b in range(2):
            for j in range(2):
                kt = 2 * (2 * pair + b) + j
                o, mm = soft.weigh(b, SEQ * j, [vx[:, m, kt * P:(kt + 1) * P] for m in range(MT)], turned[b], False)
            t = pe.do(mm)
            kt = 2 * (2 * pair + b)
            src = env["psum_c"][:, 1024 + 512 * b:1536 + 512 * b].rearrange("p (j t) -> p j t", j=2)
            env["round_split"](x_hi[:, kt:kt + 2, :], x_lo[:, kt:kt + 2, :], src, t, soft.o_free[b])


def ffn(core, env, layer):
    nc, pe, act, dve, pool = core.nc, core.pe, core.act, core.dve, core.pool
    psum_a, psum_b, psum_c, cols, col_of = (env[n] for n in ("psum_a", "psum_b", "psum_c", "cols", "col_of"))
    used, X = env["used"], env["X"]
    phase = env["phase"]
    tag = f"ffn{'' if layer is None else layer + 1}"
    hid = [core.sb(f"{tag}_hidden_{part}", [P, 2, SEQ], F32R, ctx=phase) for part in ("hi", "lo")]
    pre = core.sb(tag + "_pre", [P, 2, 2, SEQ], ctx=phase)
    h32 = core.sb(tag + "_h32", [P, 2, SEQ], ctx=phase)
    zero = core.sb(tag + "_zero", [P, P], F32R, ctx=phase)
    ready = [Count(core, f"{tag}_ready{u}") for u in range(2)]
    free = [Count(core, f"{tag}_free{u}") for u in range(2)]
    core.fence()
    nc.scalar.preload_act_table_set("silu_and_others")
    t = act.do(nc.scalar.activation(zero[:], env["ones"][:], ACT.Copy, scale=0.0))
    pe.after(t)
    for bank in range(4):
        mm = nc.tensor.matmul(psum_c[:, 512 * bank:512 * bank + 512], zero[:], X[0][:, 0:2, :].rearrange("p k t -> p (k t)"),
                              start=True, stop=False, skip_group_check=True)
    pe.do(mm)

    def gate_up(u):
        ps = (psum_a, psum_b)[u][:, 0:512]
        s = env["take_piece"]()
        w = env["weights"](s, KD, SEQ)
        pe.after(free[u].now())
        for k in range(KD):
            for j in range(2):
                mm = env["three"](ps[:, j * SEQ:(j + 1) * SEQ], [x[:, k, j * P:(j + 1) * P] for x in w],
                                  [x[:, k, :] for x in X], k == 0 and j == 0, k == KD - 1)
        pe.do(mm, used)

    def down(u):
        s = env["take_piece"]()
        w = [x[:, 0, :] for x in env["weights"](s, 1, D)]
        pe.after(ready[u].now())
        for m in range(MT):
            for n in range(2):
                mm = env["three"](psum_c[:, D * m + 512 * n:D * m + 512 * n + 512], [x[:, u, m * P:(m + 1) * P] for x in hid],
                                  [x[:, 512 * n:512 * n + 512] for x in w], False, True)
        pe.do(mm, used)

    def hidden(u, h, made):
        ps = (psum_a, psum_b)[u]

        def col(name, tap, j):
            at = col_of[name] + (layer * 6 + tap * 2 + j if name == "ffn_conv_w_2" else layer * 2 + j) * FT + h
            return cols[:, bass.ds(at, 1)]

        act.after(made, ready[u].now())
        if layer is None:
            t = act.do(nc.scalar.activation(pre[:, u, 0, :], ps[:, 0:SEQ], ACT.Silu))
            dve.after(t)
            t = dve.do(nc.vector.tensor_tensor(h32[:, u, :], ps[:, SEQ:2 * SEQ], pre[:, u, 0, :], ALU.mult), free[u])
        else:
            for j in range(2):
                t = act.do(nc.scalar.activation(pre[:, u, j, :], ps[:, j * SEQ:(j + 1) * SEQ], ACT.Identity,
                                                scale=col("ffn_conv_w_2", 2, j), bias=col("ffn_conv_b_2", 0, j)))
            for d in (1, 2):
                dve.after(t)
                for j in range(2):
                    t = dve.do(nc.vector.scalar_tensor_tensor(
                        out=pre[:, u, j, d:], in0=ps[:, j * SEQ:(j + 1) * SEQ - d], scalar=col("ffn_conv_w_2", 2 - d, j),
                        in1=pre[:, u, j, d:], op0=ALU.mult, op1=ALU.add), free[u] if (d, j) == (2, 1) else None)
            act.after(t)
            t = act.do(nc.scalar.activation(pre[:, u, 0, :], pre[:, u, 0, :], ACT.Silu))
            dve.after(t)
            t = dve.do(nc.vector.tensor_tensor(h32[:, u, :], pre[:, u, 0, :], pre[:, u, 1, :], ALU.mult))
        pool.after(t, made)
        t = pool.do(nc.gpsimd.tensor_copy(hid[0][:, u, :], h32[:, u, :]))
        dve.after(t, made)
        dve.do(nc.vector.tensor_tensor(hid[1][:, u, :], h32[:, u, :], hid[0][:, u, :].bitcast(F32), ALU.subtract), ready[u])

    gate_up(0)
    first = used.now()
    env["split_ahead"](1)
    hidden(0, 0, first)
    with env["loop"](tag, (FT - 2) // 2) as i:
        for u in (1, 2):
            gate_up(u % 2)
            made = used.now()
            down((u - 1) % 2)
            env["split_ahead"]()
            hidden(u % 2, i * 2 + u, made)
    gate_up(1)
    made = used.now()
    down(0)
    env["split_ahead"]()
    hidden(1, FT - 1, made)
    down(1)
    env["split_ahead"](1)
    for lane in (act, dve):
        lane.after(used.now())


def head_rstd(core, env, x, heads, dim, rstd, extra=None):
    nc, dve = core.nc, core.dve
    psum_c = env["psum_c"]
    for m in range(MT):
        dve.after(dve.done.now())
        t = dve.do(nc.vector.tensor_tensor(psum_c[:, 0:heads * dim[0]].rearrange("p (h d) -> p h d", h=heads), x(m), x(m), ALU.mult))
        dve.after(t)
        t = dve.do(nc.vector.tensor_reduce(rstd[:, m, :], psum_c[:, 0:heads * dim[0]].rearrange("p (h d) -> p h d", h=heads), AX, ALU.add))
        if extra is not None:
            dve.after(t)
            t = dve.do(nc.vector.tensor_scalar(rstd[:, m, :], rstd[:, m, :], extra[:, m:m + 1], None, ALU.add))
    dve.after(t)
    t = dve.do(nc.vector.tensor_scalar(rstd[:, :, :], rstd[:, :, :], 1.0 / dim[1], EPS, ALU.mult, ALU.add))
    core.pool.after(t)
    return core.pool.do(nc.gpsimd.tensor_tensor(rstd[:, :, :], rstd[:, :, :], env["half_neg"][:, 0:MT * heads]
                                                .rearrange("p (m h) -> p m h", m=MT), ALU.pow))


def scale_heads(core, dst, x, heads, rstd, ready):
    core.dve.after(ready)
    for m in range(MT):
        t = core.dve.do(core.nc.vector.tensor_tensor(dst(m), x(m), rstd[:, m, :].unsqueeze(2).to_broadcast(list(x(m).shape)), ALU.mult))
    return t


class HeadPairs:

    def __init__(self, core, env, tag, dk, phase):
        self.core, self.env, self.dk = core, env, dk
        self.qh = core.sb(tag + "_qh", [P, 2, MT, dk], ctx=phase)
        self.kh = core.sb(tag + "_kh", [P, 2, MT, dk], ctx=phase)
        self.vh = core.sb(tag + "_vh", [P, MT, P], ctx=phase)
        self.qt = core.sb(tag + "_qt", [P, 2, SEQ], ctx=phase)
        self.kt = core.sb(tag + "_kt", [P, 2, SEQ], ctx=phase)
        self.soft = Softmax(core, env, tag, phase, "x_lo")
        self.built = [Count(core, f"{tag}_built{b}") for b in range(2)]
        self.turned = [Count(core, f"{tag}_turned{b}") for b in range(2)]
        self.qk_in = [Count(core, f"{tag}_qk_in{b}") for b in range(2)]
        self.weighed = Count(core, tag + "_weighed")

    def first(self, pair):
        build, _, gains, dk, _, _ = pair
        for b in range(2):
            self.core.pool.after(self.turned[b].now())
            build(b, self.qh[:, b, :, :], self.kh[:, b, :, :], self.built[b])
        self.turn(gains, dk)

    def turn(self, gains, dk):
        core, nc, env = self.core, self.core.nc, self.env
        pe = core.pe
        for b in range(2):
            ps = env["psum_a"][0:dk, 512 * b:512 * b + 512]
            pe.after(self.built[b].now(), self.qk_in[b].now())
            for j, x in enumerate((self.qh, self.kh)):
                for m in range(MT):
                    mm = nc.tensor.transpose(ps[:, (2 * j + m) * P:(2 * j + m + 1) * P], x[:, b, m, 0:dk], env["ident"][:])
            t = pe.do(mm, self.turned[b])
            lane = (core.act, core.dve)[b]
            lane.after(t)
            for x, at, g in ((self.qt, 0, gains[0]), (self.kt, SEQ, gains[1])):
                gain = env["head_cols"][0:dk, g:g + 1]
                if b == 0:
                    lane.do(nc.scalar.activation(x[0:dk, b, :], ps[:, at:at + SEQ], ACT.Copy, scale=gain), self.qk_in[b])
                else:
                    lane.do(nc.vector.tensor_scalar(x[0:dk, b, :], ps[:, at:at + SEQ], gain, None, ALU.mult), self.qk_in[b])

    def step(self, pair, following):
        core, nc, env = self.core, self.core.nc, self.env
        pe, pool = core.pe, core.pool
        _, build_v, _, dk, causal, tile = pair
        if following:
            for b in range(2):
                pool.after(self.turned[b].now())
                following[0](b, self.qh[:, b, :, :], self.kh[:, b, :, :], self.built[b])
        pool.after(self.weighed.now())
        build_v(self.vh)
        v_in = pool.done.now()
        scored = []
        w0 = P if causal else SEQ
        for b in range(2):
            pe.after(self.qk_in[b].now(), self.soft.exped[b].now())
            sc = self.soft.scores(b)
            nc.tensor.matmul(sc[:, 0:w0], self.qt[0:dk, b, 0:P], self.kt[0:dk, b, 0:w0], start=True, stop=True, skip_group_check=True)
            scored.append(pe.do(nc.tensor.matmul(sc[:, w0:w0 + SEQ], self.qt[0:dk, b, P:SEQ], self.kt[0:dk, b, :],
                                                 start=False, stop=True, skip_group_check=True)))
        turned = self.soft.probabilities(scored, causal, lambda: following and self.turn(following[2], following[3]))
        pe.after(v_in)
        for b in range(2):
            o, mm = self.soft.weigh(b, 0, [self.vh[:, m, :] for m in range(MT)], turned[b], causal)
            t = pe.do(mm, self.weighed)
            r = slice(64 * b, 64 * b + 64)
            hi, lo = (y[r, bass.ds(tile, 1), :].rearrange("p a t -> p (a t)") for y in env["Y"])
            env["round_split"](hi, lo, o[r, :], t, self.soft.o_free[b])

    def run_all(self, name, n, pair, rest):
        self.first(pair(0))
        with self.env["loop"](name, n - 1) as i:
            self.step(pair(i), pair(i + 1))
        for this, following in zip([pair(n - 1)] + rest, rest + [None]):
            self.step(this, following)


def split_heads(x, d):
    return x.rearrange("p (h d) -> p h d", d=d)


def natural_units(core, env, dst, widths):
    nc, act, dve = core.nc, core.act, core.dve
    at = 0
    for n in widths:
        def evacuate(ps, free, ready, at=at, n=n):
            act.after(ready)
            dve.after(ready)
            act.do(nc.scalar.activation(dst[:, 0, at:at + n], ps[:, 0:n], ACT.Copy), free)
            dve.do(nc.vector.tensor_copy(dst[:, 1, at:at + n], ps[:, 512:512 + n]), free)
        env["run_product"](env["product_natural"], env["X"], evacuate, n=n)
        at += n
    dve.after(env["a_free"].now(), env["b_free"].now())


def copies(core, by, *pairs):
    for dst, src in pairs:
        core.pool.do(core.nc.gpsimd.tensor_copy(dst, src), by)


def memory_pairs(core, env, q, layer):
    HC = env["HC"]

    def pair(i):
        def build(b, qh, kh, by):
            at = (2 * i + b) * HD
            copies(core, by, (qh[:, :, 0:HD], q[:, :, at:at + HD]), (kh[:, :, 0:HD], env["mk_n"][:, :, at:at + HD]))

        def build_v(vh):
            copies(core, None, (vh[:, :, :], env["mv_n"][:, :, i * P:(i + 1) * P]))
        return build, build_v, (HC["mem_q_gain_2"] + layer, HC["mem_k_gain_2"] + layer), HD, False, HEADS // 2 + i
    return [pair(i) for i in range(MEM_HEADS // 2)]


def fox(core, env):
    nc, pe, act, dve, pool = core.nc, core.pe, core.act, core.dve, core.pool
    phase, psum_c, bcast = env["phase"], env["psum_c"], env["bcast"]
    DK = HD + 2
    fp = core.sb("fox_p", [P, MT, FOX_IN], ctx=phase)
    rstd = core.sb("fox_rstd", [P, MT, 2 * HEADS], ctx=phase)
    mrstd = core.sb("fox_mem_rstd", [P, MT, MEM_HEADS], ctx=phase)
    cum = core.sb("fox_cum", [P, 3, MT, HEADS], ctx=phase)
    logf, pos, neg = (cum[:, j, :, :] for j in range(3))
    pairs = HeadPairs(core, env, "fox", DK, phase)
    core.fence()
    natural_units(core, env, fp, [512] * 5 + [FOX_IN - 2560])
    core.fence()
    q_at = MIX * 3 + HEADS

    def qk(m):
        return split_heads(fp[:, m, 0:2 * MIX], HD)

    def mq(m):
        return split_heads(fp[:, m, q_at:q_at + MEM_W], HD)
    scale_heads(core, qk, qk, 2 * HEADS, rstd, head_rstd(core, env, qk, 2 * HEADS, (HD, HD), rstd))
    scale_heads(core, mq, mq, MEM_HEADS, mrstd, head_rstd(core, env, mq, MEM_HEADS, (HD, HD), mrstd))
    nc.scalar.preload_act_table_set("natural_log_exp_and_others")
    for m in range(MT):
        t = dve.do(nc.vector.scalar_tensor_tensor(out=logf[:, m, :], in0=fp[:, m, 3 * MIX:3 * MIX + HEADS], scalar=-1.0,
                                                  in1=bcast[:, 3, 0:HEADS], op0=ALU.mult, op1=ALU.subtract))
    dve.after(t)
    t = dve.do(nc.vector.tensor_scalar(pos, logf, 30.0, None, ALU.min))
    act.after(t)
    t = act.do(nc.scalar.activation(pos, pos, ACT.Exp))
    act.after(t)
    t = act.do(nc.scalar.activation(pos, pos, ACT.Ln, bias=1.0))
    dve.after(t)
    t = dve.do(nc.vector.tensor_tensor(logf, logf, pos, ALU.max))
    pe.after(t)
    nc.tensor.matmul(psum_c[:, 0:HEADS], env["upto"][:], logf[:, 0, :], start=True, stop=True, skip_group_check=True)
    nc.tensor.matmul(psum_c[:, 32:32 + HEADS], env["ones"][:], logf[:, 0, :], start=False, stop=False, skip_group_check=True)
    t = pe.do(nc.tensor.matmul(psum_c[:, 32:32 + HEADS], env["upto"][:], logf[:, 1, :], start=False, stop=True, skip_group_check=True))
    dve.after(t)
    sums = psum_c[:, 0:64].rearrange("p (m h) -> p m h", m=MT)[:, :, 0:HEADS]
    dve.do(nc.vector.tensor_copy(neg, sums))
    dve.do(nc.vector.tensor_scalar(pos, sums, -1.0, None, ALU.mult))
    pool.do(nc.gpsimd.memset(pairs.qh[:, :, :, :], 1.0))
    pool.do(nc.gpsimd.memset(pairs.kh[:, :, :, :], 1.0))
    core.fence()

    def pair(i):
        def build(b, qh, kh, by):
            at, head = i * P + HD * b, i * 2 + b
            copies(core, by, (qh[:, :, 0:HD], fp[:, :, bass.ds(at, HD)]), (qh[:, :, HD:HD + 1], pos[:, :, bass.ds(head, 1)]),
                   (kh[:, :, 0:HD], fp[:, :, bass.ds(at + MIX, HD)]), (kh[:, :, HD + 1:HD + 2], neg[:, :, bass.ds(head, 1)]))

        def build_v(vh):
            copies(core, None, (vh[:, :, :], fp[:, :, bass.ds(i * P + 2 * MIX, P)]))
        return build, build_v, (env["HC"]["fox_q_gain_2"], env["HC"]["fox_k_gain_2"]), DK, True, i
    pairs.run_all("fox", HEADS // 2, pair, memory_pairs(core, env, fp[:, :, q_at:q_at + MEM_W], 0))


def mla(core, env):
    nc, pe, act, dve, pool = core.nc, core.pe, core.act, core.dve, core.pool
    phase, psum_a, psum_b, psum_c = env["phase"], env["psum_a"], env["psum_b"], env["psum_c"]
    col_of, Y, used = env["col_of"], env["Y"], env["used"]
    lp = core.sb("mla_p", [P, MT, MLA_IN], ctx=phase)
    q_n = core.sb("mla_q", [P, MT, HEADS * QK], ctx=phase)
    kv_n = core.sb("mla_kv", [P, MT, HEADS * 2 * HD], ctx=phase)
    core.fence()
    natural_units(core, env, lp, [512, MLA_IN - 512])
    core.fence()
    k_r = lp[:, :, Q_RANK + KV_RANK:Q_RANK + KV_RANK + ROPE]
    mem_q = lp[:, :, MLA_IN - MEM_W:MLA_IN]
    for slot, at, n in ((0, 0, Q_RANK), (8, Q_RANK, KV_RANK)):
        t = env["row_rstd"]([lp[:, m, at:at + n] for m in range(MT)], n, slot, [dve.done.now()], q_n[:, 0, :])
        for m in range(MT):
            dve.after(t)
            t = dve.do(nc.vector.tensor_scalar(lp[:, m, at:at + n], lp[:, m, at:at + n], env["small"][:, slot + 2 + m:slot + 3 + m], None, ALU.mult))
    env["turn_and_split"](lp[:, :, 0:Q_RANK], Y, 2, col_of["mla_qa_norm_2"], t)
    t = env["turn_and_split"](lp[:, :, Q_RANK:Q_RANK + KV_RANK], Y, 1, col_of["mla_kva_norm_2"], t, k_to=2)
    pe.after(t)
    core.fence()

    def up(ps, stride, kt, k0, n):
        s = env["take_piece"]()
        w = env["weights"](s, kt, n)
        for k in range(kt):
            for m in range(MT):
                for c in range(0, n, 512):
                    wd = min(512, n - c)
                    mm = env["three"](ps[:, m * stride + c:m * stride + c + wd], [y[:, k0 + k, m * P:(m + 1) * P] for y in Y],
                                      [x[:, k, c:c + wd] for x in w], k == 0, k == kt - 1)
        return pe.do(mm, used)

    def evict(dst, ps, stride, n, ready):
        act.after(ready)
        dve.after(ready)
        a = act.do(nc.scalar.activation(dst(0), ps[:, 0:n], ACT.Copy))
        v = dve.do(nc.vector.tensor_copy(dst(1), ps[:, stride:stride + n]))
        return [a, v]

    for dst, kt, k0, rest, ps in ((q_n, 2, 0, HEADS * QK - 1024, psum_a), (kv_n, 1, 2, 512, psum_b)):
        t1 = up(psum_c, 1024, kt, k0, 1024)
        t2 = up(ps, 512, kt, k0, rest)
        env["split_ahead"]()
        t = evict(lambda m: dst[:, m, 0:1024], psum_c, 1024, 1024, t1)
        pe.after(*t)
        evict(lambda m: dst[:, m, 1024:1024 + rest], ps, 512, rest, t2)
    core.fence()

    rotary = ExitStack()
    rot = core.sb("mla_rot", [P, 6, MT, 16], ctx=rotary)
    ang, cos, sin, kk, red, posf = (rot[:, j, :, :] for j in range(6))
    TWO_PI = (6.28125, 0.0019350051879882812, 3.0199159819e-07)
    MAGIC = 12582912.0
    t = dve.do(nc.vector.tensor_copy(posf[:, :, 0:1], env["pos_i"][:].unsqueeze(2)))
    for m in range(MT):
        dve.after(t)
        t = dve.do(nc.vector.tensor_scalar(ang[:, m, :], env["inv_freq"][:], posf[:, m, 0:1], None, ALU.mult))
    nc.scalar.preload_act_table_set("silu_and_others")
    for dst, quarter in ((sin, 0.0), (cos, 0.25)):
        def step(ins):
            dve.after(dve.do(ins))
        dve.after(dve.done.now(), act.done.now())
        step(nc.vector.tensor_scalar(kk, ang, 1.0 / (2.0 * math.pi), quarter, ALU.mult, ALU.add))
        step(nc.vector.tensor_scalar(kk, kk, MAGIC, None, ALU.add))
        step(nc.vector.tensor_scalar(kk, kk, MAGIC, None, ALU.subtract))
        src = ang
        for part in TWO_PI:
            for m in range(MT):
                nc_ins = nc.vector.scalar_tensor_tensor(out=red[:, m, :], in0=kk[:, m, :], scalar=-part, in1=src[:, m, :],
                                                        op0=ALU.mult, op1=ALU.add)
                step(nc_ins)
            src = red
        step(nc.vector.tensor_scalar(red, red, quarter * 2.0 * math.pi, None, ALU.add))
        step(nc.vector.tensor_scalar(red, red, 3.1415925, -3.1415925, ALU.min, ALU.max))
        act.after(dve.done.now())
        act.do(nc.scalar.activation(dst, red, ACT.Sin))
    dve.after(act.done.now())

    def rope(x, heads):
        for m in range(MT):
            x1, x2 = x(m)[:, :, 0:16], x(m)[:, :, 16:32]
            c, s = (f[:, m, :].unsqueeze(1).to_broadcast([P, heads, 16]) for f in (cos, sin))
            tmp = [psum_c[:, 512 * j:512 * j + heads * 16].rearrange("p (h d) -> p h d", h=heads) for j in range(4)]
            sb_tmp = [core_tmp[:, j, 0:heads * 16].rearrange("p (h d) -> p h d", h=heads) for j in range(2)]
            dve.after(dve.done.now())
            dve.do(nc.vector.tensor_tensor(tmp[0], x1, c, ALU.mult))
            dve.do(nc.vector.tensor_tensor(sb_tmp[0], x2, s, ALU.mult))
            dve.do(nc.vector.tensor_tensor(tmp[1], x1, s, ALU.mult))
            t = dve.do(nc.vector.tensor_tensor(sb_tmp[1], x2, c, ALU.mult))
            dve.after(t)
            dve.do(nc.vector.tensor_tensor(x1, tmp[0], sb_tmp[0], ALU.subtract))
            dve.do(nc.vector.tensor_tensor(x2, tmp[1], sb_tmp[1], ALU.add))

    core_tmp = core.sb("mla_tmp", [P, 2, HEADS * 16], ctx=rotary)
    rope(lambda m: split_heads(q_n[:, m, :], QK)[:, :, HD:QK], HEADS)
    rope(lambda m: k_r[:, m, :].unsqueeze(1), 1)
    rotary.close()
    core.fence()

    rstd = core.sb("mla_rstd", [P, 3, MT, HEADS], ctx=phase)
    mrstd = core.sb("mla_mem_rstd", [P, MT, MEM_HEADS], ctx=phase)
    extra = core.sb("mla_extra", [P, MT], ctx=phase)
    dve.after(dve.done.now())
    for m in range(MT):
        dve.after(dve.done.now())
        dve.do(nc.vector.tensor_tensor(psum_c[:, 0:ROPE], k_r[:, m, :], k_r[:, m, :], ALU.mult))
        dve.after(dve.done.now())
        dve.do(nc.vector.tensor_reduce(extra[:, m:m + 1], psum_c[:, 0:ROPE], AX, ALU.add))

    def q(m):
        return split_heads(q_n[:, m, :], QK)

    def k(m):
        return split_heads(kv_n[:, m, :], 2 * HD)[:, :, 0:HD]

    def mq(m):
        return split_heads(mem_q[:, m, :], HD)
    scale_heads(core, q, q, HEADS, rstd[:, 0, :, :], head_rstd(core, env, q, HEADS, (QK, QK), rstd[:, 0, :, :]))
    t_k = head_rstd(core, env, k, HEADS, (HD, QK), rstd[:, 1, :, :], extra)
    scale_heads(core, k, k, HEADS, rstd[:, 1, :, :], t_k)
    scale_heads(core, mq, mq, MEM_HEADS, mrstd, head_rstd(core, env, mq, MEM_HEADS, (HD, HD), mrstd))
    pairs = HeadPairs(core, env, "mla", QK, phase)
    core.fence()
    nc.scalar.preload_act_table_set("natural_log_exp_and_others")

    def pair(i):
        def build(b, qh, kh, by):
            copies(core, by, (qh[:, :, 0:QK], q_n[:, :, bass.ds(i * (2 * QK) + QK * b, QK)]),
                   (kh[:, :, 0:HD], kv_n[:, :, bass.ds(i * (4 * HD) + 2 * HD * b, HD)]))
            pool.do(nc.gpsimd.tensor_tensor(kh[:, :, HD:QK], k_r, rstd[:, 1, :, bass.ds(i * 2 + b, 1)].to_broadcast([P, MT, ROPE]),
                                            ALU.mult), by)

        def build_v(vh):
            copies(core, None, *((vh[:, :, HD * b:HD * b + HD], kv_n[:, :, bass.ds(i * (4 * HD) + (2 * HD * b + HD), HD)])
                                 for b in range(2)))
        return build, build_v, (env["HC"]["mla_q_gain_2"], env["HC"]["mla_k_gain_2"]), QK, True, i
    pairs.run_all("mla", HEADS // 2, pair, memory_pairs(core, env, mem_q, 1))


_OUTS = [((1, SEQ, D), "float32")]


def kernel(**inputs):
    import numpy as _np
    import concourse.bacc as _bacc
    from concourse.bass_utils import run_bass_kernel_spmd as _run

    def build(strides):
        nc = _bacc.Bacc("TRN2", target_bir_lowering=False, num_devices=1)
        arrays, ins = {}, {}
        for name, value in inputs.items():
            a = _np.ascontiguousarray(value)
            if a.size == 0:
                continue
            arrays[f"in_{name}_dram"] = a
            ins[name] = nc.dram_tensor(f"in_{name}_dram", a.shape, mybir.dt.from_np(a.dtype), kind="ExternalInput").ap()
        out = nc.dram_tensor("out_0_dram", _OUTS[0][0], F32, kind="ExternalOutput").ap()
        return nc, arrays, emit(nc, ins, out, strides)

    _, _, strides = build({})
    nc, arrays, again = build(strides)
    assert again == strides
    r = _run(nc, [arrays], core_ids=[0])
    return r.results[0]["out_0_dram"]
```

```python
from contextlib import ExitStack, contextmanager
import math

import concourse.bass as bass
from concourse import mybir

F32 = mybir.dt.float32
F32R = mybir.dt.float32r
I32 = mybir.dt.int32
ALU = mybir.AluOpType
ACT = mybir.ActivationFunctionType
AX = mybir.AxisListType.X
ENG = mybir.EngineType

P = 128
SEQ = 256
MT = SEQ // P
D = 1024
KD = D // P
EPS = 1e-6
SLOTS = 4
PIECE = 2048
NEG = -1.0e30

SB_HEADS, SB_DIM = 16, 64
SSM_INNER, SSM_HEADS, SSM_HD, SSM_GROUPS, SSM_STATE = 2048, 32, 64, 4, 128
XBC = SSM_INNER + 2 * SSM_GROUPS * SSM_STATE
GROUP_HEADS = SSM_HEADS // SSM_GROUPS
XA_HEADS, XA_DIM = 4, 256
FFN = 2816
FT = FFN // P
C_Q, C_K, C_V, C_Z = 0, D, 2 * D, 3 * D
C_XBC = C_Z + SSM_INNER
C_DT = C_XBC + XBC
C_GA = C_DT + SSM_HEADS
C_GS = C_GA + D

HEADS, HD = 12, 64
MIX = HEADS * HD
MEM_HEADS = 4
MEM_W = MEM_HEADS * HD
FOX_IN = 3 * MIX + HEADS + MEM_W
FOX_UNITS = [(0, 512), (512, 512), (1024, 512), (2048, 512), (1536, 512), (2560, FOX_IN - 2560)]
Q_RANK, KV_RANK, ROPE = 256, 128, 32
QK = HD + ROPE
MLA_IN = Q_RANK + KV_RANK + ROPE + MEM_W


class Count:

    def __init__(self, core, name, unit=1):
        self.name, self.unit = name, unit
        self.sem = core.ctx.enter_context(core.nc.semaphore(name))
        self.base, self.k, self.least = 0, 0, 0
        core.counts.append(self)

    def value(self):
        return self.base + self.k

    def mark(self, ins, units=1):
        ins.then_inc(self.sem, self.unit * units)
        self.k += units
        return self.now()

    def now(self, ahead=0):
        return (self, self.base, self.k + ahead)


class Lane:

    def __init__(self, core, engine, name):
        self.e = engine
        self.done = Count(core, name + "_done")
        self.seen = {}
        self.gate = core.ctx.enter_context(core.nc.semaphore(name + "_gate")) if name == "pool" else None

    def after(self, *tokens):
        computed = False
        for count, base, k in tokens:
            if isinstance(base, int) and base + k <= 0:
                continue
            key = (count.name, base if isinstance(base, int) else id(base))
            if self.seen.get(key, -1 << 30) >= k:
                continue
            self.seen[key] = k
            self.e.wait_ge(count.sem, (base + k) * count.unit)
            if not isinstance(base, int):
                assert count.least + k > 0, count.name
                computed = True
        if computed and self.gate is not None:
            self.e.sem_inc(self.gate)
        return self

    def do(self, ins, by=None):
        return (by or self.done).mark(ins)


class Core:
    def __init__(self, nc, ctx, strides):
        self.nc, self.ctx, self.strides, self.new_strides, self.counts = nc, ctx, strides, {}, []
        self.pe = Lane(self, nc.tensor, "pe")
        self.act = Lane(self, nc.scalar, "act")
        self.dve = Lane(self, nc.vector, "dve")
        self.pool = Lane(self, nc.gpsimd, "pool")
        self.lanes = [self.pe, self.act, self.dve, self.pool]
        self.piece = 0
        self.address = {}

    def sb(self, name, shape, dt=F32, ctx=None):
        tensor = (ctx or self.ctx).enter_context(self.nc.sbuf_tensor(name, shape, dt))
        self.address[name] = self.nc.sbuf_base - 4 * math.prod(shape[1:])
        return tensor

    def over(self, name, host, skip, shape):
        return self.nc.alloc_sbuf_tensor_at(name, shape, F32, offset=self.address[host] + 4 * skip)

    def forget(self):
        for lane in self.lanes:
            lane.seen = {}

    def start_at_one(self, name):
        for c in self.counts:
            if c.k == 0 and isinstance(c.base, int) and c.base == 0 and self.strides.get(name, {}).get(c.name):
                self.nc.vector.sem_inc(c.sem, c.unit)
                c.k = 1

    @contextmanager
    def loop(self, name, n):
        self.start_at_one(name)
        stride = self.strides.get(name, {})
        starts = {c.name: (c.base + c.k) for c in self.counts}
        piece = self.piece
        self.forget()
        with self.nc.Fori(0, n, engines=[ENG.PE, ENG.Activation, ENG.DVE, ENG.Pool]) as i:
            for c in self.counts:
                d = stride.get(c.name, 0)
                c.base, c.k = (i * d + starts[c.name] if d else starts[c.name]), 0
                c.least = starts[c.name]
            yield i
        self.new_strides[name] = {c.name: c.k for c in self.counts if c.k}
        for c in self.counts:
            c.base, c.k = starts[c.name] + n * c.k, 0
        self.piece = piece + n * (self.piece - piece)
        self.forget()

    def fence(self, *lanes):
        for lane in lanes or self.lanes:
            lane.after(*[c.now() for c in self.counts if c.unit == 1])


def emit(nc, ins, out, strides):
    with ExitStack() as ctx:
        core = Core(nc, ctx, strides)
        program(core, ins, out)
        return core.new_strides


def program(core, ins, out):
    nc, pe, act, dve, pool = core.nc, core.pe, core.act, core.dve, core.pool
    sp = nc.sync
    sb = core.sb

    def count(name, unit=1):
        return Count(core, name, unit)

    raw = sb("raw", [P, SLOTS, PIECE])
    w_hi = sb("w_hi", [P, SLOTS, PIECE], F32R)
    w_lo = sb("w_lo", [P, SLOTS, PIECE], F32R)
    x_hi = sb("x_hi", [P, KD, SEQ], F32R)
    x_lo = sb("x_lo", [P, KD, SEQ], F32R)
    y_hi = sb("y_hi", [P, 2 * KD, SEQ], F32R)
    y_lo = sb("y_lo", [P, 2 * KD, SEQ], F32R)
    res = sb("res", [P, MT, D])
    ident = sb("ident", [P, P])
    ones = sb("ones", [P, P])
    upto = sb("upto", [P, P])
    beyond = sb("beyond", [P, P])
    neg_from = sb("neg_from", [P, P])
    neg_ones = sb("neg_ones", [P, P])
    strict = sb("strict", [P, P])
    causal = sb("causal", [P, P])
    half_neg = sb("half_neg", [P, 64])
    cols = sb("cols", [P, 5 * P])
    small = sb("small", [P, 16])
    psum_a = ctx_psum(core, "psum_a", [P, 1024])
    psum_b = ctx_psum(core, "psum_b", [P, 1024])
    psum_c = ctx_psum(core, "psum_c", [P, 2048])

    arrived = [count(f"arrived{s}", 16) for s in range(SLOTS)]
    rounded = count("rounded")
    split = count("split")
    used = count("used")
    a_free = count("a_free")
    b_free = count("b_free")
    loaded = count("loaded", 16)
    stored = count("stored", 16)
    rows_loaded = count("rows_loaded", 16)

    w_in = ins["w_in"][0].rearrange("(k p) n -> p k n", p=P)

    def block(w, k0, nk, col, n):
        view = w.rearrange("(k p) n -> p k n", p=P)
        return [(0, nk, n, view[:, k0:k0 + nk, bass.ds(col, n)])]

    def gate_up(w, h):
        view = w.rearrange("(k p) n -> p k n", p=P)
        return [(j * P, KD, 2 * P, view[:, :, bass.ds(h * P + j * FFN, P)]) for j in range(2)]

    def down(w, h):
        view = w.rearrange("(k p) n -> k p n", p=P)
        return [(0, 1, D, view[bass.ds(h, 1), :, :].rearrange("k p n -> p k n"))]

    def halves(w, col, n=512, k0=0):
        return [block(w, k0, 4, col, n), block(w, k0 + 4, 4, col, n)]

    def square(w, col=0):
        return [q for c in range(2) for q in halves(w, col + 512 * c)]

    def rows_first(w):
        return [block(w, k0, 4, col, 512) for k0 in (0, 4) for col in (0, 512)]

    W = {k: v[0] for k, v in ins.items() if len(v.shape) == 3 and k.startswith(("w_", "fox_w", "mla_w"))}
    win = W["w_in"]

    def ffn_entries(gu, dn):
        return [("once", [gate_up(gu, 0)]),
                ("loop", (FT - 2) // 2, lambda i: [q for u in (1, 2) for q in (
                    gate_up(gu, i * 2 + u), down(dn, i * 2 + (u - 1)))]),
                ("once", [gate_up(gu, FT - 1), down(dn, FT - 2), down(dn, FT - 1)])]

    wo2 = ins["w_out_2"]
    plan = [("once", square(win, C_Q) + square(win, C_K) + square(win, C_V)),
            ("once", square(win, C_GA) + square(W["w_br_att"])),
            ("once", halves(win, C_DT, SSM_HEADS) + square(win, C_XBC + SSM_INNER)),
            ("once", square(win, C_XBC) + square(win, C_XBC + 1024) + square(win, C_Z) + square(win, C_Z + 1024)),
            ("once", square(win, C_GS) + [q for c in range(2) for k0 in (0, KD) for q in halves(W["w_br_ssm"], 512 * c, k0=k0)]),
            ("once", square(W["w_mix_out"])),
            ("once", square(W["w_xkv"]) + square(W["w_xkv"], D) + square(W["w_xq"]) + square(W["w_xo"])),
            ("once", halves(ins["w_mem_kv_2"], 0)),
            *ffn_entries(W["w_gu"], W["w_down"]),
            ("once", [q for at, n in FOX_UNITS for q in halves(W["fox_w_in_2"], at, n)]),
            ("once", rows_first(wo2[0])),
            *ffn_entries(ins["ffn_w_up_2"][0], ins["ffn_w_down_2"][0]),
            ("once", halves(W["mla_w_in_2"], 0) + halves(W["mla_w_in_2"], 512, MLA_IN - 512)),
            ("once", [block(W["mla_w_q_up_2"], 0, 2, 0, 1024), block(W["mla_w_q_up_2"], 0, 2, 1024, HEADS * QK - 1024),
                      block(W["mla_w_kv_up_2"], 0, 1, 0, 1024), block(W["mla_w_kv_up_2"], 0, 1, 1024, 512)]),
            ("once", rows_first(wo2[1])),
            *ffn_entries(ins["ffn_w_up_2"][1], ins["ffn_w_down_2"][1])]
    shapes = []
    for kind, *rest in plan:
        for q in (rest[0] if kind == "once" else rest[1](0) * rest[0]):
            shapes.append((q[0][1] * q[0][2], len(q)))

    def weight_stream():
        at = 0

        def load(pieces, at0, step):
            for j, parts in enumerate(pieces):
                s = (at0 + j) % SLOTS
                need = step + (at0 + j - SLOTS + 1)
                if not isinstance(need, int) or need > 0:
                    sp.wait_ge(split.sem, need)
                for off, nk, n, src in parts:
                    dst = raw[:, s, 0:nk * n].rearrange("p (k n) -> p k n", n=n)[:, :, off:off + src.shape[2]]
                    sp.dma_start(dst, src).then_inc(arrived[s].sem, 16)

        for kind, *rest in plan:
            if kind == "once":
                load(rest[0], at, 0)
                at += len(rest[0])
            else:
                n, pieces = rest
                per = len(pieces(0))
                assert per % SLOTS == 0 and at >= SLOTS
                with sp.Fori(0, n) as i:
                    load(pieces(i), at, i * per)
                at += n * per

    split_at = [0]

    def split_ahead(n=2):
        for _ in range(n):
            if split_at[0] >= len(shapes):
                return
            size, loads = shapes[split_at[0]]
            s = split_at[0] % SLOTS
            split_at[0] += 1
            arrived[s].k += loads
            act.after(arrived[s].now(), (used, rounded.base, rounded.k + 1 - SLOTS))
            act.do(nc.scalar.activation(w_hi[:, s, 0:size], raw[:, s, 0:size], ACT.Copy), rounded)
            dve.after(rounded.now())
            dve.do(nc.vector.tensor_tensor(w_lo[:, s, 0:size], raw[:, s, 0:size],
                                           w_hi[:, s, 0:size].bitcast(F32), ALU.subtract), split)

    @contextmanager
    def loop(name, n):
        start = split_at[0]
        with core.loop(name, n) as i:
            yield i
        split_at[0] = start + n * (split_at[0] - start)

    def three(out_ap, l, r, start, stop):
        nc.tensor.matmul(out_ap, l[0], r[0], start=start, stop=False, skip_group_check=True)
        nc.tensor.matmul(out_ap, l[0], r[1], start=False, stop=False, skip_group_check=True)
        return nc.tensor.matmul(out_ap, l[1], r[0], start=False, stop=stop, skip_group_check=True)

    def take_piece():
        s = core.piece % SLOTS
        core.piece += 1
        pe.after((split, used.base, used.k + 1))
        return s

    def weights(s, nk, n):
        return [w[:, s, 0:nk * n].rearrange("p (k n) -> p k n", n=n) for w in (w_hi, w_lo)]

    X, Y = (x_hi, x_lo), (y_hi, y_lo)

    def product_turned(ps, act_in, k0=0, first=True, last=True):
        for half in range(2):
            s = take_piece()
            w = weights(s, 4, 512)
            for k in range(4):
                kk = half * 4 + k
                for c in range(4):
                    mm = three(ps[:, c * SEQ:(c + 1) * SEQ], [x[:, k, c * P:(c + 1) * P] for x in w],
                               [x[:, k0 + kk, :] for x in act_in], first and kk == 0 and c % 2 == 0, last and kk == 7)
            pe.do(mm, used)

    def natural_half(ps, act_in, n, half):
        s = take_piece()
        w = weights(s, 4, n)
        for k in range(4):
            kk = half * 4 + k
            for m in range(MT):
                mm = three(ps[:, m * 512:m * 512 + n], [x[:, kk, m * P:(m + 1) * P] for x in act_in],
                           [x[:, k, :] for x in w], kk == 0, kk == 7)
        pe.do(mm, used)

    def product_natural(ps, act_in, n=512):
        for half in range(2):
            natural_half(ps, act_in, n, half)

    banks = [(psum_a, a_free), (psum_b, b_free)]
    turn = [0]

    def next_bank():
        ps, free = banks[turn[0] % 2]
        turn[0] += 1
        pe.after(free.now())
        return ps, free

    def run_product(kind, act_in, evacuate, **kw):
        ps, free = next_bank()
        kind(ps, act_in, **kw)
        split_ahead()
        evacuate(ps, free, used.now())

    def round_split(hi, lo, src_f32, ready, free=None, scale=None):
        act.after(ready)
        sc = 1.0 if scale is None else scale
        t = act.do(nc.scalar.activation(hi, src_f32, ACT.Copy, scale=sc))
        dve.after(t, ready)
        return dve.do(nc.vector.scalar_tensor_tensor(out=lo, in0=src_f32, scalar=sc, in1=hi.bitcast(F32),
                                                     op0=ALU.mult, op1=ALU.subtract), free)

    def power(out_ap, in_ap, n, ready):
        pool.after(ready)
        return pool.do(nc.gpsimd.tensor_tensor(out_ap, in_ap, half_neg[:, 0:n], ALU.pow))

    def row_rstd(parts, width, slot, ready, junk):
        n = len(parts)
        act.after(*ready)
        for j, part in enumerate(parts):
            act.after(act.done.now())
            t = act.do(nc.scalar.activation(junk[:, 0:width], part, ACT.Square, accum_out=small[:, slot + j:slot + j + 1]))
        dve.after(t)
        t = dve.do(nc.vector.tensor_scalar(small[:, slot:slot + n], small[:, slot:slot + n], 1.0 / width, EPS, ALU.mult, ALU.add))
        return power(small[:, slot + n:slot + 2 * n], small[:, slot:slot + n], n, t)

    quarters = [(psum_a[:, 0:512], count("quarter0")), (psum_b[:, 0:512], count("quarter1")),
                (psum_a[:, 512:1024], count("quarter2")), (psum_b[:, 512:1024], count("quarter3"))]

    def turn_and_split(src, dst, kd, gain, ready, k_to=0, diagonal=None):
        pe.after(a_free.now(), b_free.now(), ready)
        for k in range(kd):
            ps, free = quarters[k % 4]
            pe.after(free.now())
            for m in range(MT):
                part = src[:, m, k * P:(k + 1) * P]
                if diagonal is None:
                    mm = nc.tensor.transpose(ps[:, m * P:(m + 1) * P], part, ident[:])
                else:
                    mm = nc.tensor.matmul(ps[:, m * P:(m + 1) * P], part, diagonal[:, m, :], start=m == 0, stop=True,
                                          skip_group_check=True)
            t = pe.do(mm)
            t = round_split(dst[0][:, k_to + k, :], dst[1][:, k_to + k, :], ps[:, 0:SEQ], t, free,
                            scale=cols[:, gain + k:gain + k + 1])
        pe.after(*[q[1].now() for q in quarters])
        return t

    diag = sb("diag", [P, 2, MT, P])
    squares = sb("squares", [P, 16])

    def mean_rstd(sums, out_cols, width, ready):
        dve.after(*ready)
        t = dve.do(nc.vector.tensor_scalar(sums, sums, 1.0 / width, EPS, ALU.mult, ALU.add))
        return power(out_cols, sums, sums.shape[1], t)

    def rms_diag(src, ready, which=0):
        sums, root = (squares[:, 8 + 4 * which + j:10 + 4 * which + j] for j in (0, 2))
        act.after(act.done.now(), *ready[0])
        ta = act.do(nc.scalar.activation(psum_c[:, 0:D], src[:, 0, :], ACT.Square, accum_out=sums[:, 0:1]))
        dve.after(dve.done.now(), *ready[1])
        tv = dve.do(nc.vector.scalar_tensor_tensor(out=psum_c[:, D:2 * D], in0=src[:, 1, :], scalar=1.0, in1=src[:, 1, :],
                                                   op0=ALU.mult, op1=ALU.mult, accum_out=sums[:, 1:2]))
        t = mean_rstd(sums, root, D, [ta, tv])
        dve.after(t, pe.done.now())
        for m in range(MT):
            t = dve.do(nc.vector.tensor_scalar(diag[:, which, m, :], ident[:], root[:, m:m + 1], None, ALU.mult))
        return t

    def rms_turn(src, dst, gain, ready, which=0):
        return turn_and_split(src, dst, KD, gain, ready, diagonal=diag[:, which, :, :])

    def rms_turned(src, dst, gain, ready):
        return rms_turn(src, dst, gain, rms_diag(src, ready))

    def gain_and_squares(ps, og, g, sums, ready, free=None):
        act.after(ready)
        dve.after(ready)
        a = act.do(nc.scalar.activation(og[0], ps[0], ACT.Square, accum_out=sums[0]))
        v = dve.do(nc.vector.tensor_tensor(og[1], ps[1], g, ALU.mult))
        dve.after(a)
        act.after(v, a)
        ta = act.do(nc.scalar.activation(ps[1], ps[1], ACT.Square, accum_out=sums[1]), free)
        tv = dve.do(nc.vector.tensor_tensor(og[0], ps[0], g, ALU.mult), free)
        return ta, tv

    names = [("g_pre_mix", 8), ("g_pre_xa", 8), ("g_mem", 8), ("g_pre_ffn", 8), ("norm_mix_2", 16), ("norm_ffn_2", 16),
             ("mem_norm_2", 8), ("g_ssm_norm", 16), ("conv_w", 96), ("conv_b", 24), ("ffn_conv_w_2", 264),
             ("ffn_conv_b_2", 88), ("mla_qa_norm_2", 2), ("mla_kva_norm_2", 1)]
    col_of, at = {}, 0
    for name, n in names:
        col_of[name] = at
        at += n
    assert at <= 5 * P
    rowed = {}
    for name, n in names:
        v = ins[name]
        letters = "abc"[:len(v.shape)]
        rowed[name] = v.rearrange(f"{' '.join(letters)} -> ({' '.join(letters)})") if len(v.shape) > 1 else v

    head_cols = sb("head_cols", [P, 16])
    HC = {"fox_q_gain_2": 0, "fox_k_gain_2": 1, "mla_q_gain_2": 2, "mla_k_gain_2": 3, "mem_q_gain_2": 4, "mem_k_gain_2": 6}
    bcast = sb("bcast", [P, 4, 32])
    inv_freq = sb("inv_freq", [P, 16])
    pos_i = sb("pos_i", [P, MT], I32)
    rotary = sb("rotary", [P, 2, MT, 16])

    def load_on(where, dst, src, engine=nc.gpsimd):
        return where.mark(engine.dma_start(dst, src))

    def load(dst, src):
        return load_on(loaded, dst, src)

    sp.dma_start(res[:, :, :], ins["x"][0].rearrange("(m p) d -> p m d", p=P)).then_inc(stored.sem, 16)
    stored.k += 1
    x_in = stored.now()
    weight_stream()
    stage = core.over("stage", "y_hi", 0, [P, 5, P])
    pool.do(nc.gpsimd.memset(ones[:], 1.0))

    def sel(dst, src, pattern, mult, op, fill, base=0):
        pool.after(pool.done.now())
        return pool.do(nc.gpsimd.affine_select(out=dst, in_=src, compare_op=op, fill=fill, base=base,
                                               pattern=pattern, channel_multiplier=mult))
    eye = sel(ident[:], ones[:], [[-1, P]], 1, ALU.is_equal, 0.0)
    pool.do(nc.gpsimd.memset(half_neg[:], -0.5))
    pool.do(nc.gpsimd.memset(head_cols[:], 1.0))
    pool.do(nc.gpsimd.memset(neg_ones[:], -1.0))
    pool.do(nc.gpsimd.memset(causal[:], 0.0))
    sel(upto[:], ones[:], [[1, P]], -1, ALU.is_ge, 0.0)
    sel(beyond[:], ones[:], [[-1, P]], 1, ALU.is_gt, 0.0)
    sel(strict[:], ones[:], [[1, P]], -1, ALU.is_gt, 0.0)
    sel(neg_from[:], neg_ones[:], [[-1, P]], 1, ALU.is_ge, 0.0)
    sel(causal[:], causal[:], [[-1, P]], 1, ALU.is_ge, NEG)
    for f in range(16):
        pool.do(nc.gpsimd.memset(inv_freq[:, f:f + 1], float(10000.0 ** (-2.0 * f / ROPE))))
    consts = pool.done.now()

    def load_rows(where, name, n, engine):
        done = 0
        while done < n:
            r, tile = (col_of[name] + done) % P, (col_of[name] + done) // P
            k = min(n - done, P - r)
            t = load_on(where, stage[r:r + k, tile, :], rowed[name][done * P:(done + k) * P].rearrange("(r c) -> r c", c=P), engine)
            done += k
        return t
    first_rows_in = load_rows(count("first_rows_loaded", 16), *names[0], nc.scalar)

    def turn_rows(ready, parts, ps):
        pe.after(ready, eye)
        for j, n in parts:
            mm = nc.tensor.transpose(ps[:, j * P:j * P + n], stage[0:n, j, :], ident[0:n, 0:n])
        dve.after(pe.do(mm))
        first, last = parts[0][0] * P, parts[-1][0] * P + parts[-1][1]
        v = dve.do(nc.vector.tensor_copy(cols[:, first:last], ps[:, first:last]))
        act.after(v)
        dve.after(v)

    t = rms_diag(res, [[eye, x_in]] * 2)
    for name, n in names[1:]:
        rows_in = load_rows(rows_loaded, name, n, nc.gpsimd)
    for name, c in HC.items():
        for l in range(ins[name].shape[0]):
            load(head_cols[0:ins[name].shape[1], c + l:c + l + 1], ins[name][l].rearrange("(d a) -> d a", a=1))
    for j, name in enumerate(("dt_bias", "a_log", "d_skip", "fox_b_f_2")):
        n = ins[name].shape[1]
        load(bcast[:, j, 0:n], ins[name][0].partition_broadcast(P))
    for m in range(MT):
        load(pos_i[:, m:m + 1], ins["positions_2"][0, m * P:(m + 1) * P].rearrange("(d a) -> d a", a=1))
    all_in = loaded.now()
    turn_rows(first_rows_in, [(0, 8)], psum_b)
    pe.after(dve.done.now())
    rms_turn(res, X, col_of["g_pre_mix"], t)
    split_ahead(2)

    def copy_out(dst, scale=1.0):
        def evacuate(ps, free, ready):
            act.after(ready)
            dve.after(ready)
            a = act.do(nc.scalar.activation(dst(0), ps[:, 0:512].rearrange("p (c t) -> p c t", c=dst(0).shape[1]), ACT.Copy, scale=scale), free)
            dve.do(nc.vector.tensor_scalar(dst(1), ps[:, 512:1024].rearrange("p (c t) -> p c t", c=dst(1).shape[1]), scale, None, ALU.mult), free)
        return evacuate

    mix = ExitStack()
    merged = core.sb("merged", [P, KD, SEQ], ctx=mix)
    with ExitStack() as phase:
        q_t = core.sb("q_t", [P, KD, SEQ], ctx=phase)
        k_t = core.sb("k_t", [P, KD, SEQ], ctx=phase)
        v_n = core.sb("v_n", [P, MT, D], ctx=phase)
        for dst, scale in ((q_t, SB_DIM ** -0.5), (k_t, 1.0)):
            for c in range(2):
                run_product(product_turned, X, copy_out(lambda j: dst[:, 4 * c + 2 * j:4 * c + 2 * j + 2, :], scale))
        for c in range(2):
            run_product(product_natural, X, copy_out(lambda j: v_n[:, j:j + 1, 512 * c:512 * c + 512]))
        turn_rows(rows_in, [(j, min(P, at - j * P)) for j in range(5)], psum_c)
        for lane in (act, dve, pe, pool):
            lane.after(all_in, consts)
        for c, l, dim in ((HC["fox_q_gain_2"], 1, HD), (HC["mla_q_gain_2"], 1, QK), (HC["mem_q_gain_2"], 2, HD)):
            dve.do(nc.vector.tensor_scalar(head_cols[0:dim, c:c + l], head_cols[0:dim, c:c + l], float(dim) ** -0.5, None, ALU.mult))
        stick_attention(core, locals())
        core.fence()

    def gate(dst, c):
        def evacuate(ps, free, ready):
            act.after(ready)
            for j in range(2):
                act.do(nc.scalar.activation(dst[:, 4 * c + 2 * j:4 * c + 2 * j + 2, :],
                                            ps[:, 512 * j:512 * j + 512].rearrange("p (c t) -> p c t", c=2), ACT.Sigmoid), free)
        return evacuate

    for c in range(2):
        run_product(product_turned, X, gate(merged, c))
    for c in range(2):
        def evacuate(ps, free, ready, c=c):
            dve.after(ready, a_free.now(), b_free.now())
            for j in range(2):
                m = merged[:, 4 * c + 2 * j:4 * c + 2 * j + 2, :]
                dve.do(nc.vector.tensor_tensor(m, ps[:, 512 * j:512 * j + 512].rearrange("p (c t) -> p c t", c=2), m, ALU.mult), free)
        run_product(product_turned, Y, evacuate)
    core.fence(act, dve, pool)

    with ExitStack() as phase:
        gate_s = core.sb("gate_s", [P, KD, SEQ], ctx=phase)

        def gate_product(c):
            run_product(product_turned, X, gate(gate_s, c))
        mamba(core, locals())
        for c in range(2):
            ps, free = next_bank()
            for h in range(2):
                product_turned(ps, Y, k0=KD * h, first=h == 0, last=h == 1)
                split_ahead()
            dve.after(used.now(), a_free.now(), b_free.now())
            for j in range(2):
                g = gate_s[:, 4 * c + 2 * j:4 * c + 2 * j + 2, :]
                m = merged[:, 4 * c + 2 * j:4 * c + 2 * j + 2, :]
                t = dve.do(nc.vector.tensor_tensor(g, ps[:, 512 * j:512 * j + 512].rearrange("p (c t) -> p c t", c=2), g, ALU.mult), free)
                dve.after(t)
                t = dve.do(nc.vector.tensor_tensor(g, g, m, ALU.add))
                round_split(x_hi[:, 4 * c + 2 * j:4 * c + 2 * j + 2, :], x_lo[:, 4 * c + 2 * j:4 * c + 2 * j + 2, :], g, t)
        core.fence()
    mix.close()

    def add_normed(og, columns, ready):
        dve.after(*ready)
        sums = squares[:, 4:4 + 2 * columns].rearrange("p (m c) -> p m c", m=MT)
        t = dve.do(nc.vector.tensor_reduce(squares[:, 0:2], sums, AX, ALU.add))
        t = mean_rstd(squares[:, 0:2], squares[:, 2:4], D, [t])
        dve.after(t)
        return [[dve.do(nc.vector.scalar_tensor_tensor(out=res[:, m, :], in0=og[:, m, :], scalar=squares[:, 2 + m:3 + m],
                                                       in1=res[:, m, :], op0=ALU.mult, op1=ALU.add))] for m in range(MT)]

    def post_product(gain_name, act_in, og, g, after_first):
        gain_in = load(g[:, :], ins[gain_name][0].partition_broadcast(P))
        for c in range(2):
            cs = slice(512 * c, 512 * c + 512)

            def evacuate(ps, free, ready):
                dve.after(gain_in)
                gain_and_squares([ps[:, 0:512], ps[:, 512:1024]], [og[:, 0, cs], og[:, 1, cs]], g[:, cs],
                                 [squares[:, 4 + c:5 + c], squares[:, 6 + c:7 + c]], ready, free)
            run_product(product_natural, act_in, evacuate)
            if c == 0:
                after_first()
        return [a_free.now(), b_free.now()]

    def post_norm_beside_memory(gain_name, og, g, memory, memory_gain, next_out):
        tokens = []
        core.fence(pool)
        memory_in = load(memory[:, :, :], memory_from[0].rearrange("(m p) d -> p m d", p=P))
        sums_in = post_product(gain_name, X, og, g, lambda: tokens.append(rms_diag(memory, [[memory_in]] * 2, 1)))
        rms_turn(memory, Y, memory_gain, tokens[0], 1)

        def evacuate(ps, free, ready):
            tokens.append(rms_diag(res, add_normed(og, 2, sums_in)))
            next_out[1](ps, free, ready)
        run_product(next_out[0], Y, evacuate)
        return tokens[1]

    memory_kv = core.sb("memory_kv", [P, MT, 2 * MEM_W])
    with ExitStack() as phase:
        kx = core.sb("kx", [P, KD, SEQ], ctx=phase)
        vx = core.sb("vx", [P, MT, D], ctx=phase)

        def keys_out(c):
            return copy_out(lambda j: kx[:, 4 * c + 2 * j:4 * c + 2 * j + 2, :])
        with ExitStack() as inner:
            mem, og = (core.sb(name, [P, MT, D], ctx=inner) for name in ("mem", "mix_out"))
            g = core.sb("gain_mix", [P, D], ctx=inner)
            memory_from = ins["mem"]
            normed = post_norm_beside_memory("g_post_mix", og, g, mem, col_of["g_mem"], (product_turned, keys_out(0)))
            run_product(product_turned, Y, keys_out(1))
            rotary_tables(core, dict(locals(), phase=inner))
            for c in range(2):
                run_product(product_natural, Y, copy_out(lambda j: vx[:, j:j + 1, 512 * c:512 * c + 512]))
        rms_turn(res, X, col_of["g_pre_xa"], normed)
        qx = core.sb("qx", [P, KD, SEQ], ctx=phase)
        for c in range(2):
            run_product(product_turned, X, copy_out(lambda j: qx[:, 4 * c + 2 * j:4 * c + 2 * j + 2, :], XA_DIM ** -0.5))
        cross_attention(core, locals())
        core.fence()
    with ExitStack() as phase:
        mem, og = (core.sb(name, [P, MT, D], ctx=phase) for name in ("mem2", "xa_out"))
        g = core.sb("gain_xa", [P, D], ctx=phase)
        memory_from = ins["mem_2"]
        normed = post_norm_beside_memory("g_post_xa", og, g, mem, col_of["mem_norm_2"],
                                         (product_natural, copy_out(lambda j: memory_kv[:, j:j + 1, :])))
        rms_turn(res, X, col_of["g_pre_ffn"], normed)

    with ExitStack() as phase:
        g = core.sb("gain_ffn", [P, D], ctx=phase)
        gain_in = load(g[:, :], ins["g_post_ffn"][0].partition_broadcast(P))
        ffn(core, locals(), None)
        og = core.sb("ffn_out", [P, MT, D], ctx=phase)
        dve.after(gain_in)
        ready = gain_and_squares([psum_c[:, 0:D], psum_c[:, D:2 * D]], [og[:, 0, :], og[:, 1, :]], g[:, :],
                                 [squares[:, 4:5], squares[:, 5:6]], used.now())
        normed = rms_diag(res, add_normed(og, 1, ready))
        core.fence()

    memory_rstd = sb("memory_rstd", [P, MT, MEM_HEADS])
    def out_half(c, half):
        ps, free = banks[c]
        pe.after(free.now())
        natural_half(ps, Y, 512, half)
        split_ahead(1)

    for layer in range(2):
        with ExitStack() as phase:
            rms_turn(res, X, col_of["norm_mix_2"] + KD * layer, normed)
            (fox if layer == 0 else mla)(core, locals())
            core.fence()
        for c, (ps, free) in enumerate(banks):
            out_half(c, 1)
            dve.after(used.now())
            for m in range(MT):
                r = res[:, m, 512 * c:512 * c + 512]
                dve.do(nc.vector.tensor_tensor(r, ps[:, 512 * m:512 * m + 512], r, ALU.add), free)
        core.fence()
        with ExitStack() as phase:
            rms_turned(res, X, col_of["norm_ffn_2"] + KD * layer, [[a_free.now(), b_free.now()]] * 2)
            ffn(core, locals(), layer)
            added = [dve.do(nc.vector.tensor_tensor(res[:, m, :], psum_c[:, 1024 * m:1024 * m + 1024], res[:, m, :], ALU.add))
                     for m in range(MT)]
            if layer == 0:
                normed = rms_diag(res, [[added[0]], [added[1]]])
                core.fence()

    for m in range(MT):
        act.after(added[m])
        stored.mark(nc.scalar.dma_start(out[0, m * P:(m + 1) * P, :], res[:, m, :]))
    act.after(stored.now())


def ctx_psum(core, name, shape):
    return core.ctx.enter_context(core.nc.psum_tensor(name, shape, F32))


def stick_attention(core, env):
    nc, pe, act, dve, pool = core.nc, core.pe, core.act, core.dve, core.pool
    q_t, k_t, v_n, phase = env["q_t"], env["k_t"], env["v_n"], env["phase"]
    y_hi, y_lo = env["Y"]
    W = 384
    PAIRS = SB_HEADS // 2
    kq = core.sb("stick_kq", [P, 2, 2, SEQ], ctx=phase)
    vb = core.sb("stick_v", [P, 2, MT, P], ctx=phase)
    L, w = (core.over("stick_" + name, y, KD * SEQ, [P, 2, 2, W]) for name, y in (("l", "y_hi"), ("w", "y_lo")))
    z = [ps[:, 0:1024].rearrange("p (b w) -> p b w", b=2)[:, :, 0:W] for ps in (env["psum_a"], env["psum_c"])]
    core.fence()

    def diagonal(x):
        return x.rearrange("p b (k t) -> p b k t", t=P)[:, :, 0:3:2, :]

    strict = env["strict"][:].unsqueeze(1).unsqueeze(1).to_broadcast([P, 2, 2, P])
    kq_in, v_in, z_made, z_free, l_made, w_made, v_free = (
        [Count(core, f"stick_{name}{u}") for u in range(2)]
        for name in ("kq_in", "v_in", "z_made", "z_free", "l_made", "w_made", "v_free"))
    o_made = Count(core, "stick_o_made")
    o_free = [Count(core, f"stick_o_free{b}") for b in range(2)]

    def stage_kq(j, u):
        pool.after(z_made[u].now())
        pool.do(nc.gpsimd.tensor_copy(kq[:, u, 0, :], k_t[:, bass.ds(j, 1), :].rearrange("p a t -> p (a t)")), kq_in[u])
        pool.do(nc.gpsimd.tensor_copy(kq[:, u, 1, :], q_t[:, bass.ds(j, 1), :].rearrange("p a t -> p (a t)")), kq_in[u])

    def stage_v(j, u):
        pool.after(v_free[u].now())
        for m in range(MT):
            pool.do(nc.gpsimd.tensor_copy(vb[:, u, m, :], v_n[:, m, bass.ds(j * P, P)]), v_in[u])

    def scores(u):
        pe.after(kq_in[u].now(), z_free[u].now())
        for b in range(2):
            r = slice(64 * b, 64 * b + 64)
            nc.tensor.matmul(z[u][:, b, 0:SEQ], kq[r, u, 0, 0:P], kq[r, u, 1, :], start=True, stop=False, skip_group_check=True)
            mm = nc.tensor.matmul(z[u][:, b, SEQ:W], kq[r, u, 0, P:SEQ], kq[r, u, 1, P:SEQ], start=False, stop=False,
                                  skip_group_check=True)
        pe.do(mm, z_made[u])

    def softplus(u):
        dve.after(z_made[u].now())
        t = dve.do(nc.vector.tensor_scalar(L[:, u, :, :], z[u], 30.0, None, ALU.min))
        act.after(t)
        t = act.do(nc.scalar.activation(L[:, u, :, :], L[:, u, :, :], ACT.Exp))
        act.after(t)
        t = act.do(nc.scalar.activation(L[:, u, :, :], L[:, u, :, :], ACT.Ln, bias=1.0))
        dve.after(t)
        t = dve.do(nc.vector.tensor_tensor(L[:, u, :, :], z[u], L[:, u, :, :], ALU.max))
        dve.after(t)
        dve.do(nc.vector.tensor_tensor(diagonal(L[:, u, :, :]), diagonal(L[:, u, :, :]), strict, ALU.mult), l_made[u])

    def weights(u):
        pe.after(l_made[u].now())
        for b in range(2):
            nc.tensor.matmul(z[u][:, b, 0:SEQ], env["neg_from"][:], L[:, u, b, 0:SEQ], start=False, stop=False, skip_group_check=True)
            nc.tensor.matmul(z[u][:, b, P:SEQ], env["neg_ones"][:], L[:, u, b, SEQ:W], start=False, stop=False, skip_group_check=True)
            mm = nc.tensor.matmul(z[u][:, b, SEQ:W], env["neg_from"][:], L[:, u, b, SEQ:W], start=False, stop=True,
                                  skip_group_check=True)
        act.after(pe.do(mm))
        act.do(nc.scalar.activation(w[:, u, :, :], z[u], ACT.Exp), z_free[u])
        dve.after(z_free[u].now())
        for b in range(2):
            d = diagonal(w[:, u, b:b + 1, :])[:, 0, :, :]
            dve.do(nc.vector.scalar_tensor_tensor(out=d, in0=d, scalar=3.0e38, in1=strict[:, 0, :, :], op0=ALU.min, op1=ALU.mult),
                   w_made[u])

    def output(j, u):
        pe.after(w_made[u].now(), v_in[u].now())
        for b in range(2):
            o = env["psum_b"][:, 512 * b:512 * b + SEQ]
            pe.after(o_free[b].now())
            nc.tensor.matmul(o, vb[:, u, 0, :], w[:, u, b, 0:SEQ], start=True, stop=False, skip_group_check=True)
            t = pe.do(nc.tensor.matmul(o[:, P:SEQ], vb[:, u, 1, :], w[:, u, b, SEQ:W], start=False, stop=True,
                                       skip_group_check=True), o_made if b == 0 else v_free[u])
            r = slice(64 * b, 64 * b + 64)
            act.after(t)
            dst = [y[r, bass.ds(j, 1), :].rearrange("p a t -> p (a t)") for y in (y_hi, y_lo)]
            a = act.do(nc.scalar.activation(dst[0], o[r, :], ACT.Copy))
            dve.after(a)
            dve.do(nc.vector.tensor_tensor(dst[1], o[r, :], dst[0].bitcast(F32), ALU.subtract), o_free[b])

    nc.scalar.preload_act_table_set("natural_log_exp_and_others")
    stage_kq(0, 0)
    stage_kq(1, 1)
    stage_v(0, 0)
    for u in range(2):
        scores(u)
        softplus(u)
    weights(0)
    with env["loop"]("stick", PAIRS // 2 - 1) as i:
        for j, u in ((1, 1), (2, 0)):
            stage_kq(i * 2 + (j + 1), 1 - u)
            stage_v(i * 2 + j, u)
            scores(1 - u)
            softplus(1 - u)
            weights(u)
            output(i * 2 + (j - 1), 1 - u)
    stage_v(PAIRS - 1, 1)
    weights(1)
    output(PAIRS - 2, 0)
    output(PAIRS - 1, 1)


def mamba(core, env):
    nc, pe, act, dve, pool = core.nc, core.pe, core.act, core.dve, core.pool
    psum_a, psum_b, psum_c = env["psum_a"], env["psum_b"], env["psum_c"]
    cols, small, bcast, upto, beyond, ident = (env[n] for n in ("cols", "small", "bcast", "upto", "beyond", "ident"))
    a_free, b_free, used, free_c = env["a_free"], env["b_free"], env["used"], Count(core, "c_free")
    X, col_of, run_product, loop = env["X"], env["col_of"], env["run_product"], env["loop"]
    GH, GW = GROUP_HEADS, SSM_INNER // SSM_GROUPS
    phase = env["phase"]
    b_t, c_t = env["gate_s"][:, 0:SSM_GROUPS, :], env["gate_s"][:, SSM_GROUPS:2 * SSM_GROUPS, :]
    y_n = core.sb("y_n", [P, MT, SSM_INNER], ctx=phase)
    dts = core.sb("dts", [P, 5, MT, SSM_HEADS], ctx=phase)
    dt, adt, tmp, eac = (dts[:, j, :, :] for j in range(4))
    to_end = dts[:, 4, 0, :]

    bg = core.sb("bg", [P, 2, SEQ], ctx=phase)
    cg = core.sb("cg", [P, 2, SEQ], ctx=phase)
    with ExitStack() as inner:
        conv = core.sb("conv", [P, 2, 4, SEQ], ctx=inner)

        def convolve(u, tile, dst):
            def col(name, tap, j):
                at = tile + (col_of[name] + tap * (XBC // P) + j)
                return cols[:, bass.ds(at, 1)]

            def evacuate(ps, free, ready):
                act.after(ready, pe.done.now(), act.done.now())
                for j in range(4):
                    t = act.do(nc.scalar.activation(conv[:, u, j, :], ps[:, j * SEQ:(j + 1) * SEQ], ACT.Identity,
                                                    scale=col("conv_w", 3, j), bias=col("conv_b", 0, j)))
                dve.after(t)
                for d in (1, 2, 3):
                    for j in range(4):
                        t = dve.do(nc.vector.scalar_tensor_tensor(
                            out=conv[:, u, j, d:], in0=ps[:, j * SEQ:(j + 1) * SEQ - d], scalar=col("conv_w", 3 - d, j),
                            in1=conv[:, u, j, d:], op0=ALU.mult, op1=ALU.add), free if (d, j) == (3, 3) else None)
                    dve.after(t)
                act.after(t)
                act.do(nc.scalar.activation(dst, conv[:, u, :, :], ACT.Silu))
            return evacuate

        def turn_back(u, ready, at):
            pe.after(ready, free_c.now())
            for j in range(4):
                for m in range(MT):
                    mm = nc.tensor.transpose(psum_c[:, 1024 * u + 512 * m + j * P:1024 * u + 512 * m + (j + 1) * P],
                                             conv[:, u, j, m * P:(m + 1) * P], ident[:])
            t = pe.do(mm)
            dve.after(t)
            act.after(t)
            act.do(nc.scalar.activation(y_n[:, 0, bass.ds(at, GW)], psum_c[:, 1024 * u:1024 * u + 512], ACT.Copy), free_c)
            dve.do(nc.vector.tensor_copy(y_n[:, 1, bass.ds(at, GW)], psum_c[:, 1024 * u + 512:1024 * u + 1024]), free_c)

        def evacuate(ps, free, ready):
            nc.scalar.preload_act_table_set("natural_log_exp_and_others")
            act.do(nc.scalar.activation(bcast[:, 1, :], bcast[:, 1, :], ACT.Exp))
            dve.after(ready)
            for m in range(MT):
                t = dve.do(nc.vector.tensor_tensor(dt[:, m, :], ps[:, 512 * m:512 * m + SSM_HEADS], bcast[:, 0, :], ALU.add), free)
            dve.after(t)
            t = dve.do(nc.vector.tensor_scalar(tmp, dt, 30.0, None, ALU.min))
            act.after(t, act.done.now())
            t = act.do(nc.scalar.activation(tmp, tmp, ACT.Exp))
            act.after(t)
            t = act.do(nc.scalar.activation(tmp, tmp, ACT.Ln, bias=1.0))
            dve.after(t)
            t = dve.do(nc.vector.tensor_tensor(dt, dt, tmp, ALU.max))
            dve.after(t)
            for m in range(MT):
                dve.do(nc.vector.scalar_tensor_tensor(out=adt[:, m, :], in0=dt[:, m, :], scalar=-1.0, in1=bcast[:, 1, :],
                                                      op0=ALU.mult, op1=ALU.mult))
        run_product(env["product_natural"], X, evacuate, n=SSM_HEADS)
        adt_in = dve.done.now()
        nc.scalar.preload_act_table_set("silu_and_others")
        for u, dst in ((0, b_t), (1, c_t)):
            run_product(env["product_turned"], X, convolve(u, 16 + 4 * u, dst[:, :, :]))
        pe.after(adt_in)
        for c in range(MT):
            nc.tensor.matmul(psum_c[:, 32 * c:32 * c + 32], upto[:], adt[:, c, :], start=c == 0, stop=True, skip_group_check=True)
        t = pe.do(nc.tensor.matmul(psum_c[:, 64:96], beyond[:], adt[:, 0, :], start=False, stop=True, skip_group_check=True))
        act.after(t)
        act.do(nc.scalar.activation(eac, psum_c[:, 0:64].rearrange("p (c h) -> p c h", c=MT), ACT.Exp))
        act.do(nc.scalar.activation(to_end, psum_c[:, 64:96], ACT.Exp))
        before_x = [c.now() for c in core.counts if c.unit == 1]
        turn = None
        for k in range(SSM_INNER // GW):
            run_product(env["product_turned"], X, convolve(k % 2, 4 * k, conv[:, k % 2, :, :]))
            silu = act.done.now()
            if turn:
                turn_back(*turn)
            turn = (k % 2, silu, k * GW)
        turn_back(*turn)
        core.fence(pe, act, dve)
        pool.after(*before_x)

    with ExitStack() as inner:
        b_n = core.sb("b_n", [P, 2, P], ctx=inner)
        cb = core.sb("cb", [P, 2, MT, P], ctx=inner)
        late = core.sb("late", [P, 2, GW], ctx=inner)
        rows = core.over("rows", "y_lo", 0, [P, 2, 4, 4, P])
        xc = core.over("xc", "y_hi", 0, [P, 2, MT, GH, SSM_HD])
        xd = core.over("xd", "y_hi", 2048, [P, 2, GH, SSM_HD])
        state = core.over("state", "y_hi", 3072, [P, 2, GW])
        (bc_in, bc_free, rows_in, own_made, cb_free, x_made, x_kept, seg_free) = (
            [Count(core, f"ssd_{name}{u}") for u in range(2)]
            for name in ("bc_in", "bc_free", "rows_in", "own_made", "cb_free", "x_made", "x_kept", "seg_free"))
        state_free, off_free = Count(core, "ssd_state_free"), Count(core, "ssd_off_free")
        own_free = [Count(core, f"ssd_own_free{c}") for c in range(MT)]
        ps_cb = [psum_a[:, 512 * u:512 * u + 2 * P] for u in range(2)]
        ps_state, ps_off = psum_b[:, 0:GW], psum_b[:, 512:512 + GW]
        ps_own = [psum_c[:, 512 * c:512 * c + 512] for c in range(MT)]
        ps_seg = [psum_c[:, 1024 + 512 * v:1536 + 512 * v] for v in range(2)]
        per_head = [P, MT, GH, SSM_HD]

        def group(x, g, n=GH, h0=0):
            return x[:, :, bass.ds(g * GH + h0, n)]

        def x_of(g):
            return y_n[:, :, bass.ds(g * GW, GW)].rearrange("p c (h d) -> p c h d", d=SSM_HD)

        def prepare(u, g):
            pe.after(bc_in[u].now(), cb_free[u].now())
            for c in range(MT):
                mm = nc.tensor.matmul(ps_cb[u][:, P * c:P * c + P], bg[:, u, P * c:P * c + P], cg[:, u, P * c:P * c + P],
                                      start=c == 0, stop=True, skip_group_check=True)
            t_cb = pe.do(mm)
            pe.after(state_free.now())
            t = pe.do(nc.tensor.transpose(ps_state[:, 0:P], bg[:, u, 0:P], ident[:]))
            act.after(t)
            t_bn = act.do(nc.scalar.activation(b_n[:, u, :], ps_state[:, 0:P], ACT.Copy))
            dve.after(own_made[u].now())
            t = dve.do(nc.vector.tensor_tensor(xc[:, u, :, :, :], x_of(g), group(dt, g).unsqueeze(3).to_broadcast(per_head), ALU.mult),
                       x_made[u])
            dve.after(t)
            t_xd = dve.do(nc.vector.tensor_tensor(xd[:, u, :, :], xc[:, u, 0, :, :], to_end[:, bass.ds(g * GH, GH)].unsqueeze(2)
                                                  .to_broadcast([P, GH, SSM_HD]), ALU.mult))
            dve.after(t_cb)
            dve.do(nc.vector.tensor_tensor(cb[:, u, :, :], ps_cb[u].rearrange("p (c t) -> p c t", c=MT),
                                           upto[:].unsqueeze(1).to_broadcast([P, MT, P]), ALU.mult), cb_free[u])
            pe.after(t_bn, t_xd)
            t = pe.do(nc.tensor.matmul(ps_state, b_n[:, u, :], xd[:, u, :, :].rearrange("p h d -> p (h d)"), start=True, stop=True))
            act.after(t)
            t = act.do(nc.scalar.activation(state[:, u, :], ps_state, ACT.Copy), state_free)
            pe.after(t, off_free.now())
            t_off = pe.do(nc.tensor.matmul(ps_off, cg[:, u, P:SEQ], state[:, u, :], start=True, stop=True), bc_free[u])
            skip = bcast[:, 2, bass.ds(g * GH, GH)].unsqueeze(1).unsqueeze(3).to_broadcast(per_head)
            t_x = dve.do(nc.vector.tensor_tensor(x_of(g), x_of(g), skip, ALU.mult))
            dve.after(t_off)
            t = dve.do(nc.vector.tensor_tensor(late[:, u, :].rearrange("p (h d) -> p h d", d=SSM_HD),
                                               ps_off.rearrange("p (h d) -> p h d", d=SSM_HD),
                                               eac[:, 1, bass.ds(g * GH, GH)].unsqueeze(2).to_broadcast([P, GH, SSM_HD]), ALU.mult),
                       off_free)
            dve.after(t, t_x)
            x_1 = y_n[:, 1, bass.ds(g * GW, GW)]
            dve.do(nc.vector.tensor_tensor(x_1, x_1, late[:, u, :], ALU.add), x_kept[u])

        def decay(u, c, q):
            r, v = rows[:, u, 2 * c + q, :, :], q
            pe.after(rows_in[u].now(), seg_free[v].now())
            t = pe.do(nc.tensor.matmul(ps_seg[v], beyond[:], r.rearrange("p h t -> p (h t)"), start=True, stop=True))
            act.after(t)
            t = act.do(nc.scalar.activation(r, ps_seg[v].rearrange("p (h t) -> p h t", h=4), ACT.Exp), seg_free[v])
            dve.after(t, cb_free[u].now())
            return dve.do(nc.vector.tensor_tensor(r, r, cb[:, u, c, :].unsqueeze(1).to_broadcast([P, 4, P]), ALU.mult))

        def own(u, g, c, q, ready):
            pe.after(ready, own_free[c].now(), x_made[u].now())
            for h in range(4):
                at = (4 * q + h) * SSM_HD
                mm = nc.tensor.matmul(ps_own[c][:, at:at + SSM_HD], rows[:, u, 2 * c + q, h, :], xc[:, u, c, 4 * q + h, :],
                                      start=q == 0 and h == 0, stop=True, skip_group_check=True)
            t = pe.do(mm, own_made[u])
            if q == 1:
                dve.after(t, x_kept[u].now())
                x_c = y_n[:, c, bass.ds(g * GW, GW)]
                dve.do(nc.vector.tensor_tensor(x_c, ps_own[c], x_c, ALU.add), own_free[c])

        core.fence(pe, act, dve)
        with loop("ssd", SSM_GROUPS // 2) as i:
            for u in range(2):
                pool.after(bc_free[u].now())
                pool.do(nc.gpsimd.tensor_copy(bg[:, u, :], b_t[:, bass.ds(i * 2 + u, 1), :].rearrange("p a t -> p (a t)")), bc_in[u])
                pool.do(nc.gpsimd.tensor_copy(cg[:, u, :], c_t[:, bass.ds(i * 2 + u, 1), :].rearrange("p a t -> p (a t)")), bc_in[u])
            for u in range(2):
                pool.after(own_made[u].now())
                for c in range(MT):
                    for q in range(2):
                        heads = adt[:, c, bass.ds((i * 2 + u) * GH + 4 * q, 4)].unsqueeze(2).to_broadcast([P, 4, P])
                        pool.do(nc.gpsimd.tensor_tensor(rows[:, u, 2 * c + q, :, :], upto[:].unsqueeze(1).to_broadcast([P, 4, P]),
                                                        heads, ALU.mult), rows_in[u])
            for u in range(2):
                prepare(u, i * 2 + u)
            steps = [(u, c, q) for u in range(2) for c in range(MT) for q in range(2)]
            ready = decay(*steps[0])
            for this, following in zip(steps, steps[1:] + [None]):
                following_ready = following and decay(*following)
                own(this[0], i * 2 + this[0], this[1], this[2], ready)
                ready = following_ready
        core.fence()

    with ExitStack() as inner:
        gated = core.sb("gated", [P, 2, MT, GW], ctx=inner)
        junk = core.over("junk_z", "bg", 0, [P, GW])
        turned_y = [Count(core, f"turned_y{u}") for u in range(2)]
        nc.scalar.preload_act_table_set("silu_and_others")

        def gate_norm(u, g):
            def evacuate(ps, free, ready):
                act.after(ready, turned_y[u].now())
                t = act.do(nc.scalar.activation(gated[:, u, :, :], ps[:, :].rearrange("p (m n) -> p m n", m=MT), ACT.Silu), free)
                dve.after(t)
                t = dve.do(nc.vector.tensor_tensor(gated[:, u, :, :], gated[:, u, :, :], y_n[:, :, bass.ds(g * GW, GW)], ALU.mult))
                t = env["row_rstd"]([gated[:, u, m, :] for m in range(MT)], GW, 8 * u, [t], junk)
                for m in range(MT):
                    dve.after(t)
                    dve.do(nc.vector.tensor_scalar(gated[:, u, m, :], gated[:, u, m, :], small[:, 8 * u + 2 + m:8 * u + 3 + m],
                                                   None, ALU.mult))
            return evacuate

        def turn(u, g, ready):
            pe.after(ready, free_c.now())
            for j in range(4):
                for m in range(MT):
                    mm = nc.tensor.transpose(psum_c[:, 1024 * u + j * SEQ + m * P:1024 * u + j * SEQ + (m + 1) * P],
                                             gated[:, u, m, j * P:(j + 1) * P], ident[:])
            t = pe.do(mm, turned_y[u])
            for bank in range(2):
                parts = []
                for j in (2 * bank, 2 * bank + 1):
                    hi, lo = (y[:, bass.ds(g * 4 + j, 1), :].rearrange("p a t -> p (a t)") for y in env["Y"])
                    parts.append((hi, lo, psum_c[:, 1024 * u + j * SEQ:1024 * u + (j + 1) * SEQ],
                                  cols[:, bass.ds(g * 4 + (j + col_of["g_ssm_norm"]), 1)]))
                act.after(t)
                for hi, lo, src, gain in parts:
                    a = act.do(nc.scalar.activation(hi, src, ACT.Copy, scale=gain))
                dve.after(a)
                for hi, lo, src, gain in parts:
                    dve.do(nc.vector.scalar_tensor_tensor(out=lo, in0=src, scalar=gain, in1=hi.bitcast(F32),
                                                          op0=ALU.mult, op1=ALU.subtract), free_c)

        pending = None
        for g in range(SSM_GROUPS):
            run_product(env["product_natural"], X, gate_norm(g % 2, g))
            normed = dve.done.now()
            if pending:
                turn(*pending)
            pending = (g % 2, g, normed)
        env["gate_product"](0)
        turn(*pending)
        env["gate_product"](1)
        core.fence()


class Softmax:

    def __init__(self, core, env, tag, phase, host=None):
        self.core, self.env = core, env
        self.p, self.pt = (core.sb(tag + name, [P, 2, 512], ctx=phase) if host is None else
                           core.over(tag + name, host, at, [P, 2, 512]) for name, at in (("_prob", 0), ("_prob_t", 1024)))
        self.peak = core.sb(tag + "_peak", [P, 2, MT], ctx=phase)
        self.total = core.sb(tag + "_total", [P, 2, MT], ctx=phase)
        self.o_free = [Count(core, f"{tag}_o_free{b}") for b in range(2)]
        self.normed = [Count(core, f"{tag}_normed{b}") for b in range(2)]
        self.exped = [Count(core, f"{tag}_exped{b}") for b in range(2)]

    def scores(self, b):
        return self.env["psum_b"][:, 512 * b:512 * b + 512]

    def probabilities(self, scored, causal):
        core, nc = self.core, self.core.nc
        pe, act, dve = core.pe, core.act, core.dve
        w0 = P if causal else SEQ
        parts = [(0, w0), (w0, w0 + SEQ)]
        exped = []
        for b in range(2):
            sc = self.scores(b)
            dve.after(scored[b])
            if causal:
                d = sc[:, 0:384].rearrange("p (b t) -> p b t", t=P)[:, 0:3:2, :]
                t = dve.do(nc.vector.tensor_tensor(d, d, self.env["causal"][:].unsqueeze(1).to_broadcast([P, 2, P]), ALU.add))
                dve.after(t)
            for m, (lo, hi) in enumerate(parts):
                t = dve.do(nc.vector.tensor_reduce(self.peak[:, b, m:m + 1], sc[:, lo:hi], AX, ALU.max))
            dve.after(t)
            t = dve.do(nc.vector.tensor_scalar(self.peak[:, b, :], self.peak[:, b, :], -1.0, None, ALU.mult))
            act.after(t)
            for m, (lo, hi) in enumerate(parts):
                t = act.do(nc.scalar.activation(self.p[:, b, lo:hi], sc[:, lo:hi], ACT.Exp, bias=self.peak[:, b, m:m + 1],
                                                accum_out=self.total[:, b, m:m + 1]), self.exped[b])
            exped.append(t)
        for b in range(2):
            dve.after(exped[b])
            t = dve.do(nc.vector.reciprocal(self.total[:, b, :], self.total[:, b, :]))
            dve.after(t)
            for m, (lo, hi) in enumerate(parts):
                dve.do(nc.vector.tensor_scalar(self.p[:, b, lo:hi], self.p[:, b, lo:hi], self.total[:, b, m:m + 1], None, ALU.mult),
                       self.normed[b])

    def turn(self, causal):
        core, nc = self.core, self.core.nc
        pe, act = core.pe, core.act
        out = []
        order = [0, P, SEQ] if causal else [0, SEQ, P, SEQ + P]
        for b in range(2):
            pe.after(self.normed[b].now())
            psum = self.env["psum_c"][:, 512 * b:512 * b + 512]
            for j, at in enumerate(order):
                mm = nc.tensor.transpose(psum[:, j * P:(j + 1) * P], self.p[:, b, at:at + P], self.env["ident"][:])
            t = pe.do(mm)
            act.after(t)
            n = len(order) * P
            out.append(act.do(nc.scalar.activation(self.pt[:, b, 0:n], psum[:, 0:n], ACT.Copy)))
        return out

    def weigh(self, b, at, values, turned, causal):
        nc, pe = self.core.nc, self.core.pe
        o = self.env["psum_c"][:, 1024 + 512 * b + at:1024 + 512 * b + at + SEQ]
        pe.after(turned, self.o_free[b].now())
        nc.tensor.matmul(o, values[0], self.pt[:, b, 0:SEQ], start=at == 0, stop=False, skip_group_check=True)
        if causal:
            mm = nc.tensor.matmul(o[:, P:SEQ], values[1], self.pt[:, b, SEQ:384], start=False, stop=True, skip_group_check=True)
        else:
            mm = nc.tensor.matmul(o, values[1], self.pt[:, b, SEQ:512], start=False, stop=True, skip_group_check=True)
        return o, mm


def cross_attention(core, env):
    nc, pe, act, dve = core.nc, core.pe, core.act, core.dve
    qx, kx, vx = env["qx"], env["kx"], env["vx"]
    x_hi, x_lo = env["X"]
    soft = Softmax(core, env, "xa", env["phase"])
    core.fence()
    nc.scalar.preload_act_table_set("natural_log_exp_and_others")
    for pair in range(XA_HEADS // 2):
        scored = []
        for b in range(2):
            tiles = range(2 * (2 * pair + b), 2 * (2 * pair + b) + 2)
            pe.after(soft.exped[b].now())
            for m in range(MT):
                for kt in tiles:
                    mm = nc.tensor.matmul(soft.scores(b)[:, SEQ * m:SEQ * m + SEQ], qx[:, kt, m * P:(m + 1) * P], kx[:, kt, :],
                                          start=m == 0 and kt == tiles[0], stop=kt == tiles[1], skip_group_check=True)
            scored.append(pe.do(mm))
        soft.probabilities(scored, False)
        turned = soft.turn(False)
        for b in range(2):
            for j in range(2):
                kt = 2 * (2 * pair + b) + j
                o, mm = soft.weigh(b, SEQ * j, [vx[:, m, kt * P:(kt + 1) * P] for m in range(MT)], turned[b], False)
            t = pe.do(mm)
            kt = 2 * (2 * pair + b)
            src = env["psum_c"][:, 1024 + 512 * b:1536 + 512 * b].rearrange("p (j t) -> p j t", j=2)
            env["round_split"](x_hi[:, kt:kt + 2, :], x_lo[:, kt:kt + 2, :], src, t, soft.o_free[b])


def ffn(core, env, layer):
    nc, pe, act, dve, pool = core.nc, core.pe, core.act, core.dve, core.pool
    psum_a, psum_b, psum_c, cols, col_of = (env[n] for n in ("psum_a", "psum_b", "psum_c", "cols", "col_of"))
    used, X = env["used"], env["X"]
    phase = env["phase"]
    tag = f"ffn{'' if layer is None else layer + 1}"
    hid = [core.sb(f"{tag}_hidden_{part}", [P, 2, SEQ], F32R, ctx=phase) for part in ("hi", "lo")]
    pre = core.sb(tag + "_pre", [P, 2, 2, SEQ], ctx=phase)
    h32 = core.sb(tag + "_h32", [P, 2, SEQ], ctx=phase)
    zero = core.sb(tag + "_zero", [P, P], F32R, ctx=phase)
    ready = [Count(core, f"{tag}_ready{u}") for u in range(2)]
    free = [Count(core, f"{tag}_free{u}") for u in range(2)]
    core.fence()
    nc.scalar.preload_act_table_set("silu_and_others")
    t = act.do(nc.scalar.activation(zero[:], env["ones"][:], ACT.Copy, scale=0.0))
    pe.after(t)
    for bank in range(4):
        mm = nc.tensor.matmul(psum_c[:, 512 * bank:512 * bank + 512], zero[:], X[0][:, 0:2, :].rearrange("p k t -> p (k t)"),
                              start=True, stop=False, skip_group_check=True)
    pe.do(mm)

    def gate_up(u):
        ps = (psum_a, psum_b)[u][:, 0:512]
        s = env["take_piece"]()
        w = env["weights"](s, KD, SEQ)
        pe.after(free[u].now())
        for k in range(KD):
            for j in range(2):
                mm = env["three"](ps[:, j * SEQ:(j + 1) * SEQ], [x[:, k, j * P:(j + 1) * P] for x in w],
                                  [x[:, k, :] for x in X], k == 0 and j == 0, k == KD - 1)
        pe.do(mm, used)

    def down(u):
        s = env["take_piece"]()
        w = [x[:, 0, :] for x in env["weights"](s, 1, D)]
        pe.after(ready[u].now())
        for m in range(MT):
            for n in range(2):
                mm = env["three"](psum_c[:, D * m + 512 * n:D * m + 512 * n + 512], [x[:, u, m * P:(m + 1) * P] for x in hid],
                                  [x[:, 512 * n:512 * n + 512] for x in w], False, True)
        pe.do(mm, used)

    def hidden(u, h, made):
        ps = (psum_a, psum_b)[u]

        def col(name, tap, j):
            at = col_of[name] + (layer * 6 + tap * 2 + j if name == "ffn_conv_w_2" else layer * 2 + j) * FT + h
            return cols[:, bass.ds(at, 1)]

        act.after(made, ready[u].now())
        if layer is None:
            t = act.do(nc.scalar.activation(pre[:, u, 0, :], ps[:, 0:SEQ], ACT.Silu))
            dve.after(t)
            t = dve.do(nc.vector.tensor_tensor(h32[:, u, :], ps[:, SEQ:2 * SEQ], pre[:, u, 0, :], ALU.mult), free[u])
        else:
            for j in range(2):
                t = act.do(nc.scalar.activation(pre[:, u, j, :], ps[:, j * SEQ:(j + 1) * SEQ], ACT.Identity,
                                                scale=col("ffn_conv_w_2", 2, j), bias=col("ffn_conv_b_2", 0, j)))
            for d in (1, 2):
                dve.after(t)
                for j in range(2):
                    t = dve.do(nc.vector.scalar_tensor_tensor(
                        out=pre[:, u, j, d:], in0=ps[:, j * SEQ:(j + 1) * SEQ - d], scalar=col("ffn_conv_w_2", 2 - d, j),
                        in1=pre[:, u, j, d:], op0=ALU.mult, op1=ALU.add), free[u] if (d, j) == (2, 1) else None)
            act.after(t)
            t = act.do(nc.scalar.activation(pre[:, u, 0, :], pre[:, u, 0, :], ACT.Silu))
            dve.after(t)
            t = dve.do(nc.vector.tensor_tensor(h32[:, u, :], pre[:, u, 0, :], pre[:, u, 1, :], ALU.mult))
        pool.after(t, made)
        t = pool.do(nc.gpsimd.tensor_copy(hid[0][:, u, :], h32[:, u, :]))
        dve.after(t, made)
        dve.do(nc.vector.tensor_tensor(hid[1][:, u, :], h32[:, u, :], hid[0][:, u, :].bitcast(F32), ALU.subtract), ready[u])

    core.start_at_one(tag)
    gate_up(0)
    first = used.now()
    env["split_ahead"](1)
    hidden(0, 0, first)
    with env["loop"](tag, (FT - 2) // 2) as i:
        for u in (1, 2):
            gate_up(u % 2)
            made = used.now()
            down((u - 1) % 2)
            env["split_ahead"]()
            hidden(u % 2, i * 2 + u, made)
    gate_up(1)
    made = used.now()
    down(0)
    env["split_ahead"]()
    hidden(1, FT - 1, made)
    down(1)
    env["split_ahead"](1)
    for lane in (act, dve):
        lane.after(used.now())


def rotary_tables(core, env):
    nc, act, dve, rotary = core.nc, core.act, core.dve, env["rotary"]
    rot = core.sb("rotary_work", [P, 4, MT, 16], ctx=env["phase"])
    ang, kk, red, posf = (rot[:, j, :, :] for j in range(4))
    TWO_PI = (6.28125, 0.0019350051879882812, 3.0199159819e-07)
    MAGIC = 12582912.0

    def step(ins):
        dve.after(dve.do(ins))
    core.fence(dve)
    step(nc.vector.tensor_copy(posf[:, :, 0:1], env["pos_i"][:].unsqueeze(2)))
    for m in range(MT):
        step(nc.vector.tensor_scalar(ang[:, m, :], env["inv_freq"][:], posf[:, m, 0:1], None, ALU.mult))
    for dst, quarter in ((rotary[:, 1, :, :], 0.0), (rotary[:, 0, :, :], 0.25)):
        step(nc.vector.tensor_scalar(kk, ang, 1.0 / (2.0 * math.pi), quarter, ALU.mult, ALU.add))
        step(nc.vector.tensor_scalar(kk, kk, MAGIC, None, ALU.add))
        step(nc.vector.tensor_scalar(kk, kk, MAGIC, None, ALU.subtract))
        src = ang
        for part in TWO_PI:
            for m in range(MT):
                step(nc.vector.scalar_tensor_tensor(out=red[:, m, :], in0=kk[:, m, :], scalar=-part, in1=src[:, m, :],
                                                    op0=ALU.mult, op1=ALU.add))
            src = red
        step(nc.vector.tensor_scalar(red, red, quarter * 2.0 * math.pi, None, ALU.add))
        step(nc.vector.tensor_scalar(dst, red, 3.1415925, -3.1415925, ALU.min, ALU.max))
    act.after(dve.done.now())
    act.after(act.do(nc.scalar.activation(rotary[:, :, :, :], rotary[:, :, :, :], ACT.Sin)))


class HeadPairs:

    def __init__(self, core, env, tag, dk, phase):
        self.core, self.env, self.dk = core, env, dk
        self.qh = core.sb(tag + "_qh", [P, 2, MT, dk], ctx=phase)
        self.kh = core.sb(tag + "_kh", [P, 2, MT, dk], ctx=phase)
        self.vh = core.sb(tag + "_vh", [P, MT, P], ctx=phase)
        self.qt = core.sb(tag + "_qt", [P, 2, SEQ], ctx=phase)
        self.kt = core.sb(tag + "_kt", [P, 2, SEQ], ctx=phase)
        self.soft = Softmax(core, env, tag, phase, "x_lo")
        self.built = [Count(core, f"{tag}_built{b}") for b in range(2)]
        self.turned = [Count(core, f"{tag}_turned{b}") for b in range(2)]
        self.qk_in = [Count(core, f"{tag}_qk_in{b}") for b in range(2)]
        self.weighed = Count(core, tag + "_weighed")

    def build(self, pair):
        for b in range(2):
            self.core.pool.after(self.turned[b].now())
            pair[0](b, self.qh[:, b, :, :], self.kh[:, b, :, :], self.built[b])

    def turn(self, pair):
        _, _, gains, dk, _, _ = pair
        core, nc, env = self.core, self.core.nc, self.env
        pe = core.pe
        for b in range(2):
            ps = env["psum_a"][0:dk, 512 * b:512 * b + 512]
            pe.after(self.built[b].now(), self.qk_in[b].now())
            for j, x in enumerate((self.qh, self.kh)):
                for m in range(MT):
                    mm = nc.tensor.transpose(ps[:, (2 * j + m) * P:(2 * j + m + 1) * P], x[:, b, m, 0:dk], env["ident"][:])
            t = pe.do(mm, self.turned[b])
            lane = (core.act, core.dve)[b]
            lane.after(t)
            for x, at, g in ((self.qt, 0, gains[0]), (self.kt, SEQ, gains[1])):
                gain = env["head_cols"][0:dk, g:g + 1]
                if b == 0:
                    lane.do(nc.scalar.activation(x[0:dk, b, :], ps[:, at:at + SEQ], ACT.Copy, scale=gain), self.qk_in[b])
                else:
                    lane.do(nc.vector.tensor_scalar(x[0:dk, b, :], ps[:, at:at + SEQ], gain, None, ALU.mult), self.qk_in[b])

    def scores(self, pair):
        pe, nc = self.core.pe, self.core.nc
        _, _, _, dk, causal, _ = pair
        scored = []
        w0 = P if causal else SEQ
        for b in range(2):
            pe.after(self.qk_in[b].now(), self.soft.exped[b].now())
            sc = self.soft.scores(b)
            nc.tensor.matmul(sc[:, 0:w0], self.qt[0:dk, b, 0:P], self.kt[0:dk, b, 0:w0], start=True, stop=True, skip_group_check=True)
            scored.append(pe.do(nc.tensor.matmul(sc[:, w0:w0 + SEQ], self.qt[0:dk, b, P:SEQ], self.kt[0:dk, b, :],
                                                 start=False, stop=True, skip_group_check=True)))
        return scored

    def step(self, pair, second, third):
        core, nc, env = self.core, self.core.nc, self.env
        pe, pool = core.pe, core.pool
        _, build_v, _, _, causal, tile = pair
        pool.after(self.weighed.now())
        build_v(self.vh)
        v_in = pool.done.now()
        if third:
            self.build(third)
        turned = self.soft.turn(causal)
        if second:
            scored = self.scores(second)
        pe.after(v_in)
        outputs = []
        for b in range(2):
            o, mm = self.soft.weigh(b, 0, [self.vh[:, m, :] for m in range(MT)], turned[b], causal)
            outputs.append((o, pe.do(mm, self.weighed)))
        if second:
            self.soft.probabilities(scored, second[4])
        for b, (o, t) in enumerate(outputs):
            r = slice(64 * b, 64 * b + 64)
            hi, lo = (y[r, bass.ds(tile, 1), :].rearrange("p a t -> p (a t)") for y in env["Y"])
            env["round_split"](hi, lo, o[r, :], t, self.soft.o_free[b])
        if third:
            self.turn(third)

    def run_all(self, name, n, pair, rest, for_rest=None, other_norms=None):
        self.build(pair(0))
        self.turn(pair(0))
        self.build(pair(1))
        if other_norms:
            other_norms()
        self.soft.probabilities(self.scores(pair(0)), pair(0)[4])
        self.turn(pair(1))
        with self.env["loop"](name, n - 2) as i:
            self.step(pair(i), pair(i + 1), pair(i + 2))
        if for_rest:
            for_rest()
            self.core.pool.after(self.core.pool.done.now())
        last = [pair(n - 2), pair(n - 1)] + rest
        for this, second, third in zip(last, last[1:] + [None], last[2:] + [None, None]):
            self.step(this, second, third)
            if this is last[-2]:
                self.env["out_half"](0, 0)
        self.core.pe.after(*[c.now() for c in self.soft.exped])
        self.env["out_half"](1, 0)


def split_heads(x, d):
    return x.rearrange("p (h d) -> p h d", d=d)


def natural_unit(core, env, dst, at, n, sums=None):
    nc, act, dve = core.nc, core.act, core.dve

    def evacuate(ps, free, ready):
        act.after(ready)
        dve.after(ready)
        by = free if sums is None else None
        a = act.do(nc.scalar.activation(dst[:, 0, at:at + n], ps[:, 0:n], ACT.Copy), by)
        v = dve.do(nc.vector.tensor_copy(dst[:, 1, at:at + n], ps[:, 512:512 + n]), by)
        if sums is not None:
            for m, copied in enumerate((a, v)):
                square = ps[:, 512 * m:512 * m + n]
                act.after(copied)
                t = act.do(nc.scalar.activation(square, square, ACT.Square))
                dve.after(t)
                dve.do(nc.vector.tensor_reduce(sums[:, m, :], split_heads(square, HD), AX, ALU.add), free)
    env["run_product"](env["product_natural"], env["X"], evacuate, n=n)


def head_sums(core, sums, squares, x, ready):
    core.act.after(*ready)
    core.dve.after(*ready)
    for m in range(MT):
        t = core.act.do(core.nc.scalar.activation(squares(m), x(m), ACT.Square))
        core.dve.after(t)
        t = core.dve.do(core.nc.vector.tensor_reduce(sums[:, m, :], squares(m), AX, ALU.add))
    return t


def sums_to_rstd(core, env, sums, dim, ready):
    dve, pool, nc = core.dve, core.pool, core.nc
    dve.after(*ready)
    t = dve.do(nc.vector.tensor_scalar(sums, sums, 1.0 / dim, EPS, ALU.mult, ALU.add))
    pool.after(t)
    n = sums.shape[2]
    return pool.do(nc.gpsimd.tensor_tensor(sums, sums, env["half_neg"][:, 0:MT * n].rearrange("p (m h) -> p m h", m=MT), ALU.pow))


def copies(core, by, *pairs):
    for dst, src in pairs:
        core.pool.do(core.nc.gpsimd.tensor_copy(dst, src), by)


def scaled(core, by, dst, src, rstd):
    core.pool.do(core.nc.gpsimd.tensor_tensor(dst, src, rstd.to_broadcast([P, MT, src.shape[2]]), ALU.mult), by)


def memory_pairs(core, env, q, rstd, layer):
    HC = env["HC"]

    def pair(i):
        def build(b, qh, kh, by):
            at = (2 * i + b) * HD
            scaled(core, by, qh[:, :, 0:HD], q[:, :, at:at + HD], rstd[:, :, 2 * i + b:2 * i + b + 1])
            scaled(core, by, kh[:, :, 0:HD], env["memory_kv"][:, :, at:at + HD], env["memory_rstd"][:, :, 2 * i + b:2 * i + b + 1])

        def build_v(vh):
            copies(core, None, (vh[:, :, :], env["memory_kv"][:, :, MEM_W + i * P:MEM_W + (i + 1) * P]))
        return build, build_v, (HC["mem_q_gain_2"] + layer, HC["mem_k_gain_2"] + layer), HD, False, HEADS // 2 + i
    return [pair(i) for i in range(MEM_HEADS // 2)]


def fox(core, env):
    nc, pe, act, dve, pool = core.nc, core.pe, core.act, core.dve, core.pool
    phase, psum_c, bcast = env["phase"], env["psum_c"], env["bcast"]
    DK = HD + 2
    fp = core.sb("fox_p", [P, MT, FOX_IN], ctx=phase)
    rstd = core.sb("fox_rstd", [P, MT, 2 * HEADS], ctx=phase)
    mrstd = core.sb("fox_mem_rstd", [P, MT, MEM_HEADS], ctx=phase)
    cum = core.sb("fox_cum", [P, 3, MT, HEADS], ctx=phase)
    logf, pos, neg = (cum[:, j, :, :] for j in range(3))
    pairs = HeadPairs(core, env, "fox", DK, phase)
    core.fence()
    pool.do(nc.gpsimd.memset(pairs.qh[:, :, :, :], 1.0))
    pool.do(nc.gpsimd.memset(pairs.kh[:, :, :, :], 1.0))
    q_at = MIX * 3 + HEADS
    evacuated = [env["a_free"], env["b_free"]]
    for at, n in FOX_UNITS[:3]:
        natural_unit(core, env, fp, at, n, rstd[:, :, at // HD:(at + n) // HD])
    sums_to_rstd(core, env, rstd[:, :, :], HD, [c.now() for c in evacuated])
    natural_unit(core, env, fp, *FOX_UNITS[3])
    dve.after(*[c.now() for c in evacuated])
    for m in range(MT):
        t = dve.do(nc.vector.scalar_tensor_tensor(out=logf[:, m, :], in0=fp[:, m, 3 * MIX:3 * MIX + HEADS], scalar=-1.0,
                                                  in1=bcast[:, 3, 0:HEADS], op0=ALU.mult, op1=ALU.subtract))
    dve.after(t)
    t = dve.do(nc.vector.tensor_scalar(pos, logf, 30.0, None, ALU.min))
    act.after(t)
    t = act.do(nc.scalar.activation(pos, pos, ACT.Exp))
    act.after(t)
    t = act.do(nc.scalar.activation(pos, pos, ACT.Ln, bias=1.0))
    dve.after(t)
    t = dve.do(nc.vector.tensor_tensor(logf, logf, pos, ALU.max))
    natural_unit(core, env, fp, *FOX_UNITS[4])
    pe.after(t)
    nc.tensor.matmul(psum_c[:, 0:HEADS], env["upto"][:], logf[:, 0, :], start=True, stop=True, skip_group_check=True)
    nc.tensor.matmul(psum_c[:, 32:32 + HEADS], env["ones"][:], logf[:, 0, :], start=False, stop=False, skip_group_check=True)
    t = pe.do(nc.tensor.matmul(psum_c[:, 32:32 + HEADS], env["upto"][:], logf[:, 1, :], start=False, stop=True, skip_group_check=True))
    dve.after(t)
    sums = psum_c[:, 0:64].rearrange("p (m h) -> p m h", m=MT)[:, :, 0:HEADS]
    dve.do(nc.vector.tensor_copy(neg, sums))
    dve.do(nc.vector.tensor_scalar(pos, sums, -1.0, None, ALU.mult))
    decays_in = dve.done.now()
    natural_unit(core, env, fp, *FOX_UNITS[5])
    nc.scalar.preload_act_table_set("natural_log_exp_and_others")
    squares = core.over("fox_squares", "x_hi", 0, [P, MT, MEM_W])

    def memory_norms():
        t = None
        for x, sums in ((fp[:, :, q_at:q_at + MEM_W], mrstd), (env["memory_kv"][:, :, 0:MEM_W], env["memory_rstd"])):
            t = head_sums(core, sums, lambda m: split_heads(squares[:, m, :], HD), lambda m: split_heads(x[:, m, :], HD),
                          [t] if t else [act.done.now()])
            sums_to_rstd(core, env, sums[:, :, :], HD, [t])
    pool.after(decays_in, pool.done.now(), *[c.now() for c in evacuated])
    pe.after(dve.done.now(), act.done.now(), *[c.now() for c in evacuated])

    def pair(i):
        def build(b, qh, kh, by):
            at, head = i * P + HD * b, i * 2 + b
            scaled(core, by, qh[:, :, 0:HD], fp[:, :, bass.ds(at, HD)], rstd[:, :, bass.ds(head, 1)])
            scaled(core, by, kh[:, :, 0:HD], fp[:, :, bass.ds(at + MIX, HD)], rstd[:, :, bass.ds(head + HEADS, 1)])
            copies(core, by, (qh[:, :, HD:HD + 1], pos[:, :, bass.ds(head, 1)]), (kh[:, :, HD + 1:HD + 2], neg[:, :, bass.ds(head, 1)]))

        def build_v(vh):
            copies(core, None, (vh[:, :, :], fp[:, :, bass.ds(i * P + 2 * MIX, P)]))
        return build, build_v, (env["HC"]["fox_q_gain_2"], env["HC"]["fox_k_gain_2"]), DK, True, i
    pairs.run_all("fox", HEADS // 2, pair, memory_pairs(core, env, fp[:, :, q_at:q_at + MEM_W], mrstd, 0), memory_norms)


def mla(core, env):
    nc, pe, act, dve, pool = core.nc, core.pe, core.act, core.dve, core.pool
    phase, psum_a, psum_b, psum_c = env["phase"], env["psum_a"], env["psum_b"], env["psum_c"]
    col_of, Y, used = env["col_of"], env["Y"], env["used"]
    lp = core.sb("mla_p", [P, MT, MLA_IN], ctx=phase)
    q_n = core.sb("mla_q", [P, MT, HEADS * QK], ctx=phase)
    kv_n = core.sb("mla_kv", [P, MT, HEADS * 2 * HD], ctx=phase)
    rstd = core.sb("mla_rstd", [P, 2, MT, HEADS], ctx=phase)
    mrstd = core.sb("mla_mem_rstd", [P, MT, MEM_HEADS], ctx=phase)
    extra = core.sb("mla_extra", [P, MT], ctx=phase)
    pairs = HeadPairs(core, env, "mla", QK, phase)
    squares = [core.over(f"mla_squares{m}", ("x_hi", "x_lo")[m], 0, [P, 2048]) for m in range(MT)]
    kv_diag = core.over("mla_kv_diag", "y_lo", KD * SEQ, [P, MT, P])
    q_diag = env["diag"][:, 0, :, :]
    core.fence()
    k_r = lp[:, :, Q_RANK + KV_RANK:Q_RANK + KV_RANK + ROPE]
    mem_q = lp[:, :, MLA_IN - MEM_W:MLA_IN]
    evacuated = [env["a_free"], env["b_free"]]
    sums, root = env["squares"][:, 0:4], env["squares"][:, 4:8]

    def latents(ps, free, ready):
        act.after(ready)
        dve.after(ready)
        a = act.do(nc.scalar.activation(lp[:, 0, 0:512], ps[:, 0:512], ACT.Copy))
        v = dve.do(nc.vector.tensor_copy(lp[:, 1, 0:512], ps[:, 512:1024]))
        for m, copied in enumerate((a, v)):
            act.after(copied)
            for j, (at, n) in enumerate(((0, Q_RANK), (Q_RANK, KV_RANK))):
                part = ps[:, 512 * m + at:512 * m + at + n]
                act.do(nc.scalar.activation(part, part, ACT.Square, accum_out=sums[:, 2 * j + m:2 * j + m + 1]),
                       free if j else None)
    env["run_product"](env["product_natural"], env["X"], latents)
    dve.after(act.done.now(), *[c.now() for c in evacuated])
    for j, n in enumerate((Q_RANK, KV_RANK)):
        t = dve.do(nc.vector.tensor_scalar(sums[:, 2 * j:2 * j + 2], sums[:, 2 * j:2 * j + 2], 1.0 / n, EPS, ALU.mult, ALU.add))
    t = env["power"](root, sums, 4, t)
    dve.after(t)
    for j, d in enumerate((q_diag, kv_diag)):
        for m in range(MT):
            t = dve.do(nc.vector.tensor_scalar(d[:, m, :], env["ident"][:], root[:, 2 * j + m:2 * j + m + 1], None, ALU.mult))
    natural_unit(core, env, lp, 512, MLA_IN - 512)
    env["turn_and_split"](lp[:, :, 0:Q_RANK], Y, 2, col_of["mla_qa_norm_2"], t, diagonal=q_diag)
    t = env["turn_and_split"](lp[:, :, Q_RANK:Q_RANK + KV_RANK], Y, 1, col_of["mla_kva_norm_2"], t, k_to=2, diagonal=kv_diag)
    pe.after(t)

    def up(ps, stride, kt, k0, n):
        s = env["take_piece"]()
        w = env["weights"](s, kt, n)
        for k in range(kt):
            for m in range(MT):
                for c in range(0, n, 512):
                    wd = min(512, n - c)
                    mm = env["three"](ps[:, m * stride + c:m * stride + c + wd], [y[:, k0 + k, m * P:(m + 1) * P] for y in Y],
                                      [x[:, k, c:c + wd] for x in w], k == 0, k == kt - 1)
        return pe.do(mm, used)

    def evict(dst, ps, stride, n, ready):
        act.after(ready)
        dve.after(ready)
        a = act.do(nc.scalar.activation(dst(0), ps[:, 0:n], ACT.Copy))
        v = dve.do(nc.vector.tensor_copy(dst(1), ps[:, stride:stride + n]))
        return [a, v]

    rotated = core.over("mla_rotated", "y_hi", KD * SEQ, [P, MT, 4, HEADS * 16])

    def rope(lane, engine, m, x, heads, ready):
        x1, x2 = x[:, :, 0:16], x[:, :, 16:32]
        c, s = (env["rotary"][:, j, m, :].unsqueeze(1).to_broadcast([P, heads, 16]) for j in range(2))
        tmp = [rotated[:, m, j, 0:heads * 16].rearrange("p (h d) -> p h d", h=heads) for j in range(4)]
        lane.after(lane.done.now(), *ready)
        for j, (a, b) in enumerate(((x1, c), (x2, s), (x1, s), (x2, c))):
            t = lane.do(engine.tensor_tensor(tmp[j], a, b, ALU.mult))
        lane.after(t)
        lane.do(engine.tensor_tensor(x1, tmp[0], tmp[1], ALU.subtract))
        lane.do(engine.tensor_tensor(x2, tmp[2], tmp[3], ALU.add))

    def up_and_evict(dst, kt, k0, rest, ps):
        t1 = up(psum_c, 1024, kt, k0, 1024)
        t2 = up(ps, 512, kt, k0, rest)
        if dst is q_n:
            env["split_ahead"]()
        t = evict(lambda m: dst[:, m, 0:1024], psum_c, 1024, 1024, t1)
        pe.after(*t)
        return t + evict(lambda m: dst[:, m, 1024:1024 + rest], ps, 512, rest, t2)

    t = head_sums(core, mrstd, lambda m: split_heads(squares[m][:, HEADS * QK:HEADS * QK + MEM_W], HD),
                  lambda m: split_heads(mem_q[:, m, :], HD), [c.now() for c in evacuated])
    sums_to_rstd(core, env, mrstd[:, :, :], HD, [t])
    for m in range(MT):
        squared_k_r = act.do(nc.scalar.activation(squares[m][:, 1984:1984 + ROPE], k_r[:, m, :], ACT.Square,
                                                  accum_out=extra[:, m:m + 1]))
    both = ((dve, nc.vector), (pool, nc.gpsimd))
    for m, (lane, engine) in enumerate(both):
        rope(lane, engine, m, k_r[:, m, :].unsqueeze(1), 1, [squared_k_r])
    q_in = up_and_evict(q_n, 2, 0, HEADS * QK - 1024, psum_a)
    t_q = head_sums(core, rstd[:, 0, :, :], lambda m: split_heads(squares[m][:, 0:HEADS * QK], QK),
                    lambda m: split_heads(q_n[:, m, :], QK), q_in)
    EARLY = 4
    sums_to_rstd(core, env, rstd[:, 0, :, 0:EARLY], QK, [t_q])
    q_squared = act.done.now()
    kv_in = up_and_evict(kv_n, 1, 2, 512, psum_b)
    for m, (lane, engine) in enumerate(both):
        rope(lane, engine, m, split_heads(q_n[:, m, :], QK)[:, :, HD:QK], HEADS, [q_squared])
    t = head_sums(core, rstd[:, 1, :, :], lambda m: split_heads(squares[m][:, HEADS * QK:HEADS * (QK + HD)], HD),
                  lambda m: split_heads(kv_n[:, m, :], 2 * HD)[:, :, 0:HD], kv_in)
    dve.after(t, squared_k_r)
    for m in range(MT):
        t = dve.do(nc.vector.tensor_scalar(rstd[:, 1, m, :], rstd[:, 1, m, :], extra[:, m:m + 1], None, ALU.add))
    sums_to_rstd(core, env, rstd[:, 1, :, 0:EARLY], QK, [t])
    nc.scalar.preload_act_table_set("natural_log_exp_and_others")
    core.fence(pool)

    def other_heads():
        for j in range(2):
            sums_to_rstd(core, env, rstd[:, j, :, EARLY:HEADS], QK, [])
        pool.after(pool.done.now())
        env["split_ahead"]()

    act.after(act.done.now())
    pe.after(*kv_in)

    def pair(i):
        def build(b, qh, kh, by):
            r_q, r_k = (rstd[:, j, :, bass.ds(i * 2 + b, 1)] for j in range(2))
            scaled(core, by, qh[:, :, 0:QK], q_n[:, :, bass.ds(i * (2 * QK) + QK * b, QK)], r_q)
            scaled(core, by, kh[:, :, 0:HD], kv_n[:, :, bass.ds(i * (4 * HD) + 2 * HD * b, HD)], r_k)
            scaled(core, by, kh[:, :, HD:QK], k_r, r_k)

        def build_v(vh):
            copies(core, None, *((vh[:, :, HD * b:HD * b + HD], kv_n[:, :, bass.ds(i * (4 * HD) + (2 * HD * b + HD), HD)])
                                 for b in range(2)))
        return build, build_v, (env["HC"]["mla_q_gain_2"], env["HC"]["mla_k_gain_2"]), QK, True, i
    pairs.run_all("mla", HEADS // 2, pair, memory_pairs(core, env, mem_q, mrstd, 1), other_norms=other_heads)


_OUTS = [((1, SEQ, D), "float32")]


def kernel(**inputs):
    import numpy as _np
    import concourse.bacc as _bacc
    from concourse.bass_utils import run_bass_kernel_spmd as _run

    def build(strides):
        nc = _bacc.Bacc("TRN2", target_bir_lowering=False, num_devices=1)
        arrays, ins = {}, {}
        for name, value in inputs.items():
            a = _np.ascontiguousarray(value)
            if a.size == 0:
                continue
            arrays[f"in_{name}_dram"] = a
            ins[name] = nc.dram_tensor(f"in_{name}_dram", a.shape, mybir.dt.from_np(a.dtype), kind="ExternalInput").ap()
        out = nc.dram_tensor("out_0_dram", _OUTS[0][0], F32, kind="ExternalOutput").ap()
        return nc, arrays, emit(nc, ins, out, strides)

    _, _, strides = build({})
    nc, arrays, again = build(strides)
    assert again == strides
    r = _run(nc, [arrays], core_ids=[0])
    return r.results[0]["out_0_dram"]
```
